# Optimizing a Trainium2 kernel written in Bass

```python
import jax, jax.numpy as jnp
from jax import lax
import numpy as np

D_MODEL = 1024
BATCH = 1
SEQ = 512
DEPTH = 2

N_EVEN = (DEPTH + 1) // 2
N_ODD = DEPTH // 2
D_FF = 2816
RMS_EPS = 1e-6
ROPE_THETA = 10000.0

GLA_HEADS = 4
GLA_DK = 64
GLA_DV = 128
GLA_GATE_RANK = 16
GLA_GATE_TAU = 16.0
GLA_CHUNK = 64

POOL_WINDOWS = (2, 4, 8, 16)
POOL_GROUPS = 4
POOL_GROUP_DIM = 128
POOL_DIM = POOL_GROUPS * POOL_GROUP_DIM

ATT_HEADS = 8
ATT_KV_HEADS = 2
ATT_HEAD_DIM = 128
IDX_HEADS = 4
IDX_DIM = 64
TOPK_MAX = 256
Q_BLOCK = 128

EVEN_SIZES = (GLA_HEADS * GLA_DK, GLA_HEADS * GLA_DK, GLA_HEADS * GLA_DV, GLA_HEADS * GLA_DV, GLA_GATE_RANK, POOL_DIM)
EVEN_IN = sum(EVEN_SIZES)
EVEN_SPLITS = tuple(int(s) for s in np.cumsum(EVEN_SIZES)[:-1])
EVEN_MIX = GLA_HEADS * GLA_DV + POOL_DIM
ODD_SIZES = (ATT_HEADS * ATT_HEAD_DIM, ATT_KV_HEADS * ATT_HEAD_DIM, ATT_KV_HEADS * ATT_HEAD_DIM, IDX_HEADS * IDX_DIM, IDX_DIM, IDX_HEADS)
ODD_IN = sum(ODD_SIZES)
ODD_SPLITS = tuple(int(s) for s in np.cumsum(ODD_SIZES)[:-1])
ODD_MIX = ATT_HEADS * ATT_HEAD_DIM


def rms_norm(x, g):
    xf = x.astype(jnp.float32)
    y = xf * lax.rsqrt(jnp.mean(xf * xf, axis=-1, keepdims=True) + RMS_EPS)
    return (y * g.astype(jnp.float32)).astype(x.dtype)

def swiglu(x, wi, wo):
    gate, up = jnp.split(x @ wi, 2, axis=-1)
    return (jax.nn.silu(gate) * up) @ wo

def rope(x, positions):
    d = x.shape[-1]
    inv = ROPE_THETA ** (-jnp.arange(0, d, 2, dtype=jnp.float32) / d)
    ang = positions.astype(jnp.float32)[..., None] * inv
    cos = jnp.cos(ang)[:, :, None, :]
    sin = jnp.sin(ang)[:, :, None, :]
    xf = x.astype(jnp.float32)
    x1, x2 = jnp.split(xf, 2, axis=-1)
    out = jnp.concatenate([x1 * cos - x2 * sin, x2 * cos + x1 * sin], axis=-1)
    return out.astype(x.dtype)

def gla_chunked(q, k, v, log_a):
    B, S, H, DK = q.shape
    DV = v.shape[-1]
    C = GLA_CHUNK
    n = S // C

    def to_chunks(t):
        return t.astype(jnp.float32).reshape(B, n, C, H, t.shape[-1]).transpose(1, 0, 3, 2, 4)

    qc = to_chunks(q.astype(jnp.float32) * (DK ** -0.5))
    kc, vc, ac = to_chunks(k), to_chunks(v), to_chunks(log_a)
    causal = jnp.tril(jnp.ones((C, C), dtype=bool))[:, :, None]

    def step(state, inp):
        qb, kb, vb, ab = inp
        b = jnp.cumsum(ab, axis=2)
        inter = jnp.einsum('bhcd,bhde->bhce', qb * jnp.exp(b), state)
        rel = jnp.where(causal, b[:, :, :, None, :] - b[:, :, None, :, :], -jnp.inf)
        scores = jnp.einsum('bhid,bhjd,bhijd->bhij', qb, kb, jnp.exp(rel))
        intra = jnp.einsum('bhij,bhje->bhie', scores, vb)
        b_last = b[:, :, -1, :]
        k_dec = kb * jnp.exp(b_last[:, :, None, :] - b)
        state = jnp.exp(b_last)[..., None] * state + jnp.einsum('bhcd,bhce->bhde', k_dec, vb)
        return state, inter + intra

    s0 = jnp.zeros((B, H, DK, DV), jnp.float32)
    _, out = lax.scan(step, s0, (qc, kc, vc, ac))
    return out.transpose(1, 0, 3, 2, 4).reshape(B, S, H, DV)

def multiscale_pool(u):
    B, S, _ = u.shape
    ug = u.astype(jnp.float32).reshape(B, S, POOL_GROUPS, POOL_GROUP_DIM)
    csum = jnp.cumsum(ug, axis=1)
    t = jnp.arange(1, S + 1, dtype=jnp.float32)
    outs = []
    for g, w in enumerate(POOL_WINDOWS):
        c = csum[:, :, g]
        c_prev = jnp.pad(c, ((0, 0), (w, 0), (0, 0)))[:, :S]
        count = jnp.minimum(t, float(w))[None, :, None]
        outs.append((c - c_prev) / count - ug[:, :, g])
    return jnp.stack(outs, axis=2)

def gla_pool_mixer(hn, w_in, gate_w, gate_b, out_norm, pool_w, pool_scale, w_out):
    B, S, _ = hn.shape
    proj = hn @ w_in
    q, k, v, g, a_lr, u = jnp.split(proj, EVEN_SPLITS, axis=-1)
    log_a = jax.nn.log_sigmoid((a_lr @ gate_w + gate_b).astype(jnp.float32)) / GLA_GATE_TAU
    o = gla_chunked(q.reshape(B, S, GLA_HEADS, GLA_DK), k.reshape(B, S, GLA_HEADS, GLA_DK),
                    v.reshape(B, S, GLA_HEADS, GLA_DV), log_a.reshape(B, S, GLA_HEADS, GLA_DK))
    o = rms_norm(o, out_norm.reshape(GLA_HEADS, GLA_DV)).reshape(B, S, GLA_HEADS * GLA_DV)
    o = (o * jax.nn.silu(g.astype(jnp.float32))).astype(hn.dtype)
    p = multiscale_pool(u)
    p = jnp.einsum('bsgc,gcd->bsgd', p, pool_w.astype(jnp.float32)).reshape(B, S, POOL_DIM)
    p = (p * pool_scale.astype(jnp.float32)).astype(hn.dtype)
    return jnp.concatenate([o, p], axis=-1) @ w_out

def dsa_attention(q, k, v, qi, ki, wi):
    B, S, H, Dh = q.shape
    G = k.shape[2]
    R = H // G
    top_k = min(TOPK_MAX, S // 4)
    n_blocks = S // Q_BLOCK
    idx_scale = (IDX_DIM ** -0.5) * (IDX_HEADS ** -0.5)
    key_pos = jnp.arange(S)
    ki_f = ki.astype(jnp.float32)

    def block(i):
        start = i * Q_BLOCK
        qb = lax.dynamic_slice_in_dim(q, start, Q_BLOCK, axis=1).reshape(B, Q_BLOCK, G, R, Dh)
        qib = lax.dynamic_slice_in_dim(qi, start, Q_BLOCK, axis=1).astype(jnp.float32)
        wib = lax.dynamic_slice_in_dim(wi, start, Q_BLOCK, axis=1).astype(jnp.float32)
        q_pos = start + jnp.arange(Q_BLOCK)
        logits = jax.nn.relu(jnp.einsum('bthd,bsd->bths', qib, ki_f))
        iscore = jnp.einsum('bth,bths->bts', wib, logits) * idx_scale
        admissible = key_pos[None, :] <= q_pos[:, None]
        iscore = jnp.where(admissible[None], iscore, -jnp.inf)
        _, sel = lax.top_k(iscore, top_k)
        valid = sel <= q_pos[None, :, None]
        k_sel = jax.vmap(lambda a, ix: a[ix])(k, sel)
        v_sel = jax.vmap(lambda a, ix: a[ix])(v, sel)
        s = jnp.einsum('btgrd,btkgd->btgrk', qb.astype(jnp.float32), k_sel.astype(jnp.float32)) * (Dh ** -0.5)
        s = jnp.where(valid[:, :, None, None, :], s, -jnp.inf)
        p = jax.nn.softmax(s, axis=-1)
        o = jnp.einsum('btgrk,btkgd->btgrd', p, v_sel.astype(jnp.float32))
        return o.reshape(B, Q_BLOCK, H * Dh).astype(q.dtype)

    out = lax.map(block, jnp.arange(n_blocks))
    return out.transpose(1, 0, 2, 3).reshape(B, S, H * Dh)

def dsa_mixer(hn, positions, w_in, w_out):
    B, S, _ = hn.shape
    proj = hn @ w_in
    q, k, v, qi, ki, wi = jnp.split(proj, ODD_SPLITS, axis=-1)
    q = rope(q.reshape(B, S, ATT_HEADS, ATT_HEAD_DIM), positions)
    k = rope(k.reshape(B, S, ATT_KV_HEADS, ATT_HEAD_DIM), positions)
    v = v.reshape(B, S, ATT_KV_HEADS, ATT_HEAD_DIM)
    qi = rope(qi.reshape(B, S, IDX_HEADS, IDX_DIM), positions)
    ki = rope(ki.reshape(B, S, 1, IDX_DIM), positions)[:, :, 0]
    o = dsa_attention(q, k, v, qi, ki, wi)
    return o @ w_out

def first_inputs(seed: int = 0) -> dict:
    key = jax.random.key(seed)
    ks = jax.random.split(key, 20)
    f32 = jnp.float32

    def nrm(k, shape, scale):
        return jax.random.normal(k, shape, f32) * scale

    def gain(k, shape):
        return 1.0 + 0.02 * jax.random.normal(k, shape, f32)

    x = jax.random.normal(ks[0], (BATCH, SEQ, D_MODEL), f32)
    positions = jnp.broadcast_to(jnp.arange(SEQ, dtype=jnp.int32)[None, :], (BATCH, SEQ)).astype(jnp.int32)
    return {
        "x": x,
        "positions": positions,
        "ffn1_norm": gain(ks[1], (DEPTH, D_MODEL)),
        "ffn1_wi": nrm(ks[2], (DEPTH, D_MODEL, 2 * D_FF), D_MODEL ** -0.5),
        "ffn1_wo": nrm(ks[3], (DEPTH, D_FF, D_MODEL), D_FF ** -0.5),
        "mix_norm": gain(ks[4], (DEPTH, D_MODEL)),
        "ffn2_norm": gain(ks[5], (DEPTH, D_MODEL)),
        "ffn2_wi": nrm(ks[6], (DEPTH, D_MODEL, 2 * D_FF), D_MODEL ** -0.5),
        "ffn2_wo": nrm(ks[7], (DEPTH, D_FF, D_MODEL), D_FF ** -0.5),
        "even_w_in": nrm(ks[8], (N_EVEN, D_MODEL, EVEN_IN), D_MODEL ** -0.5),
        "gla_gate_w": nrm(ks[9], (N_EVEN, GLA_GATE_RANK, GLA_HEADS * GLA_DK), GLA_GATE_RANK ** -0.5),
        "gla_gate_b": nrm(ks[10], (N_EVEN, GLA_HEADS * GLA_DK), 0.1),
        "gla_out_norm": gain(ks[11], (N_EVEN, GLA_HEADS * GLA_DV)),
        "pool_w": nrm(ks[12], (N_EVEN, POOL_GROUPS, POOL_GROUP_DIM, POOL_GROUP_DIM), POOL_GROUP_DIM ** -0.5),
        "pool_scale": gain(ks[13], (N_EVEN, POOL_DIM)),
        "even_w_out": nrm(ks[14], (N_EVEN, EVEN_MIX, D_MODEL), EVEN_MIX ** -0.5),
        "odd_w_in": nrm(ks[15], (N_ODD, D_MODEL, ODD_IN), D_MODEL ** -0.5),
        "odd_w_out": nrm(ks[16], (N_ODD, ODD_MIX, D_MODEL), ODD_MIX ** -0.5),
        "final_norm": gain(ks[17], (D_MODEL,)),
    }

def first_block(x, positions, ffn1_norm, ffn1_wi, ffn1_wo, mix_norm, ffn2_norm, ffn2_wi, ffn2_wo,
              even_w_in, gla_gate_w, gla_gate_b, gla_out_norm, pool_w, pool_scale, even_w_out,
              odd_w_in, odd_w_out, final_norm):
    h = x
    for li in range(DEPTH):
        h = h + 0.5 * swiglu(rms_norm(h, ffn1_norm[li]), ffn1_wi[li], ffn1_wo[li])
        hn = rms_norm(h, mix_norm[li])
        if li % 2 == 0:
            j = li // 2
            mix = gla_pool_mixer(hn, even_w_in[j], gla_gate_w[j], gla_gate_b[j], gla_out_norm[j],
                                 pool_w[j], pool_scale[j], even_w_out[j])
        else:
            j = li // 2
            mix = dsa_mixer(hn, positions, odd_w_in[j], odd_w_out[j])
        h = h + mix
        h = h + 0.5 * swiglu(rms_norm(h, ffn2_norm[li]), ffn2_wi[li], ffn2_wo[li])
    return rms_norm(h, final_norm)


CHUNK = 64
N_MIXERS = 2
EPS = 1e-6

GDN_QK_HEADS = 8
GDN_V_HEADS = 16
GDN_HEAD_DIM = 128
GDN_QK_WIDTH = GDN_QK_HEADS * GDN_HEAD_DIM
GDN_V_WIDTH = GDN_V_HEADS * GDN_HEAD_DIM
GDN_CONV_CH = 2 * GDN_QK_WIDTH + GDN_V_WIDTH
GDN_IN_WIDTH = GDN_CONV_CH + GDN_V_WIDTH + 2 * GDN_V_HEADS
CONV_WIDTH = 4

FOX_HEADS = 16
FOX_HEAD_DIM = 64
FOX_WIDTH = FOX_HEADS * FOX_HEAD_DIM
FOX_IN_WIDTH = 4 * FOX_WIDTH + FOX_HEADS

N_LAYERS_A = (DEPTH + 1) // 2
N_LAYERS_B = DEPTH // 2


def rmsnorm(x, w):
    xf = x.astype(jnp.float32)
    y = xf * lax.rsqrt(jnp.mean(xf * xf, axis=-1, keepdims=True) + EPS)
    return (y * w.astype(jnp.float32)).astype(x.dtype)

def l2norm(x):
    return x * lax.rsqrt(jnp.sum(x * x, axis=-1, keepdims=True) + EPS)

def causal_depthwise_conv(x, w):
    C = x.shape[-1]
    return lax.conv_general_dilated(
        x, w[:, None, :].astype(x.dtype), window_strides=(1,),
        padding=[(CONV_WIDTH - 1, 0)], dimension_numbers=('NWC', 'WIO', 'NWC'),
        feature_group_count=C)

def gated_delta_rule(q, k, v, g, beta):
    B, S, H, DK = q.shape
    DV = v.shape[-1]
    N = S // CHUNK

    def to_chunks(t):
        t = jnp.moveaxis(t, 2, 1)
        return t.reshape(t.shape[:2] + (N, CHUNK) + t.shape[3:])

    q, k, v, g, beta = (to_chunks(t) for t in (q, k, v, g, beta))
    g = jnp.cumsum(g, axis=-1)
    idx = jnp.arange(CHUNK)
    lower = idx[:, None] >= idx[None, :]
    strict = idx[:, None] > idx[None, :]
    decay = jnp.exp(jnp.where(lower, g[..., :, None] - g[..., None, :], -jnp.inf))
    kb = k * beta[..., None]
    vb = v * beta[..., None]
    L = jnp.where(strict, jnp.einsum('bhncd,bhnsd->bhncs', kb, k) * decay, 0.0)
    eye = jnp.eye(CHUNK, dtype=q.dtype)
    T = lax.linalg.triangular_solve(eye + L, jnp.broadcast_to(eye, L.shape),
                                    left_side=True, lower=True, unit_diagonal=True)
    u = T @ vb
    w = T @ (kb * jnp.exp(g)[..., None])
    attn = jnp.einsum('bhncd,bhnsd->bhncs', q, k) * decay
    q_dec = q * jnp.exp(g)[..., None]
    k_dec = k * jnp.exp(g[..., -1:] - g)[..., None]
    g_last = jnp.exp(g[..., -1])
    xs = tuple(jnp.moveaxis(t, 2, 0) for t in (q_dec, k_dec, u, w, attn, g_last))

    def step(state, inp):
        q_n, k_n, u_n, w_n, a_n, gl_n = inp
        v_new = u_n - jnp.einsum('bhcd,bhde->bhce', w_n, state)
        o = (jnp.einsum('bhcd,bhde->bhce', q_n, state)
             + jnp.einsum('bhcs,bhse->bhce', a_n, v_new))
        state = state * gl_n[..., None, None] + jnp.einsum('bhcd,bhce->bhde', k_n, v_new)
        return state, o

    state0 = jnp.zeros((B, H, DK, DV), q.dtype)
    _, o = lax.scan(step, state0, xs)
    o = jnp.moveaxis(o, 0, 2).reshape(B, H, S, DV)
    return jnp.moveaxis(o, 1, 2)

def gdn_mixer(h, w_in, conv_w, A_log, dt_bias, norm_w, w_out):
    B, S, _ = h.shape
    proj = h @ w_in
    qkv, z, b, a = jnp.split(proj, [GDN_CONV_CH, GDN_CONV_CH + GDN_V_WIDTH,
                                    GDN_CONV_CH + GDN_V_WIDTH + GDN_V_HEADS], axis=-1)
    qkv = jax.nn.silu(causal_depthwise_conv(qkv, conv_w))
    q, k, v = jnp.split(qkv, [GDN_QK_WIDTH, 2 * GDN_QK_WIDTH], axis=-1)
    rep = GDN_V_HEADS // GDN_QK_HEADS
    q = l2norm(q.reshape(B, S, GDN_QK_HEADS, GDN_HEAD_DIM).astype(jnp.float32)) * GDN_HEAD_DIM ** -0.5
    k = l2norm(k.reshape(B, S, GDN_QK_HEADS, GDN_HEAD_DIM).astype(jnp.float32))
    q = jnp.repeat(q, rep, axis=2)
    k = jnp.repeat(k, rep, axis=2)
    v = v.reshape(B, S, GDN_V_HEADS, GDN_HEAD_DIM).astype(jnp.float32)
    beta = jax.nn.sigmoid(b.astype(jnp.float32))
    g = -jnp.exp(A_log.astype(jnp.float32)) * jax.nn.softplus(
        a.astype(jnp.float32) + dt_bias.astype(jnp.float32))
    o = gated_delta_rule(q, k, v, g, beta)
    zg = jax.nn.silu(z.reshape(B, S, GDN_V_HEADS, GDN_HEAD_DIM).astype(jnp.float32))
    o = rmsnorm(o, norm_w) * zg
    return o.reshape(B, S, GDN_V_WIDTH).astype(h.dtype) @ w_out

def forgetting_attention(q, k, v, cum):
    B, S, H, DH = q.shape
    NB = S // Q_BLOCK
    cum_k = jnp.moveaxis(cum, 1, 2)
    q_blocks = jnp.moveaxis(q.reshape(B, NB, Q_BLOCK, H, DH), 1, 0)
    c_blocks = jnp.moveaxis(cum_k.reshape(B, H, NB, Q_BLOCK), 2, 0)
    key_pos = jnp.arange(S)

    def block(inp):
        q_b, c_b, start = inp
        logits = jnp.einsum('bqhd,bkhd->bhqk', q_b, k)
        logits = logits + (c_b[..., :, None] - cum_k[..., None, :])
        q_pos = start + jnp.arange(Q_BLOCK)
        mask = key_pos[None, :] <= q_pos[:, None]
        p = jax.nn.softmax(jnp.where(mask, logits, -jnp.inf), axis=-1)
        return jnp.einsum('bhqk,bkhd->bqhd', p, v)

    o = lax.map(block, (q_blocks, c_blocks, jnp.arange(NB) * Q_BLOCK))
    return jnp.moveaxis(o, 0, 1).reshape(B, S, H, DH)

def fox_mixer(h, w_in, f_bias, qn_w, kn_w, w_out):
    B, S, _ = h.shape
    proj = h @ w_in
    q, k, v, z, f = jnp.split(proj, [FOX_WIDTH, 2 * FOX_WIDTH, 3 * FOX_WIDTH, 4 * FOX_WIDTH], axis=-1)
    shp = (B, S, FOX_HEADS, FOX_HEAD_DIM)
    q = rmsnorm(q.reshape(shp).astype(jnp.float32), qn_w) * FOX_HEAD_DIM ** -0.5
    k = rmsnorm(k.reshape(shp).astype(jnp.float32), kn_w)
    v = v.reshape(shp).astype(jnp.float32)
    log_f = jax.nn.log_sigmoid(f.astype(jnp.float32) + f_bias.astype(jnp.float32))
    cum = jnp.cumsum(log_f, axis=1)
    o = forgetting_attention(q, k, v, cum).reshape(B, S, FOX_WIDTH)
    o = o * jax.nn.silu(z.astype(jnp.float32))
    return o.astype(h.dtype) @ w_out

def second_inputs(seed: int = 0) -> dict:
    key = jax.random.key(seed)
    ks = jax.random.split(key, 20)
    nrm = jax.random.normal
    D = D_MODEL
    dt = jnp.exp(jax.random.uniform(ks[7], (N_LAYERS_A, GDN_V_HEADS),
                                    minval=np.log(1e-3), maxval=np.log(1e-1)))
    return {
        "x": nrm(ks[0], (BATCH, SEQ, D), jnp.float32),
        "c": nrm(ks[1], (BATCH, D), jnp.float32),
        "norm_w": 1.0 + 0.1 * nrm(ks[2], (DEPTH, D), jnp.float32),
        "ada_w": 0.5 * D ** -0.5 * nrm(ks[3], (DEPTH, D, 3 * D), jnp.float32),
        "ada_b": 0.02 * nrm(ks[4], (DEPTH, 3 * D), jnp.float32),
        "a_w_in": D ** -0.5 * nrm(ks[5], (N_LAYERS_A, D, GDN_IN_WIDTH), jnp.float32),
        "a_conv_w": CONV_WIDTH ** -0.5 * nrm(ks[6], (N_LAYERS_A, CONV_WIDTH, GDN_CONV_CH), jnp.float32),
        "a_A_log": jnp.log(jax.random.uniform(ks[8], (N_LAYERS_A, GDN_V_HEADS), minval=1.0, maxval=16.0)),
        "a_dt_bias": dt + jnp.log(-jnp.expm1(-dt)),
        "a_norm_w": 1.0 + 0.1 * nrm(ks[9], (N_LAYERS_A, GDN_HEAD_DIM), jnp.float32),
        "a_w_out": GDN_V_WIDTH ** -0.5 * nrm(ks[10], (N_LAYERS_A, GDN_V_WIDTH, D), jnp.float32),
        "b_w_in": D ** -0.5 * nrm(ks[11], (N_LAYERS_B, D, FOX_IN_WIDTH), jnp.float32),
        "b_f_bias": jax.random.uniform(ks[12], (N_LAYERS_B, FOX_HEADS), minval=1.0, maxval=5.0),
        "b_qn_w": 1.0 + 0.1 * nrm(ks[13], (N_LAYERS_B, FOX_HEAD_DIM), jnp.float32),
        "b_kn_w": 1.0 + 0.1 * nrm(ks[14], (N_LAYERS_B, FOX_HEAD_DIM), jnp.float32),
        "b_w_out": FOX_WIDTH ** -0.5 * nrm(ks[15], (N_LAYERS_B, FOX_WIDTH, D), jnp.float32),
        "final_norm_w": 1.0 + 0.1 * nrm(ks[16], (D,), jnp.float32),
    }

def second_block(x, c, norm_w, ada_w, ada_b, a_w_in, a_conv_w, a_A_log, a_dt_bias, a_norm_w,
              a_w_out, b_w_in, b_f_bias, b_qn_w, b_kn_w, b_w_out, final_norm_w):
    cond = jax.nn.silu(c)
    for i in range(DEPTH):
        mod = cond @ ada_w[i] + ada_b[i]
        shift, scale, gate = jnp.split(mod[:, None, :], 3, axis=-1)
        h = rmsnorm(x, norm_w[i]) * (1 + scale) + shift
        j = i // N_MIXERS
        if i % N_MIXERS == 0:
            y = gdn_mixer(h, a_w_in[j], a_conv_w[j], a_A_log[j], a_dt_bias[j], a_norm_w[j], a_w_out[j])
        else:
            y = fox_mixer(h, b_w_in[j], b_f_bias[j], b_qn_w[j], b_kn_w[j], b_w_out[j])
        x = x + gate * y
    return rmsnorm(x, final_norm_w)


def setup_inputs(seed=0):
    out = dict(first_inputs(seed))
    for name, value in second_inputs(seed + 1).items():
        if name != "x":
            out[name + "_2"] = value
    return out


def reference(
    x, positions, ffn1_norm, ffn1_wi, ffn1_wo, mix_norm, ffn2_norm, ffn2_wi, ffn2_wo, even_w_in,
    gla_gate_w, gla_gate_b, gla_out_norm, pool_w, pool_scale, even_w_out, odd_w_in, odd_w_out,
    final_norm, c_2, norm_w_2, ada_w_2, ada_b_2, a_w_in_2, a_conv_w_2, a_A_log_2, a_dt_bias_2,
    a_norm_w_2, a_w_out_2, b_w_in_2, b_f_bias_2, b_qn_w_2, b_kn_w_2, b_w_out_2, final_norm_w_2,
):
    x = first_block(
        x, positions, ffn1_norm, ffn1_wi, ffn1_wo, mix_norm, ffn2_norm, ffn2_wi, ffn2_wo,
        even_w_in, gla_gate_w, gla_gate_b, gla_out_norm, pool_w, pool_scale, even_w_out,
        odd_w_in, odd_w_out, final_norm,
    )
    return second_block(
        x, c_2, norm_w_2, ada_w_2, ada_b_2, a_w_in_2, a_conv_w_2, a_A_log_2, a_dt_bias_2,
        a_norm_w_2, a_w_out_2, b_w_in_2, b_f_bias_2, b_qn_w_2, b_kn_w_2, b_w_out_2,
        final_norm_w_2,
    )


_drawn_inputs = setup_inputs


def setup_inputs(seed=0):
    import zlib

    import numpy as np

    out = dict(_drawn_inputs(seed))
    spreads = {}
    factors = {'ffn1_norm': 3.213,
     'ffn2_norm': 4.175,
     'gla_out_norm': 14.901,
     'pool_scale': 10.645,
     'final_norm': 2.782,
     'ada_b_2': 3.18,
     'a_norm_w_2': 3.113,
     'b_qn_w_2': 8.0,
     'b_kn_w_2': 8.0}
    for name, (base, spread) in spreads.items():
        noise = np.random.default_rng([zlib.crc32(name.encode()), seed]).standard_normal(out[name].shape)
        drawn = base * np.exp(spread * noise) if base else spread * noise
        out[name] = __import__('jax').numpy.asarray(drawn.astype(out[name].dtype))
    for name, factor in factors.items():
        out[name] = (out[name] * factor).astype(out[name].dtype)
    return out
```

```python
from contextlib import ExitStack

import concourse.bass as bass
from concourse import mybir

ALU = mybir.AluOpType
ACT = mybir.ActivationFunctionType
AX = mybir.AxisListType
F32 = mybir.dt.float32
F32R = mybir.dt.float32r
I32 = mybir.dt.int32

P = 128
T = 512
D = 1024
KT = D // P
TT = T // P
FF = 2816
FT = FF // P
EPS = 1e-6
NEG = -1.0e30
TAKEN = -3.0e38
ROPE_THETA = 10000.0
TWO_PI = 6.283185307179586
ROUND = 12582912.0
PI_A, PI_B, PI_C = 6.28125, 1.9350051879882812e-3, 3.0199157e-7

GLA_HEADS, GLA_DK, GLA_CHUNK, GLA_TAU = 4, 64, 64, 16.0
GLA_CH = T // GLA_CHUNK
POOL_GROUPS = 4
ATT_HEADS, ATT_KV, ATT_DH = 8, 2, 128
IDX_HEADS, IDX_DIM, TOPK = 4, 64, 128
GDN_QK, GDN_HEADS, GDN_DH, CONV = 8, 16, 128, 4
GDN_QW, GDN_VW = GDN_QK * GDN_DH, GDN_HEADS * GDN_DH
GDN_Z, GDN_B = 2 * GDN_QW + GDN_VW, 2 * GDN_QW + 2 * GDN_VW
FOX_HEADS, FOX_DH = 16, 64
INV_BLOCK = 16

RAW, SPLIT, BANKS = 4, 4, 4
AHEAD = 2

OUT3 = 3
FFN_B, FFN_T = 2 * FT + OUT3 * KT, 2 * FT + KT
GLA_P = 17
DSA_P = 16
GDN_P = 1 + 6 * GDN_QK
FOX_P = 1 + 4 * (FOX_HEADS // 2)
ADA_P = 2 * 3 * KT
STAGES = [("ffn0", FFN_B, FFN_T), ("gla", GLA_P + KT, GLA_P + KT), ("ffn1", FFN_B, FFN_T), ("ffn2", FFN_B, FFN_T),
          ("dsa", DSA_P + KT, DSA_P + KT), ("ffn3", FFN_B, FFN_T), ("ada", ADA_P, ADA_P),
          ("gdn", GDN_P + 2 * KT, GDN_P + KT), ("fox", FOX_P + KT, FOX_P + KT)]
BASE, _b, _t = {}, 0, 0
for _n, _nb, _nt in STAGES:
    BASE[_n] = (_b, _t)
    _b, _t = _b + _nb, _t + _nt

BLOCKS = _b

R_FFN1, R_MIX, R_FFN2, R_FINAL, R_NORM2, R_FINAL2 = 0, 16, 32, 48, 56, 72
R_GLAN, R_POOLS, R_GATEB, R_GDNN, R_C, R_QN, R_KN, R_INV128, R_INV64 = 80, 84, 88, 90, 91, 99, 100, 101, 102
R_CONV, R_ADAB = P, 2 * P


class Steps:

    def __init__(self, sem, names, lead=0):
        self.sem, self.names, self.n, self.lead = sem, list(names), len(names), lead
        self.at = {name: k + 1 + lead for k, name in enumerate(self.names)}
        assert len(self.at) == self.n
        self.next = 0

    def done(self, name):
        assert self.names[self.next % self.n] == name, (name, self.names[self.next % self.n])
        self.next += 1
        return self.sem, 1

    def after(self, name, turn=0):
        return self.sem, turn * self.n + self.at[name]

    def turns_before(self, turn):
        return self.sem, turn * self.n + self.lead


def col(i, n=1, step=T):
    return bass.ds(i * step, n * step)


def first_and_second_block(nc, a, out):
    with ExitStack() as ctx:
        def sem(name):
            return ctx.enter_context(nc.semaphore(name))

        cursor = [16512]

        def sb(name, cols, dt=F32, parts=P):
            at = cursor[0]
            cursor[0] += -(-cols * 4 // 32) * 32
            return nc.alloc_sbuf_tensor_at(name, [parts, cols], dt, offset=at)

        hres = sb("hres", KT * T)
        x_hi, x_lo = sb("x_hi", KT * T, F32R), sb("x_lo", KT * T, F32R)
        w_raw = [sb(f"w_raw{s}", D) for s in range(RAW)]
        w_hi = [sb(f"w_hi{s}", D, F32R) for s in range(SPLIT)]
        w_lo = [sb(f"w_lo{s}", D, F32R) for s in range(SPLIT)]
        sumsq, rstd = sb("sumsq", T), sb("rstd", T)
        arena = cursor[0]
        cursor[0] += 48 * T * 4

        def tile(name, k, n=1, dt=F32):
            assert k + n <= 48
            return nc.alloc_sbuf_tensor_at(name, [P, n * T], dt, offset=arena + k * T * 4)

        h_hi, h_lo = tile("h_hi", 0, FT, F32R), tile("h_lo", FT, FT, F32R)
        gdn_hi, gdn_lo = tile("gdn_hi", FT, 16, F32R), tile("gdn_lo", 0, 16, F32R)
        gate_s = [tile(f"gate_s{s}", 44 + s) for s in range(2)]
        prod = [tile(f"prod{s}", 46 + s) for s in range(2)]
        xn = [tile(f"xn{s}", 44 + s) for s in range(2)]
        std, square = tile("std", 46), tile("square", 47)

        ident, ones, ones64 = sb("ident", P), sb("ones", P), sb("ones64", P)
        swap128, swap64 = sb("swap128", P), sb("swap64", P)
        above_big, in_block, off_block = sb("above_big", P), sb("in_block", P), sb("off_block", P)
        causal = sb("causal", P)
        chunk_T = sb("chunk_T", P)
        par = sb("par", 3 * P)
        gate_w, pool_w = sb("gate_w", 256, parts=16), sb("pool_w", POOL_GROUPS * P)
        gla_cols = sb("gla_cols", 8 * GLA_CH)
        inv_count = sb("inv_count", 16 * POOL_GROUPS)
        small = sb("small", 64)
        eps_c, half_pi, nfox_b, dt_b, neg_a = (small[:, k:k + 1] for k in range(5))
        cond2 = sb("cond2", 2 * KT)
        cond_hi, cond_lo = sb("cond_hi", 2 * KT, F32R), sb("cond_lo", 2 * KT, F32R)
        mod = sb("mod", ADA_P)
        gain2 = sb("gain2", 2 * KT)
        assert cursor[0] <= 229344, cursor[0]
        stage_rows = [tile(f"stage_rows{k}", 16 + k) for k in range(3)]
        x_in = tile("x_in", 0, 8)

        bank = [ctx.enter_context(nc.psum_tensor(f"bank{k}", [P, T], F32)) for k in range(8)]

        w_loaded = [sem(f"w_loaded{s}") for s in range(RAW)]
        part_loaded = sem("part_loaded")
        w_hi_done = sem("w_hi_done")
        w_lo_done = sem("w_lo_done")
        block_done = sem("block_done")
        tile_free = sem("tile_free")
        x_loaded, x_turned, x_taken = sem("x_loaded"), sem("x_turned"), sem("x_taken")
        params_loaded, rows_zeroed = sem("params_loaded"), sem("rows_zeroed")
        rows_turned, rows_taken = sem("rows_turned"), sem("rows_taken")
        consts_made, ident_made = sem("consts_made"), sem("ident_made")
        eps_made, cond_made = sem("eps_made"), sem("cond_made")
        cond_split = sem("cond_split")
        sum_cleared, sum_square, sum_added = sem("sum_cleared"), sem("sum_square"), sem("sum_added")
        mean_done, std_done, rstd_done = sem("mean_done"), sem("std_done"), sem("rstd_done")
        xn_done, x_hi_done, x_ready = sem("xn_done"), sem("x_hi_done"), sem("x_ready")
        silu_done, h_hi_done, h_ready = sem("silu_done"), sem("h_hi_done"), sem("h_ready")
        normed = sem("normed")
        mod_done = sem("mod_done")
        gain_done = sem("gain_done")
        out_normed, out_turned, out_taken, out_stored = (sem(n) for n in ("out_normed", "out_turned", "out_taken", "out_stored"))

        block = ctx.enter_context(nc.Block())
        pe_, act_, dve_, pool_, sp_ = nc.tensor, nc.scalar, nc.vector, nc.gpsimd, nc.sync

        def load(sp, b, src, i=0, n=0, cols=(0, P), kts=KT):
            sp.wait_ge(w_lo_done, b + 1 + i * n)
            dst = w_raw[b % RAW].rearrange("p (k c) -> p k c", c=P)[:, 0:kts, cols[0]:cols[1]]
            sp.dma_start(dst, src).then_inc(w_loaded[b % RAW], 16)

        def load_pair(sp, b, pair, parts):
            sp.wait_ge(w_lo_done, b + 1)
            for k, (src, (c0, c1)) in enumerate(parts):
                dst = w_raw[b % RAW].rearrange("p (k c) -> p k c", c=P)[:, :, c0:c1]
                if k == 0:
                    sp.dma_start(dst, src).then_inc(part_loaded, 16)
                    sp.wait_ge(part_loaded, 16 * (pair + 1))
                else:
                    sp.dma_start(dst, src).then_inc(w_loaded[b % RAW], 16)

        def split_hi(act, b, i=0, n=0):
            act.wait_ge(w_loaded[b % RAW], 16 * (b // RAW + 1) + i * (16 * n // RAW))
            act.wait_ge(block_done, b + 1 + i * n)
            act.activation(w_hi[b % SPLIT][:], w_raw[b % RAW][:], ACT.Copy).then_inc(w_hi_done, 1)

        def split_lo(dve, b, i=0, n=0):
            dve.wait_ge(w_hi_done, b + 1 + i * n)
            s = b % SPLIT
            dve.tensor_tensor(w_lo[s][:], w_raw[b % RAW][:], w_hi[s][:].bitcast(F32), ALU.subtract).then_inc(w_lo_done, 1)

        def products(pe, b, out, rhs_hi, rhs_lo, kts, first, last, i=0, n=0):
            pe.wait_ge(w_lo_done, RAW + b + 1 + i * n)
            s = b % SPLIT
            for kk, kt in enumerate(kts):
                w = slice(kk * P, kk * P + P)
                for m, (lhs, rhs) in enumerate(((w_hi[s], rhs_hi), (w_hi[s], rhs_lo), (w_lo[s], rhs_hi))):
                    mm = pe.matmul(out, lhs[:, w], rhs(kt), start=first and kk == 0 and m == 0,
                                   stop=last and kk == len(kts) - 1 and m == 2)
            mm.then_inc(block_done, 1)

        def x_of(buf):
            return lambda kt: buf[:, kt * T:kt * T + T]

        def weight_cols(w, i, k0=0, k1=KT):
            return w.rearrange("(k p) n -> p k n", p=P)[:, k0:k1, i]

        def in_turns(eng, count, body):
            turns = count // 4
            if turns > 1:
                with eng.Fori(0, turns) as i:
                    for u in range(4):
                        body(u, i, 4)
            else:
                turns = 0
            for u in range(4 * turns, count):
                body(u, 0, 0)

        def project_sp(sp, w, b0, count, col0):
            in_turns(sp, count, lambda u, i, n: load(sp, b0 + u, weight_cols(w, bass.ds(col0 + u * P + i * (n * P), P)), i, n))

        def project_act(act, b0, count):
            in_turns(act, count, lambda u, i, n: split_hi(act, b0 + u + AHEAD, i, n))

        def project_pe(pe, run, b0, t0, count):
            pe.wait_ge(x_ready, KT * (run + 1))

            def one(u, i, n):
                pe.wait_ge(tile_free, t0 + u + 1 + i * n)
                products(pe, b0 + u, bank[(t0 + u) % BANKS][:], x_of(x_hi), x_of(x_lo), range(KT), True, True, i, n)
            in_turns(pe, count, one)

        def project_dve(dve, b0, t0, count, take):
            def one(u, i, n):
                split_lo(dve, b0 + u + AHEAD, i, n)
                dve.wait_ge(block_done, SPLIT + b0 + u + 1 + i * n)
                take(u + i * n, bank[(t0 + u) % BANKS][:]).then_inc(tile_free, 1)
            in_turns(dve, count, one)

        def cuts(kts):
            return [range(k, min(k + KT, kts)) for k in range(0, kts, KT)]

        def down_sp(sp, w, b0, kts):
            parts = cuts(kts)
            with sp.Fori(0, KT // 4) as i:
                for q in range(4):
                    for m, ks in enumerate(parts):
                        load(sp, b0 + q * len(parts) + m, weight_cols(w, bass.ds(i * (4 * P) + q * P, P), ks[0], ks[-1] + 1),
                             i, 4 * len(parts), kts=len(ks))

        def down_act(act, b0, kts):
            n = len(cuts(kts))
            with act.Fori(0, KT // 4) as i:
                for u in range(4 * n):
                    split_hi(act, b0 + u + AHEAD, i, 4 * n)

        def down_pe(pe, b0, t0, kts, hi, lo, h_sem, h_count):
            parts = cuts(kts)
            pe.wait_ge(h_sem, h_count)
            with pe.Fori(0, KT // 4) as i:
                for q in range(4):
                    pe.wait_ge(tile_free, t0 + q + 1 + i * 4)
                    for m, ks in enumerate(parts):
                        products(pe, b0 + q * len(parts) + m, bank[(t0 + q) % BANKS][:], x_of(hi), x_of(lo), ks,
                                 m == 0, m == len(parts) - 1, i, 4 * len(parts))

        def down_dve(dve, b0, t0, kts, scale):
            n = len(cuts(kts))
            with dve.Fori(0, KT // 4) as i:
                for q in range(4):
                    for m in range(n):
                        split_lo(dve, b0 + q * n + m + AHEAD, i, 4 * n)
                    dve.wait_ge(block_done, SPLIT + b0 + q * n + n + i * (4 * n))
                    r = hres[:, col(i * 4 + q)]
                    s = scale if isinstance(scale, float) else scale[:, bass.ds(i * 4 + q, 1)]
                    dve.scalar_tensor_tensor(r, bank[(t0 + q) % BANKS][:], s, r, ALU.mult, ALU.add).then_inc(tile_free, 1)

        def squares_pool(pool, r, ready, count0):
            if r:
                pool.wait_ge(mean_done, r)
            pool.memset(sumsq[:], 0.0).then_inc(sum_cleared, 1)
            pool.wait_ge(sum_cleared, r + 1)
            with pool.Fori(0, KT) as n:
                pool.wait_ge(ready, n + count0)
                x = hres[:, col(n)]
                pool.tensor_tensor(square[:], x, x, ALU.mult).then_inc(sum_square, 1)
                pool.wait_ge(sum_square, n + KT * r + 1)
                pool.tensor_tensor(sumsq[:], sumsq[:], square[:], ALU.add).then_inc(sum_added, 1)
                pool.wait_ge(sum_added, n + KT * r + 1)

        def mean_pe(pe, r):
            pe.wait_ge(sum_added, KT * (r + 1))
            pe.matmul(bank[4][:], ones[:], sumsq[:], start=True, stop=True).then_inc(mean_done, 1)

        def std_act(act, r):
            act.wait_ge(mean_done, r + 1)
            act.activation(std[:], bank[4][:], ACT.Sqrt, bias=eps_c, scale=1.0 / D).then_inc(std_done, 1)

        def rstd_dve(dve, r):
            dve.wait_ge(std_done, r + 1)
            dve.reciprocal(rstd[:], std[:]).then_inc(rstd_done, 1)
            dve.wait_ge(rstd_done, r + 1)

        def norm_act(act, r, run, shift=None):
            std_act(act, r)
            for k in range(KT):
                act.wait_ge(xn_done, KT * run + k + 1)
                if shift is None:
                    act.activation(x_hi[:, k * T:k * T + T], xn[k % 2][:], ACT.Copy).then_inc(x_hi_done, 1)
                else:
                    act.activation(x_hi[:, k * T:k * T + T], xn[k % 2][:], ACT.Identity,
                                   bias=shift[:, k:k + 1]).then_inc(x_hi_done, 1)

        def norm_dve(dve, r, run, gain, shift=None):
            rstd_dve(dve, r)

            def low(k):
                dve.wait_ge(x_hi_done, KT * run + k + 1)
                hi = x_hi[:, k * T:k * T + T].bitcast(F32)
                if shift is None:
                    dve.tensor_tensor(x_lo[:, k * T:k * T + T], xn[k % 2][:], hi, ALU.subtract).then_inc(x_ready, 1)
                else:
                    dve.scalar_tensor_tensor(x_lo[:, k * T:k * T + T], xn[k % 2][:], shift[:, k:k + 1], hi,
                                             ALU.add, ALU.subtract).then_inc(x_ready, 1)
            for k in range(KT):
                if k >= 2:
                    low(k - 2)
                    dve.wait_ge(x_ready, KT * run + k - 1)
                dve.scalar_tensor_tensor(xn[k % 2][:], hres[:, k * T:k * T + T], gain[:, k:k + 1], rstd[:],
                                         ALU.mult, ALU.mult).then_inc(xn_done, 1)
            low(KT - 2)
            low(KT - 1)

        def ffn_sp(sp, f, wi, wo):
            b0, _ = BASE[f"ffn{f}"]
            with sp.Fori(0, FT // 2) as i:
                for s in range(2):
                    for g in range(2):
                        load(sp, b0 + 2 * s + g, weight_cols(wi, bass.ds(i * (2 * P) + s * P + g * FF, P)), i, 4)
            down_sp(sp, wo, b0 + 2 * FT, FT)

        def ffn_pe(pe, f, run, h0):
            b0, t0 = BASE[f"ffn{f}"]
            project_pe(pe, run, b0, t0, 2 * FT)
            down_pe(pe, b0 + 2 * FT, t0 + 2 * FT, FT, h_hi, h_lo, h_ready, h0 + FT)

        def ffn_act(act, f):
            b0, t0 = BASE[f"ffn{f}"]
            with act.Fori(0, FT // 2) as i:
                for s in range(2):
                    for g in range(2):
                        split_hi(act, b0 + 2 * s + g + AHEAD, i, 4)
                    act.wait_ge(block_done, SPLIT + b0 + 2 * s + 1 + i * 4)
                    act.activation(gate_s[s][:], bank[(t0 + 2 * s) % BANKS][:], ACT.Silu).then_inc(silu_done, 1)
                    act.wait_ge(tile_free, BANKS + t0 + 2 * s + 2 + i * 4)
                    act.activation(h_hi[:, col(i * 2 + s)], prod[s][:], ACT.Copy).then_inc(h_hi_done, 1)
            down_act(act, b0 + 2 * FT, FT)

        def ffn_dve(dve, f):
            b0, t0 = BASE[f"ffn{f}"]
            with dve.Fori(0, FT // 2) as i:
                for s in range(2):
                    for g in range(2):
                        split_lo(dve, b0 + 2 * s + g + AHEAD, i, 4)
                    dve.wait_ge(silu_done, FT * f + s + 1 + i * 2)
                    dve.wait_ge(block_done, SPLIT + b0 + 2 * s + 2 + i * 4)
                    dve.tensor_tensor(prod[s][:], gate_s[s][:], bank[(t0 + 2 * s + 1) % BANKS][:], ALU.mult).then_inc(tile_free, 2)
                    dve.wait_ge(h_hi_done, FT * f + s + 1 + i * 2)
                    h = col(i * 2 + s)
                    dve.tensor_tensor(h_lo[:, h], prod[s][:], h_hi[:, h].bitcast(F32), ALU.subtract).then_inc(h_ready, 1)
            down_dve(dve, b0 + 2 * FT, t0 + 2 * FT, FT, 0.5)

        def gla_windows(g):
            return [f"{n}{d}_{g}" for d in range(g + 1) for n in ("head", "sum")] + [f"cnt{g}", f"rest{g}", f"less{g}"]

        gla_qkvg = tile("gla_qkvg", 9, 12)

        class Gla:
            b0, t0 = BASE["gla"]
            a_lr = tile("gla_a_lr", 8)
            q, k, v, g = ([gla_qkvg[:, n * T:n * T + T] for n in range(n0, n1)] for n0, n1 in ((0, 2), (2, 4), (4, 8), (8, 12)))
            g_all = gla_qkvg[:, 8 * T:12 * T]
            u = [tile(f"gla_u{n}", (21, 30, 31, 32)[n]) for n in range(4)]
            zb, az, cum, rel = ([tile(f"gla_{n}{m}", 33 + 2 * k + m) for m in range(2)]
                                for k, n in enumerate(("zb", "az", "cum", "rel")))
            v_tok = [tile(f"gla_v_tok{k}", 41 + k) for k in range(TT)]
            k_tok = [tile(f"gla_k_tok{m}", 45 + m) for m in range(2)]
            states = [tile(f"gla_states{m}", 33 + 2 * m, 2) for m in range(2)]
            probs = [tile(f"gla_probs{h}", (37, 38, 45, 46)[h]) for h in range(4)]
            o_sq, o_std, o_rs, o_n = tile("gla_o_sq", 13), tile("gla_o_std", 39), a_lr, tile("gla_o_n", 40)
            reset = tile("gla_reset", 47)
            win = [sumsq, rstd]
            e_mid, e_end, e_all, end = ([gla_cols[:, (2 * k + m) * GLA_CH:(2 * k + m + 1) * GLA_CH] for m in range(2)] for k in range(4))
            run_s, add_s = tile("gla_state", 14)[:, 0:P], tile("gla_add", 15)[:, 0:P]

            pe = Steps(sem("gla_pe"), ["z0", "z1"] + [f"vt{t}" for t in range(TT)] + ["kt0", "kt1"]
                       + ["kv00", "kv01", "kv10", "kv11"] + [f"sc{h}" for h in range(4)]
                       + [f"{n}{h}" for h in range(4) for n in ("o", "sum")] + [f"pw{g}" for g in range(4)])
            act = Steps(sem("gla_act"), [f"{n}{m}" for m in range(2) for n in ("zb", "az", "ez", "lz")]
                        + [f"{n}{m}" for m in range(2) for n in ("eq", "ek", "e_mid", "e_all", "e_end")]
                        + [f"vt{t}" for t in range(TT)] + ["kt0", "kt1", "silu"]
                        + [f"{n}{h}" for h in range(4) for n in ("sq", "std")] + [f"hi{h}" for h in range(8)])
            dve = Steps(sem("gla_dve"), [f"{n}{m}" for m in range(2) for n in ("la", "cum", "rel", "end")]
                        + ["q0", "k0", "q1", "k1"]
                        + [f"{n}{m}{c}" for m in range(2) for c in range(GLA_CH - 1) for n in ("add", "state", "scaled")]
                        + [f"pr{h}" for h in range(4)] + [f"{n}{h}" for h in range(4) for n in ("rs", "on")]
                        + [f"pw{g}" for g in range(4)] + [f"lo{h}" for h in range(8)])
            pool = Steps(sem("gla_pool"), ["ones", "reset"] + [n for g in range(4) for n in gla_windows(g)]
                         + [f"og{h}" for h in range(4)])

            def out(h):
                return Gla.g[h] if h < 4 else Gla.u[h - 4]

        def gla_sp(sp):
            w, b0 = a["even_w_in"][0], Gla.b0
            load(sp, b0, weight_cols(w, slice(1536, 1552)), cols=(0, 16))
            project_sp(sp, w, b0 + 1, 12, 0)
            project_sp(sp, w, b0 + 13, 4, 1552)
            down_sp(sp, a["even_w_out"][0], b0 + GLA_P, KT)

        def gla_taken(k):
            return tile_free, BANKS + Gla.t0 + k + 1

        def c3(x):
            return x[:, :].rearrange("p (c j) -> p c j", j=GLA_CHUNK)

        def gla_pe(pe, run):
            G, s = Gla, Gla.pe
            project_pe(pe, run, G.b0, G.t0, 1)
            project_pe(pe, run, G.b0 + 1, G.t0 + 1, 12)
            project_pe(pe, run, G.b0 + 13, G.t0 + 13, 4)
            pe.wait_ge(*gla_taken(0))
            for m in range(2):
                pe.matmul(bank[4 + m][:], gate_w[:, m * P:m * P + P], G.a_lr[0:16, :], start=True, stop=True).then_inc(*s.done(f"z{m}"))
            pe.wait_ge(*gla_taken(8))
            for t in range(TT):
                if t >= 2:
                    pe.wait_ge(*G.act.after(f"vt{t - 2}"))
                for h in range(4):
                    mm = pe.transpose(bank[6 + t % 2][:, h * P:h * P + P], G.v[h][:, t * P:t * P + P], ident[:])
                mm.then_inc(*s.done(f"vt{t}"))
            for m in range(2):
                pe.wait_ge(*G.dve.after(f"k{m}"))
                for t in range(TT):
                    mm = pe.transpose(bank[4 + m][:, t * P:t * P + P], G.k[m][:, t * P:t * P + P], ident[:])
                mm.then_inc(*s.done(f"kt{m}"))
            for m in range(2):
                pe.wait_ge(*G.act.after(f"kt{m}"))
                for f in range(2):
                    if m:
                        pe.wait_ge(*G.dve.after(f"add0{(6, 5)[f]}"))
                    for c in range(f, GLA_CH - 1, 2):
                        r = slice(64 * f, 64 * f + 64)
                        for hh in range(2):
                            mm = pe.matmul(bank[6 + f][64 * hh:64 * hh + 64, (c // 2) * P:(c // 2) * P + P],
                                           G.k_tok[m][r, (c // 2) * P + 64 * hh:(c // 2) * P + 64 * hh + 64],
                                           G.v_tok[c // 2][r, (2 * m + hh) * P:(2 * m + hh + 1) * P], start=True, stop=True)
                    mm.then_inc(*s.done(f"kv{m}{f}"))
            for h in range(4):
                m, r = h // 2, slice(64 * (h % 2), 64 * (h % 2) + 64)
                if h >= 2:
                    pe.wait_ge(*G.dve.after(f"pr{h - 2}"))
                for c in range(GLA_CH):
                    x = slice(c * 64, c * 64 + 64)
                    mm = pe.matmul(bank[4 + h % 2][64 * (c % 2):64 * (c % 2) + 64, (c // 2) * 64:(c // 2) * 64 + 64],
                                   G.k[m][r, x], G.q[m][r, x], start=True, stop=True)
                mm.then_inc(*s.done(f"sc{h}"))
            pe.wait_ge(*G.dve.after("pr3"))
            for h in range(4):
                m, r = h // 2, slice(64 * (h % 2), 64 * (h % 2) + 64)
                if h >= 2:
                    pe.wait_ge(*G.dve.after(f"on{h - 2}"))
                for c in range(GLA_CH):
                    x = slice(c * 64, c * 64 + 64)
                    if c % 2 == 0:
                        y = slice(c * 64, c * 64 + P)
                        pe.matmul(bank[6 + h % 2][:, y], G.v_tok[c // 2][:, h * P:h * P + P], G.probs[h][:, y], start=True, stop=False)
                    if c:
                        mm = pe.matmul(bank[6 + h % 2][:, x], G.states[m][r, c * P:c * P + P], G.q[m][r, x], start=False, stop=c % 2 == 1)
                mm.then_inc(*s.done(f"o{h}"))
                pe.wait_ge(*G.act.after(f"sq{h}"))
                pe.matmul(bank[4 + h % 2][:], ones[:], G.o_sq[:], start=True, stop=True).then_inc(*s.done(f"sum{h}"))
            for g in range(4):
                pe.wait_ge(*(G.act.after("std3") if g < 2 else G.dve.after(f"pw{g - 2}")))
                pe.wait_ge(*G.pool.after(f"less{g}"))
                pe.matmul(bank[4 + g % 2][:], pool_w[:, g * P:g * P + P], G.u[g][:], start=True, stop=True).then_inc(*s.done(f"pw{g}"))
            down_pe(pe, G.b0 + GLA_P, G.t0 + GLA_P, KT, h_hi, h_lo, *G.dve.after("lo7"))

        def gla_act(act):
            G, s = Gla, Gla.act
            project_act(act, G.b0, 1)
            project_act(act, G.b0 + 1, 12)
            project_act(act, G.b0 + 13, 4)
            for m in range(2):
                gb = par[:, R_GATEB + m:R_GATEB + m + 1]
                act.wait_ge(*G.pe.after(f"z{m}"))
                act.activation(G.zb[m][:], bank[4 + m][:], ACT.Identity, bias=gb).then_inc(*s.done(f"zb{m}"))
                act.activation(G.az[m][:], bank[4 + m][:], ACT.Abs, bias=gb).then_inc(*s.done(f"az{m}"))
                act.wait_ge(*s.after(f"az{m}"))
                act.activation(G.rel[m][:], G.az[m][:], ACT.Exp, scale=-1.0).then_inc(*s.done(f"ez{m}"))
                act.wait_ge(*s.after(f"ez{m}"))
                act.activation(G.az[m][:], G.rel[m][:], ACT.Ln, bias=1.0).then_inc(*s.done(f"lz{m}"))
            for m in range(2):
                tau = 1.0 / GLA_TAU
                act.wait_ge(*G.dve.after(f"rel{m}"))
                act.activation(G.zb[m][:], G.rel[m][:], ACT.Exp, scale=tau).then_inc(*s.done(f"eq{m}"))
                act.activation(G.az[m][:], G.rel[m][:], ACT.Exp, scale=-tau).then_inc(*s.done(f"ek{m}"))
                act.activation(G.e_mid[m], c3(G.cum[m])[:, :, 31], ACT.Exp, scale=tau).then_inc(*s.done(f"e_mid{m}"))
                act.activation(G.e_all[m], c3(G.cum[m])[:, :, 63], ACT.Exp, scale=tau).then_inc(*s.done(f"e_all{m}"))
                act.wait_ge(*G.dve.after(f"end{m}"))
                act.activation(G.e_end[m], G.end[m], ACT.Exp, scale=tau).then_inc(*s.done(f"e_end{m}"))
            for t in range(TT):
                act.wait_ge(*G.pe.after(f"vt{t}"))
                act.activation(G.v_tok[t][:], bank[6 + t % 2][:], ACT.Copy).then_inc(*s.done(f"vt{t}"))
            for m in range(2):
                act.wait_ge(*G.pe.after(f"kt{m}"))
                act.activation(G.k_tok[m][:], bank[4 + m][:], ACT.Copy).then_inc(*s.done(f"kt{m}"))
            act.wait_ge(*gla_taken(12))
            act.activation(G.g_all[:], G.g_all[:], ACT.Silu).then_inc(*s.done("silu"))
            for h in range(4):
                act.wait_ge(*G.pe.after(f"o{h}"))
                act.activation(G.o_sq[:], bank[6 + h % 2][:], ACT.Square).then_inc(*s.done(f"sq{h}"))
                act.wait_ge(*G.pe.after(f"sum{h}"))
                if h:
                    act.wait_ge(*G.dve.after(f"rs{h - 1}"))
                act.activation(G.o_std[:], bank[4 + h % 2][:], ACT.Sqrt, bias=eps_c, scale=1.0 / P).then_inc(*s.done(f"std{h}"))
            for h in range(8):
                act.wait_ge(*(G.pool.after(f"og{h}") if h < 4 else G.dve.after(f"pw{h - 4}")))
                act.activation(h_hi[:, h * T:h * T + T], G.out(h)[:], ACT.Copy).then_inc(*s.done(f"hi{h}"))
            down_act(act, G.b0 + GLA_P, KT)

        def gla_dve(dve):
            G, s = Gla, Gla.dve

            project_dve(dve, G.b0, G.t0, 1, lambda k, src: dve.tensor_copy(G.a_lr[:], src))
            project_dve(dve, G.b0 + 1, G.t0 + 1, 12, lambda k, src: dve.tensor_copy(gla_qkvg[:, col(k)], src))
            project_dve(dve, G.b0 + 13, G.t0 + 13, 4, lambda k, src: dve.tensor_copy(G.u[k][:], src))
            for m in range(2):
                dve.wait_ge(*G.act.after(f"lz{m}"))
                dve.scalar_tensor_tensor(G.zb[m][:], G.zb[m][:], 0.0, G.az[m][:], ALU.min, ALU.subtract).then_inc(*s.done(f"la{m}"))
                dve.wait_ge(*s.after(f"la{m}"))
                dve.wait_ge(*G.pool.after("reset"))
                dve.tensor_tensor_scan(G.cum[m][:], G.reset[:], G.zb[m][:], 0.0, ALU.mult, ALU.add).then_inc(*s.done(f"cum{m}"))
                dve.wait_ge(*s.after(f"cum{m}"))
                b = c3(G.cum[m])
                dve.tensor_tensor(c3(G.rel[m]), b, b[:, :, 31:32].to_broadcast([P, GLA_CH, GLA_CHUNK]),
                                  ALU.subtract).then_inc(*s.done(f"rel{m}"))
                dve.tensor_tensor(G.end[m], b[:, :, 63], b[:, :, 31], ALU.subtract).then_inc(*s.done(f"end{m}"))
            for m in range(2):
                dve.wait_ge(*G.act.after(f"ek{m}"))
                dve.scalar_tensor_tensor(G.q[m][:], G.q[m][:], GLA_DK ** -0.5, G.zb[m][:], ALU.mult, ALU.mult).then_inc(*s.done(f"q{m}"))
                dve.tensor_tensor(G.k[m][:], G.k[m][:], G.az[m][:], ALU.mult).then_inc(*s.done(f"k{m}"))
            for m in range(2):
                dve.wait_ge(*G.act.after(f"e_end{m}"))
                for c in range(GLA_CH - 1):
                    kv = bank[6 + c % 2][:, (c // 2) * P:(c // 2) * P + P]
                    if c < 2:
                        dve.wait_ge(*G.pe.after(f"kv{m}{c}"))
                    if c or m:
                        dve.wait_ge(*s.after(f"scaled{m}{c - 1}" if c else f"scaled0{GLA_CH - 2}"))
                    dve.tensor_scalar(G.add_s, kv, G.e_end[m][:, c:c + 1], None, ALU.mult).then_inc(*s.done(f"add{m}{c}"))
                    dve.wait_ge(*s.after(f"add{m}{c}"))
                    if c:
                        dve.scalar_tensor_tensor(G.run_s, G.run_s, G.e_all[m][:, c:c + 1], G.add_s,
                                                 ALU.mult, ALU.add).then_inc(*s.done(f"state{m}{c}"))
                    else:
                        dve.tensor_copy(G.run_s, G.add_s).then_inc(*s.done(f"state{m}{c}"))
                    dve.wait_ge(*s.after(f"state{m}{c}"))
                    dve.tensor_scalar(G.states[m][:, (c + 1) * P:(c + 2) * P], G.run_s, G.e_mid[m][:, c + 1:c + 2], None,
                                      ALU.mult).then_inc(*s.done(f"scaled{m}{c}"))
            for h in range(4):
                dve.wait_ge(*G.pe.after(f"sc{h}"))
                halves = [P, TT, 2, GLA_CHUNK]
                dve.tensor_tensor(G.probs[h][:, :].rearrange("p (t r j) -> p t r j", r=2, j=GLA_CHUNK),
                                  bank[4 + h % 2][:, 0:T // 2].rearrange("p (t r j) -> p t r j", r=1, j=GLA_CHUNK).to_broadcast(halves),
                                  chunk_T[:, :].rearrange("p (t r j) -> p t r j", t=1, r=2).to_broadcast(halves),
                                  ALU.mult).then_inc(*s.done(f"pr{h}"))
            for h in range(4):
                dve.wait_ge(*G.act.after(f"std{h}"))
                if h:
                    dve.wait_ge(*s.after(f"on{h - 1}"))
                dve.reciprocal(G.o_rs[:], G.o_std[:]).then_inc(*s.done(f"rs{h}"))
                dve.wait_ge(*s.after(f"rs{h}"))
                if h:
                    dve.wait_ge(*G.pool.after(f"og{h - 1}"))
                dve.scalar_tensor_tensor(G.o_n[:], bank[6 + h % 2][:], par[:, R_GLAN + h:R_GLAN + h + 1], G.o_rs[:],
                                         ALU.mult, ALU.mult).then_inc(*s.done(f"on{h}"))
            for g in range(4):
                dve.wait_ge(*G.pe.after(f"pw{g}"))
                dve.tensor_scalar(G.u[g][:], bank[4 + g % 2][:], par[:, R_POOLS + g:R_POOLS + g + 1], None,
                                  ALU.mult).then_inc(*s.done(f"pw{g}"))
            for h in range(8):
                dve.wait_ge(*G.act.after(f"hi{h}"))
                x = slice(h * T, h * T + T)
                dve.tensor_tensor(h_lo[:, x], G.out(h)[:], h_hi[:, x].bitcast(F32), ALU.subtract).then_inc(*s.done(f"lo{h}"))
            down_dve(dve, G.b0 + GLA_P, G.t0 + GLA_P, KT, 1.0)

        def gla_pool(pool):
            G, s = Gla, Gla.pool
            pool.wait_ge(*gla_taken(0))
            pool.memset(G.reset[:], 1.0).then_inc(*s.done("ones"))
            pool.wait_ge(*s.after("ones"))
            pool.memset(c3(G.reset)[:, :, 0:1], 0.0).then_inc(*s.done("reset"))
            for g in range(POOL_GROUPS):
                pool.wait_ge(*gla_taken(13 + g))
                src = G.u[g]
                for d in range(g + 1):
                    w, dst = 2 ** d, G.win[d % 2]
                    pool.tensor_copy(dst[:, 0:w], src[:, 0:w]).then_inc(*s.done(f"head{d}_{g}"))
                    pool.tensor_tensor(dst[:, w:T], src[:, w:T], src[:, 0:T - w], ALU.add).then_inc(*s.done(f"sum{d}_{g}"))
                    pool.wait_ge(*s.after(f"sum{d}_{g}"))
                    src = dst
                pool.tensor_tensor(src[:, 0:16], src[:, 0:16], inv_count[:, 16 * g:16 * g + 16], ALU.mult).then_inc(*s.done(f"cnt{g}"))
                pool.tensor_scalar(src[:, 16:T], src[:, 16:T], 2.0 ** -(g + 1), None, ALU.mult).then_inc(*s.done(f"rest{g}"))
                pool.wait_ge(*s.after(f"rest{g}"))
                pool.tensor_tensor(G.u[g][:], src[:], G.u[g][:], ALU.subtract).then_inc(*s.done(f"less{g}"))
                pool.wait_ge(*s.after(f"less{g}"))
            pool.wait_ge(*G.act.after("silu"))
            for h in range(4):
                pool.wait_ge(*G.dve.after(f"on{h}"))
                pool.tensor_tensor(G.g[h][:], G.o_n[:], G.g[h][:], ALU.mult).then_inc(*s.done(f"og{h}"))

        nmax, rowsum, rinv = (small[:, 8 + 8 * k:16 + 8 * k] for k in range(3))

        def pipelined(units, first, second, third):
            out = [first(0)]
            for u in range(units):
                if u + 1 < units:
                    out.append(first(u + 1))
                out.append(second(u))
                if u and third:
                    out.append(third(u - 1))
            if third:
                out.append(third(units - 1))
            return out

        def att_names(units):
            return dict(pe=pipelined(units, "s{}".format, "pt{}".format, "pv{}".format),
                        dve=[n for ns in pipelined(units, lambda u: [f"mx{u}", f"nm{u}"], lambda u: [f"ri{u}"], None) for n in ns],
                        act=pipelined(units, "ex{}".format, "pc{}".format, None),
                        pool=[f"pn{u}" for u in range(units)])

        def att_pe(pe, S, turn, units, width, scores, values, p, pT):
            def score(u):
                if u >= 2:
                    pe.wait_ge(*S.act.after(f"ex{u - 2}", turn))
                scores(u, bank[4 + u % 2][:, 0:width(u)]).then_inc(*S.pe.done(f"s{u}"))

            def turned(u):
                pe.wait_ge(*S.pool.after(f"pn{u}", turn))
                if u >= 2:
                    pe.wait_ge(*S.act.after(f"pc{u - 2}", turn))
                for j in range(width(u) // P):
                    mm = pe.transpose(bank[(6, 1)[u % 2]][:, j * P:j * P + P], p[u % 2][:, j * P:j * P + P], ident[:])
                mm.then_inc(*S.pe.done(f"pt{u}"))

            def value(u):
                pe.wait_ge(*S.act.after(f"pc{u}", turn))
                out, n = values(u)
                for j in range(width(u) // P):
                    mm = pe.matmul(out, n(j), pT[u % 2][:, j * P:j * P + P], start=j == 0, stop=(j + 1) * P == width(u))
                mm.then_inc(*S.pe.done(f"pv{u}"))
            pipelined(units, score, turned, value)

        def att_dve(dve, S, turn, units, width, scale):
            def top(u):
                dve.wait_ge(*S.pe.after(f"s{u}", turn))
                dve.tensor_reduce(rowsum[:, u:u + 1], bank[4 + u % 2][:, 0:width(u)], AX.X, ALU.max).then_inc(*S.dve.done(f"mx{u}"))
                dve.wait_ge(*S.dve.after(f"mx{u}", turn))
                dve.tensor_scalar(nmax[:, u:u + 1], rowsum[:, u:u + 1], -scale, None, ALU.mult).then_inc(*S.dve.done(f"nm{u}"))

            def inverse(u):
                dve.wait_ge(*S.act.after(f"ex{u}", turn))
                dve.reciprocal(rinv[:, u:u + 1], rowsum[:, u:u + 1]).then_inc(*S.dve.done(f"ri{u}"))
            pipelined(units, top, inverse, None)

        def att_act(act, S, turn, units, width, scale, p, pT):
            def exponentials(u):
                act.wait_ge(*S.dve.after(f"nm{u}", turn))
                act.activation(p[u % 2][:, 0:width(u)], bank[4 + u % 2][:, 0:width(u)], ACT.Exp, bias=nmax[:, u:u + 1],
                               scale=scale, accum_out=rowsum[:, u:u + 1]).then_inc(*S.act.done(f"ex{u}"))

            def copies(u):
                act.wait_ge(*S.pe.after(f"pt{u}", turn))
                if u >= 2:
                    act.wait_ge(*S.pe.after(f"pv{u - 2}", turn))
                act.activation(pT[u % 2][:, 0:width(u)], bank[(6, 1)[u % 2]][:, 0:width(u)], ACT.Copy).then_inc(*S.act.done(f"pc{u}"))
            pipelined(units, exponentials, copies, None)

        def att_pool(pool, S, turn, units, width, p):
            for u in range(units):
                pool.wait_ge(*S.dve.after(f"ri{u}", turn))
                x = p[u % 2][:, 0:width(u)]
                pool.tensor_tensor(x, x, rinv[:, u:u + 1].to_broadcast([P, width(u)]), ALU.mult).then_inc(*S.pool.done(f"pn{u}"))

        dsa_qkv = tile("dsa_qkv", 30, 12)

        class Dsa:
            b0, t0 = BASE["dsa"]
            kk, wi, qi = tile("dsa_kk", 8), tile("dsa_wi", 9), [tile(f"dsa_qi{m}", 10 + m) for m in range(2)]
            qkv = dsa_qkv
            k, v = ([dsa_qkv[:, n * T:n * T + T] for n in range(n0, n0 + 2)] for n0 in (8, 10))
            cos, sin = [tile(f"dsa_cos{m}", 12 + m) for m in range(2)], [tile(f"dsa_sin{m}", 14 + m) for m in range(2)]
            bias = [tile(f"dsa_bias{t}", 16 + t) for t in range(TT)]
            v_tok = tile("dsa_v_tok", 20, 2)
            work = [None, tile("dsa_work1", 42), tile("dsa_work2", 43), tile("dsa_work3", 46)]
            relu = [tile(f"dsa_relu{m}", 44 + m) for m in range(2)]
            part = tile("dsa_part", 47)
            part2 = tile("dsa_part2", 44)
            q_cur = [tile(f"dsa_q_cur{m}", 42 + m) for m in range(2)]
            p, pT = [tile(f"dsa_p{m}", 8 + m) for m in range(2)], [tile(f"dsa_pT{m}", 10 + m) for m in range(2)]
            pos = nc.alloc_sbuf_tensor_at("dsa_pos", [P, T], I32, offset=arena + 42 * T * 4)
            posf, ang, turns_ = tile("dsa_posf", 43), tile("dsa_ang", 44), tile("dsa_turns", 45)
            wi_tok, top8 = small[:, 32:48], small[:, 48:56]
            ropes = ["kk", "qi0", "qi1"]
            late = ["k0", "k1"]
            n_angle = ("ang", "near", "whole", "r1", "r2", "r3", "r4")
            rounds = TOPK // 8
            pos_loaded = sem("dsa_pos_loaded")
            pe = Steps(sem("dsa_pe"), ["wt"] + [f"sw_{n}" for n in ropes] + [f"is{t}{h}" for t in range(1, TT) for h in range(IDX_HEADS)]
                       + ["sw_k0", "sw_k1", "vt0", "vt1"])
            act = Steps(sem("dsa_act"), [f"{n}{m}" for m in range(2) for n in ("sin", "abs", "cos")]
                        + [f"rl{t}{h}" for t in range(1, TT) for h in range(IDX_HEADS)] + ["vt0", "vt1"])
            dve = Steps(sem("dsa_dve"), ["posf"] + [f"{n}{m}" for m in range(2) for n in ("ang", "near", "whole", "r1", "r2", "r3", "r4")]
                        + ["wt"] + [f"{n}_{r}" for r in ("kk", "qi0", "qi1") for n in ("sw", "add")]
                        + [n for t in range(1, TT) for n in [f"ac{t}{h}" for h in range(IDX_HEADS)] + [f"diag{t}"] + [f"rest{t}"] * (t < TT - 1)]
                        + [f"{n}{t}_{k}" for t in range(1, TT) for k in range(TOPK // 8) for n in ("top", "out")]
                        + ["bias0", "bias1", "bias2", "bias3"] + [f"{n}_{r}" for r in ("k0", "k1") for n in ("sw", "add")])
            pool = Steps(sem("dsa_pool"), [f"cos_{r}" for r in ("kk", "qi0", "qi1", "k0", "k1")])

        class DsaHead:
            n = att_names(TT)
            pe = Steps(sem("dsa_head_pe"), ["sw"] + n["pe"], 1)
            act = Steps(sem("dsa_head_act"), n["act"] + ["hi"], 1)
            dve = Steps(sem("dsa_head_dve"), ["sw", "q"] + n["dve"] + ["lo"], 1)
            pool = Steps(sem("dsa_head_pool"), ["cos"] + n["pool"], 1)

        def dsa_taken(k):
            return tile_free, BANKS + Dsa.t0 + k + 1

        def dsa_heads(eng, body):
            for g in range(ATT_KV):
                with eng.Fori(0, ATT_HEADS // ATT_KV // 2) as i:
                    for m in range(2):
                        body(i * 2 + (g * (ATT_HEADS // ATT_KV) + m), g, m)

        def width4(u):
            return (u + 1) * P

        def dsa_sp(sp):
            b0, w = Dsa.b0, a["odd_w_in"][0]
            ki = weight_cols(w, slice(1792, 1856))
            load_pair(sp, b0, 0, ((ki, (0, 64)), (ki, (64, P))))
            load(sp, b0 + 1, weight_cols(w, slice(1856, 1860)), cols=(0, 4))
            for m in range(2):
                load(sp, b0 + 2 + m, weight_cols(w, slice(1536 + m * P, 1536 + m * P + P)))
            project_sp(sp, w, b0 + 4, 12, 0)
            down_sp(sp, a["odd_w_out"][0], b0 + DSA_P, KT)

        def rope_tile(r):
            return {"kk": Dsa.kk, "qi0": Dsa.qi[0], "qi1": Dsa.qi[1], "k0": Dsa.k[0], "k1": Dsa.k[1]}[r]

        def dsa_pe(pe, run):
            S, H, s = Dsa, DsaHead, Dsa.pe
            project_pe(pe, run, S.b0, S.t0, 4)
            pe.wait_ge(*dsa_taken(1))
            for t in range(TT):
                mm = pe.transpose(bank[7][:, 4 * t:4 * t + 4], S.wi[0:4, t * P:t * P + P], ident[0:4, 0:4])
            mm.then_inc(*s.done("wt"))

            def swap(r, k):
                pe.wait_ge(*dsa_taken({"kk": 0, "qi0": 2, "qi1": 3, "k0": 12, "k1": 13}[r]))
                m = (swap64 if k < 3 else swap128)
                pe.matmul(bank[4 + k][:] if k < 3 else bank[k + 1][:], m[:], rope_tile(r)[:], start=True, stop=True).then_inc(*s.done(f"sw_{r}"))
            for k, r in enumerate(S.ropes):
                swap(r, k)
            for t in range(1, TT):
                for h in range(IDX_HEADS):
                    x = slice(64 * (h % 2), 64 * (h % 2) + 64)
                    if t == 1:
                        pe.wait_ge(*S.dve.after("add_qi1"))
                    else:
                        pe.wait_ge(*S.act.after(f"rl{t - 1}{h}"))
                    pe.matmul(bank[4 + h][:], S.qi[h // 2][x, t * P:t * P + P], S.kk[x, :], start=True, stop=True).then_inc(*s.done(f"is{t}{h}"))
            project_pe(pe, run, S.b0 + 4, S.t0 + 4, 12)
            pe.wait_ge(*S.act.after(f"rl3{IDX_HEADS - 1}"))
            for k, r in enumerate(S.late):
                swap(r, 3 + k)
            pe.wait_ge(*dsa_taken(15))
            for f in range(2):
                for t in range(2):
                    for g in range(2):
                        mm = pe.transpose(bank[6 + f][:, (2 * t + g) * P:(2 * t + g + 1) * P],
                                          S.v[g][:, (2 * f + t) * P:(2 * f + t + 1) * P], ident[:])
                mm.then_inc(*s.done(f"vt{f}"))
            pe.wait_ge(*S.dve.after("add_k1"))
            pe.wait_ge(*S.act.after("vt1"))
            pe.sem_inc(H.pe.sem, 1)

            def head(turn, g, m):
                pe.wait_ge(*H.dve.turns_before(turn))
                pe.matmul(bank[0][:], swap128[:], S.qkv[:, col(turn)], start=True, stop=True).then_inc(*H.pe.done("sw"))
                pe.wait_ge(*H.dve.after("q", turn))

                def scores(u, out):
                    pe.matmul(out, S.q_cur[m][:, u * P:u * P + P], S.k[g][:, 0:width4(u)], start=True, stop=False)
                    return pe.matmul(out, ident[:], S.bias[u][:, 0:width4(u)], start=False, stop=True)

                def values(u):
                    return bank[7][:, u * P:u * P + P], lambda j: S.v_tok[:, (2 * j + g) * P:(2 * j + g + 1) * P]
                att_pe(pe, H, turn, TT, width4, scores, values, S.p, S.pT)
            dsa_heads(pe, head)
            down_pe(pe, S.b0 + DSA_P, S.t0 + DSA_P, KT, h_hi, h_lo, *H.dve.turns_before(ATT_HEADS))

        def dsa_act(act):
            S, H, s = Dsa, DsaHead, Dsa.act
            act.dma_start(S.pos[:], a["positions"].to_broadcast([P, T])).then_inc(S.pos_loaded, 16)
            project_act(act, S.b0, 4)
            for m in range(2):
                act.wait_ge(*S.dve.after(f"r4{m}"))
                act.activation(S.sin[m][:], S.ang[:], ACT.Sin).then_inc(*s.done(f"sin{m}"))
                act.activation(S.cos[m][:], S.ang[:], ACT.Abs).then_inc(*s.done(f"abs{m}"))
                act.wait_ge(*s.after(f"abs{m}"))
                act.activation(S.cos[m][:], S.cos[m][:], ACT.Sin, bias=half_pi, scale=-1.0).then_inc(*s.done(f"cos{m}"))
            for t in range(1, TT):
                for h in range(IDX_HEADS):
                    act.wait_ge(*S.pe.after(f"is{t}{h}"))
                    n = IDX_HEADS * (t - 1) + h
                    if n >= 2:
                        tt, hh = divmod(n - 2, IDX_HEADS)
                        act.wait_ge(*S.dve.after(f"ac{tt + 1}{hh}"))
                    act.activation(S.relu[n % 2][:], bank[4 + h][:], ACT.Relu).then_inc(*s.done(f"rl{t}{h}"))
            project_act(act, S.b0 + 4, 12)
            for f in range(2):
                act.wait_ge(*S.pe.after(f"vt{f}"))
                act.activation(S.v_tok[:, f * T:f * T + T], bank[6 + f][:], ACT.Copy).then_inc(*s.done(f"vt{f}"))
            act.sem_inc(H.act.sem, 1)

            def head(turn, g, m):
                act.wait_ge(*H.dve.turns_before(turn))
                att_act(act, H, turn, TT, width4, ATT_DH ** -0.5, S.p, S.pT)
                act.wait_ge(*H.pe.after("pv3", turn))
                act.activation(h_hi[:, col(turn)], bank[7][:], ACT.Copy).then_inc(*H.act.done("hi"))
            dsa_heads(act, head)
            down_act(act, S.b0 + DSA_P, KT)

        def dsa_dve(dve):
            S, H, s = Dsa, DsaHead, Dsa.dve
            project_dve(dve, S.b0, S.t0, 4, lambda k, src: dve.tensor_copy([S.kk, S.wi, S.qi[0], S.qi[1]][k][:], src))
            dve.wait_ge(S.pos_loaded, 16)
            dve.tensor_copy(S.posf[:], S.pos[:]).then_inc(*s.done("posf"))
            dve.wait_ge(*s.after("posf"))
            for m, row in enumerate((R_INV128, R_INV64)):
                if m:
                    dve.wait_ge(*S.act.after("abs0"))
                dve.tensor_scalar(S.ang[:], S.posf[:], par[:, row:row + 1], None, ALU.mult).then_inc(*s.done(f"ang{m}"))
                dve.wait_ge(*s.after(f"ang{m}"))
                dve.tensor_scalar(S.turns_[:], S.ang[:], 1.0 / TWO_PI, ROUND, ALU.mult, ALU.add).then_inc(*s.done(f"near{m}"))
                dve.wait_ge(*s.after(f"near{m}"))
                dve.tensor_scalar(S.turns_[:], S.turns_[:], -ROUND, None, ALU.add).then_inc(*s.done(f"whole{m}"))
                dve.wait_ge(*s.after(f"whole{m}"))
                for k, c in enumerate((PI_A, PI_B, PI_C)):
                    dve.scalar_tensor_tensor(S.ang[:], S.turns_[:], -c, S.ang[:], ALU.mult, ALU.add).then_inc(*s.done(f"r{k + 1}{m}"))
                    dve.wait_ge(*s.after(f"r{k + 1}{m}"))
                dve.tensor_scalar(S.ang[:], S.ang[:], 3.1415925, -3.1415925, ALU.min, ALU.max).then_inc(*s.done(f"r4{m}"))
            dve.wait_ge(*S.pe.after("wt"))
            dve.tensor_scalar(S.wi_tok, bank[7][:, 0:16], IDX_DIM ** -0.5 * IDX_HEADS ** -0.5, None, ALU.mult).then_inc(*s.done("wt"))

            def rotate(r, bk, m):
                dve.wait_ge(*S.pe.after(f"sw_{r}"))
                dve.wait_ge(*S.act.after("cos1"))
                if r != "kk":
                    dve.wait_ge(*s.after({"qi0": "add_kk", "qi1": "add_qi0", "k0": "bias3", "k1": "add_k0"}[r]))
                dve.tensor_tensor(S.part2[:], bank[bk][:], S.sin[m][:], ALU.mult).then_inc(*s.done(f"sw_{r}"))
                dve.wait_ge(*s.after(f"sw_{r}"))
                dve.wait_ge(*S.pool.after(f"cos_{r}"))
                dve.tensor_tensor(rope_tile(r)[:], S.part[:], S.part2[:], ALU.add).then_inc(*s.done(f"add_{r}"))
            for k, r in enumerate(S.ropes):
                rotate(r, 4 + k, 1)
            for t in range(1, TT):
                for h in range(IDX_HEADS):
                    dve.wait_ge(*S.act.after(f"rl{t}{h}"))
                    r, w = S.relu[h % 2][:], S.wi_tok[:, 4 * t + h:4 * t + h + 1]
                    if h == 0:
                        dve.tensor_scalar(S.work[t][:], r, w, None, ALU.mult).then_inc(*s.done(f"ac{t}{h}"))
                    else:
                        dve.wait_ge(*s.after(f"ac{t}{h - 1}"))
                        dve.scalar_tensor_tensor(S.work[t][:], r, w, S.work[t][:], ALU.mult, ALU.add).then_inc(*s.done(f"ac{t}{h}"))
                dve.wait_ge(*s.after(f"ac{t}{IDX_HEADS - 1}"))
                x = slice(t * P, t * P + P)
                dve.tensor_tensor(S.work[t][:, x], S.work[t][:, x], causal[:], ALU.add).then_inc(*s.done(f"diag{t}"))
                if t < TT - 1:
                    dve.memset(S.work[t][:, (t + 1) * P:T], NEG).then_inc(*s.done(f"rest{t}"))
            dve.wait_ge(*s.after("diag3"))
            for u in range(12):
                split_lo(dve, S.b0 + 4 + u + AHEAD)
                dve.wait_ge(block_done, SPLIT + S.b0 + 4 + u + 1)
                dve.tensor_copy(S.qkv[:, u * T:u * T + T], bank[(S.t0 + 4 + u) % BANKS][:]).then_inc(tile_free, 1)
                t = 1 + u // 4
                w = S.work[t][:, 0:width4(t)]
                for k in range(4 * (u % 4), 4 * (u % 4) + 4):
                    if k or t > 1:
                        dve.wait_ge(*s.after(f"out{t}_{k - 1}" if k else f"out{t - 1}_{S.rounds - 1}"))
                    dve.max(S.top8, w).then_inc(*s.done(f"top{t}_{k}"))
                    dve.wait_ge(*s.after(f"top{t}_{k}"))
                    dve.match_replace(w, S.top8, w, TAKEN).then_inc(*s.done(f"out{t}_{k}"))
            dve.wait_ge(*s.after(f"out3_{S.rounds - 1}"))
            dve.tensor_copy(S.bias[0][:, 0:P], causal[:]).then_inc(*s.done("bias0"))
            for t in range(1, TT):
                w = slice(0, width4(t))
                dve.tensor_scalar(S.bias[t][:, w], S.work[t][:, w], TAKEN / 2, NEG, ALU.is_gt, ALU.mult).then_inc(*s.done(f"bias{t}"))
            for k, r in enumerate(S.late):
                rotate(r, 4 + k, 0)
            dve.sem_inc(H.dve.sem, 1)

            def head(turn, g, m):
                dve.wait_ge(*H.pe.after("sw", turn))
                dve.tensor_tensor(S.part2[:], bank[0][:], S.sin[0][:], ALU.mult).then_inc(*H.dve.done("sw"))
                dve.wait_ge(*H.dve.after("sw", turn))
                dve.wait_ge(*H.pool.after("cos", turn))
                dve.tensor_tensor(S.q_cur[m][:], S.part[:], S.part2[:], ALU.add).then_inc(*H.dve.done("q"))
                att_dve(dve, H, turn, TT, width4, ATT_DH ** -0.5)
                dve.wait_ge(*H.act.after("hi", turn))
                dve.tensor_tensor(h_lo[:, col(turn)], bank[7][:], h_hi[:, col(turn)].bitcast(F32), ALU.subtract).then_inc(*H.dve.done("lo"))
            dsa_heads(dve, head)
            down_dve(dve, S.b0 + DSA_P, S.t0 + DSA_P, KT, 1.0)

        def dsa_pool(pool):
            S, H, s = Dsa, DsaHead, Dsa.pool
            pool.wait_ge(*dsa_taken(3))
            pool.wait_ge(*S.act.after("cos1"))
            for r in S.ropes + S.late:
                if r == "k0":
                    pool.wait_ge(*dsa_taken(13))
                if r != "kk":
                    pool.wait_ge(*S.dve.after({"qi0": "add_kk", "qi1": "add_qi0", "k0": "add_qi1", "k1": "add_k0"}[r]))
                pool.tensor_tensor(S.part[:], rope_tile(r)[:], S.cos[0 if r[0] == "k" and r != "kk" else 1][:], ALU.mult).then_inc(*s.done(f"cos_{r}"))
            pool.wait_ge(*S.dve.after("add_k1"))
            pool.sem_inc(H.pool.sem, 1)

            def head(turn, g, m):
                pool.wait_ge(*H.dve.turns_before(turn))
                pool.tensor_tensor(S.part[:], S.qkv[:, col(turn)], S.cos[0][:], ALU.mult).then_inc(*H.pool.done("cos"))
                att_pool(pool, H, turn, TT, width4, S.p)
            dsa_heads(pool, head)

        def ada_sp(sp):
            for m in range(2):
                project_sp(sp, a["ada_w_2"][m], BASE["ada"][0] + m * 3 * KT, 3 * KT, 0)

        def ada_act(act):
            project_act(act, BASE["ada"][0], ADA_P)

        def ada_pe(pe):
            b0, t0 = BASE["ada"]
            pe.wait_ge(cond_split, 2)

            def one(u, i, n):
                pe.wait_ge(tile_free, t0 + u + 1 + i * n)
                products(pe, b0 + u, bank[(t0 + u) % BANKS][:, 0:2], lambda k: cond_hi[:, 2 * k:2 * k + 2],
                         lambda k: cond_lo[:, 2 * k:2 * k + 2], range(KT), True, True, i, n)
            in_turns(pe, ADA_P, one)

        def ada_dve(dve):
            for k in range(KT):
                x = hres[:, k * T:k * T + T]
                dve.scalar_tensor_tensor(x, x, par[:, R_FINAL + k:R_FINAL + k + 1], rstd[:], ALU.mult, ALU.mult).then_inc(normed, 1)
            project_dve(dve, *BASE["ada"], ADA_P, lambda n, src: dve.tensor_tensor(
                mod[:, bass.ds(n, 1)], src[:, 0:1], par[:, bass.ds(n + R_ADAB, 1)], ALU.add))
            dve.wait_ge(tile_free, BANKS + BASE["ada"][1] + ADA_P)
            for m in range(2):
                s = 3 * KT * m + KT
                dve.scalar_tensor_tensor(gain2[:, m * KT:m * KT + KT], mod[:, s:s + KT], 1.0,
                                         par[:, R_NORM2 + m * KT:R_NORM2 + m * KT + KT], ALU.add, ALU.mult).then_inc(gain_done, 1)
            dve.wait_ge(gain_done, 2)

        gdn_cols = tile("gdn_cols", 22)

        def both(names):
            return [f"{n}_{h}" for n in names for h in range(2)]

        class Gdn:
            b0, t0 = BASE["gdn"]
            o = tile("gdn_o", 0, 16)
            qT, kT, k_tok, gates = tile("gdn_qT", 16), tile("gdn_kT", 17), tile("gdn_k_tok", 20), tile("gdn_gates", 21)
            zs = [tile(f"gdn_zs{h}", 18 + h) for h in range(2)]
            vb, kbg, kdec, qdec, attnT, E, Pw, W1, W2, W3, W4, W5 = (
                [tile(f"gdn_{n}{h}", 23 + 12 * h + k) for h in range(2)]
                for k, n in enumerate(("vb", "kbg", "kdec", "qdec", "attnT", "E", "P", "W1_", "W2_", "W3_", "W4_", "W5_")))
            gsel = [sumsq, rstd]
            beta, g, kd, egl, bexp, negb, eg, diff = (gdn_cols[:, 64 * k:64 * k + 64] for k in range(8))
            conv_to = [qT, kT, E[0], E[1]]
            raw, x, ax, ex = W1[0], W2[0], W3[0], W4[0]
            reset, last_row = W5[0], W1[1]
            prep_pe = Steps(sem("gdn_prep_pe"), ["turn", "last"])
            prep_act = Steps(sem("gdn_prep_act"), ["beta", "x", "ax", "ex", "ln", "ea", "eg", "egl", "kd"])
            prep_dve = Steps(sem("gdn_prep_dve"), ["sp", "g", "cum", "last_row", "beta", "gt", "diff", "bexp", "negb"])
            prep_pool = Steps(sem("gdn_prep_pool"), ["gates", "ones", "reset"])
            end_act = Steps(sem("gdn_end_act"), [f"hi{k}" for k in range(16)])
            end_dve = Steps(sem("gdn_end_dve"), [f"lo{k}" for k in range(16)])

        class GdnTurn:
            pe = Steps(sem("gdn_pe"), ["sum_q", "sum_k", "kt", "vt_0", "vt_1", "gb_0", "gb_1", "qk", "kk"]
                       + both(["at", "y1", "x2", "y2", "x4", "y4", "y8", "p1", "p2", "p3", "q3", "f", "g1", "f2", "g2", "v1", "f4", "v2", "tt", "wt"])
                       + [n for t in range(TT) for n in both([f"vn{t}"]) + [f"{n}{t}_{h}" for h in range(2) for n in (["o", "ds"] if t < TT - 1 else ["o"])]]
                       + both(["sum"]))
            act = Steps(sem("gdn_act"), [f"cw{u}" for u in range(4)] + [f"cs{u}" for u in range(4)] + ["sq_q", "sq_k", "sd_q", "sd_k", "zs0", "zs1", "kc"]
                        + both(["eg", "dec", "at", "y1", "y2", "y4", "y8", "q3", "g1", "g2", "f4", "tt", "wt"])
                        + [n for t in range(TT) for n in both([f"vn{t}"])] + both(["sq", "sd"]))
            dve = Steps(sem("gdn_dve"), [f"c{n}{u}" for u in range(4) for n in "ab"] + ["rc_q", "n_q", "rc_k", "n_k", "gs_0", "gs_1", "vb_0", "vb_1"]
                        + both(["da", "db"]) + both(["at", "kk"]) + both(["nb", "m"])
                        + both(["x2", "x4", "p1", "p2", "p3", "f", "v0", "f2", "v1", "v2"])
                        + [n for t in range(TT - 1) for n in both([f"s{t}"])] + [f"{n}_{h}" for h in range(2) for n in ("rc", "on", "o")], 1)
            pool = Steps(sem("gdn_pool"), both(["kd", "kb", "qd", "en", "p0"]))

        def gdn_turns(eng, body):
            with eng.Fori(0, GDN_QK // 2) as i:
                for m in range(2):
                    body(i * 2 + m, i, m)

        def gdn_block(m, u):
            return Gdn.b0 + 1 + 6 * m + u

        def gdn_bank(m, u):
            return bank[(Gdn.t0 + 1 + 6 * m + u) % BANKS]

        def gdn_taken(m, u, i):
            return tile_free, BANKS + Gdn.t0 + 1 + 6 * m + u + 1 + i * 12

        def first(h):
            return bank[(4, 7)[h]]

        def second(h):
            return bank[(5, 6)[h]]

        def t3(x):
            return x[:, :].rearrange("p (t c) -> p t c", c=P)

        def by_row(x):
            return x[:, :].rearrange("p (t c) -> p t c", t=1).to_broadcast([P, TT, P])

        def by_col(x, h):
            return x[:, bass.ds(h * TT, TT)].rearrange("p (t c) -> p t c", c=1).to_broadcast([P, TT, P])

        def gdn_sp(sp):
            w, b0 = a["a_w_in_2"][0], Gdn.b0
            load_pair(sp, b0, 1, tuple((weight_cols(w, slice(GDN_B + 16 * k, GDN_B + 16 * k + 16)), (32 * k, 32 * k + 16)) for k in range(2)))
            with sp.Fori(0, GDN_QK // 2) as i:
                for m in range(2):
                    for u, (c, width) in enumerate(((0, P), (GDN_QW, P), (2 * GDN_QW, 2 * P), (2 * GDN_QW + P, 2 * P),
                                                    (GDN_Z, 2 * P), (GDN_Z + P, 2 * P))):
                        load(sp, gdn_block(m, u), weight_cols(w, bass.ds(i * (2 * width) + (c + m * width), P)), i, 12)
            down_sp(sp, a["a_w_out_2"][0], b0 + GDN_P, 16)

        def gdn_pe(pe, run):
            G, H = Gdn, GdnTurn
            project_pe(pe, run, G.b0, G.t0, 1)
            s = G.prep_pe
            pe.wait_ge(*G.prep_act.after("beta"))
            pe.wait_ge(*G.prep_dve.after("cum"))
            for t in range(TT):
                mm = pe.transpose(bank[6][:, t * 48:t * 48 + 48], G.gates[0:48, t * P:t * P + P], ident[0:48, 0:48])
            mm.then_inc(*s.done("turn"))
            pe.wait_ge(*G.prep_dve.after("gt"))
            pe.wait_ge(*G.prep_dve.after("last_row"))
            pe.matmul(bank[7][:, 0:64], G.last_row[:, 0:P], G.g, start=True, stop=True).then_inc(*s.done("last"))

            def four(out, lhs, rhs, step):
                for t in range(TT):
                    x = slice(t * P, t * P + P)
                    mm = pe.matmul(out[:, x], lhs[:, x], rhs[:, x], start=True, stop=True)
                mm.then_inc(*H.pe.done(step))

            def turned(out, x, step):
                for t in range(TT):
                    c = slice(t * P, t * P + P)
                    mm = pe.transpose(out[:, c], x[:, c], ident[:])
                mm.then_inc(*H.pe.done(step))

            def turn(j, i, m):
                act, dve, pool = ((lambda n, S=S: pe.wait_ge(*S.after(n, j))) for S in (H.act, H.dve, H.pool))

                def project(u):
                    pe.wait_ge(tile_free, G.t0 + 1 + 6 * m + u + 1 + i * 12)
                    products(pe, gdn_block(m, u), gdn_bank(m, u)[:], x_of(x_hi), x_of(x_lo), range(KT), True, True, i, 12)
                for u in range(5):
                    project(u)
                act("sq_q")
                pe.matmul(first(0)[:], ones[:], G.Pw[0][:], start=True, stop=True).then_inc(*H.pe.done("sum_q"))
                act("sq_k")
                pe.matmul(second(1)[:], ones[:], G.Pw[1][:], start=True, stop=True).then_inc(*H.pe.done("sum_k"))
                project(5)
                dve("n_k")
                turned(second(0), G.kT, "kt")
                act("cs2")
                turned(first(1), G.E[0], "vt_0")
                act("cs3")
                act("sd_q")
                turned(first(0), G.E[1], "vt_1")
                for h in range(2):
                    act(("kc", "sd_k")[h])
                    dve(f"gs_{h}")
                    pe.matmul(second(h)[:], ones[32:48, :], G.gsel[h][32:48, :], start=True, stop=True).then_inc(*H.pe.done(f"gb_{h}"))
                dve("vb_0")
                four(first(1), G.qT, G.kT, "qk")
                dve("vb_1")
                four(first(0), G.kT, G.kT, "kk")
                for h in range(2):
                    act(f"eg_{h}")
                    dve(f"at_{h}")
                    turned(second(h), G.W2[h], f"at_{h}")
                for h in range(2):
                    dve(f"m_{h}")
                    dve(f"kk_1")
                    turned(first(h), G.W4[h], f"y1_{h}")
                for h in range(2):
                    act(f"at_{h}")
                    act(f"y1_{h}")
                    four(second(h), G.W1[h], G.W4[h], f"x2_{h}")
                for h in range(2):
                    four(first(h), G.W4[h], G.W1[h], f"y2_{h}")
                for h in range(2):
                    dve(f"x2_{h}")
                    act(f"y2_{h}")
                    four(second(h), G.W3[h], G.W2[h], f"x4_{h}")
                for h in range(2):
                    four(first(h), G.W2[h], G.W3[h], f"y4_{h}")
                for h in range(2):
                    dve(f"x4_{h}")
                    act(f"y4_{h}")
                    four(second(h), G.W1[h], G.W4[h], f"y8_{h}")
                for h in range(2):
                    pool(f"p0_{h}")
                    four(first(h), G.W3[h], G.Pw[h], f"p1_{h}")
                for h in range(2):
                    act(f"y8_{h}")
                    dve(f"p1_{h}")
                    four(second(h), G.W4[h], G.Pw[h], f"p2_{h}")
                for h in range(2):
                    dve(f"p2_{h}")
                    four(first(h), G.W2[h], G.Pw[h], f"p3_{h}")
                for h in range(2):
                    dve(f"p3_{h}")
                    turned(second(h), G.Pw[h], f"q3_{h}")
                for h in range(2):
                    act(f"q3_{h}")
                    pool(f"en_{h}")
                    four(first(h), G.W1[h], G.E[h], f"f_{h}")
                for h in range(2):
                    four(second(h), G.E[h], G.W1[h], f"g1_{h}")
                for h in range(2):
                    dve(f"f_{h}")
                    act(f"g1_{h}")
                    four(first(h), G.W4[h], G.W3[h], f"f2_{h}")
                for h in range(2):
                    dve(f"v0_{h}")
                    four(second(h), G.W3[h], G.W4[h], f"g2_{h}")
                for h in range(2):
                    dve(f"f2_{h}")
                    four(first(h), G.W1[h], G.W5[h], f"v1_{h}")
                for h in range(2):
                    act(f"g2_{h}")
                    four(second(h), G.W2[h], G.W1[h], f"f4_{h}")
                for h in range(2):
                    act(f"f4_{h}")
                    dve(f"v1_{h}")
                    four(first(h), G.W3[h], G.W5[h], f"v2_{h}")
                for h in range(2):
                    dve(f"v2_{h}")
                    four(second(h), G.Pw[h], G.W5[h], f"tt_{h}")
                for h in range(2):
                    act(f"tt_{h}")
                    pool(f"kb_{h}")
                    four(first(h), G.kbg[h], G.W4[h], f"wt_{h}")
                for t in range(TT):
                    x = slice(t * P, t * P + P)
                    for h in range(2):
                        act(f"wt_{h}")
                        if t:
                            dve(f"s{t - 1}_{h}")
                        S, vn = G.W1[h][:, 0:P], first(h)[:, (t % 2) * P:(t % 2) * P + P]
                        mm = pe.matmul(vn, G.W4[h][:, x], G.vb[h][:, x], start=True, stop=t == 0)
                        if t:
                            mm = pe.matmul(vn, G.W2[h][:, x], S, start=False, stop=True)
                        mm.then_inc(*H.pe.done(f"vn{t}_{h}"))
                    for h in range(2):
                        S, new = G.W1[h][:, 0:P], G.W1[h][:, (1 + t % 2) * P:(2 + t % 2) * P]
                        if t:
                            pool(f"qd_{h}")
                            pe.matmul(second(h)[:, x], S, G.qdec[h][:, x], start=True, stop=False)
                        act(f"vn{t}_{h}")
                        pe.matmul(second(h)[:, x], new, G.attnT[h][:, x], start=t == 0, stop=True).then_inc(*H.pe.done(f"o{t}_{h}"))
                        if t < TT - 1:
                            pool(f"kd_{h}")
                            pe.matmul(first(h)[:, 2 * P:3 * P], G.kdec[h][:, x], new, start=True, stop=True).then_inc(*H.pe.done(f"ds{t}_{h}"))
                for h in range(2):
                    act(f"sq_{h}")
                    pe.matmul(first(h)[:], ones[:], G.W3[h][:], start=True, stop=True).then_inc(*H.pe.done(f"sum_{h}"))
            gdn_turns(pe, turn)
            down_pe(pe, G.b0 + GDN_P, G.t0 + GDN_P, 16, gdn_hi, gdn_lo, *G.end_dve.after("lo15"))

        def gdn_act(act):
            G, H, s = Gdn, GdnTurn, Gdn.prep_act
            project_act(act, G.b0, 1)
            act.wait_ge(tile_free, BANKS + G.t0 + 1)
            act.wait_ge(*G.prep_pool.after("gates"))
            r = slice(32, 48)
            act.activation(G.gates[0:16, :], G.raw[0:16, :], ACT.Sigmoid).then_inc(*s.done("beta"))
            act.activation(G.x[r, :], G.raw[r, :], ACT.Identity, bias=dt_b[r, :]).then_inc(*s.done("x"))
            act.activation(G.ax[r, :], G.raw[r, :], ACT.Abs, bias=dt_b[r, :]).then_inc(*s.done("ax"))
            act.wait_ge(*s.after("ax"))
            act.activation(G.ex[r, :], G.ax[r, :], ACT.Exp, scale=-1.0).then_inc(*s.done("ex"))
            act.wait_ge(*s.after("ex"))
            act.activation(G.ax[r, :], G.ex[r, :], ACT.Ln, bias=1.0).then_inc(*s.done("ln"))
            act.activation(neg_a[r, :], neg_a[r, :], ACT.Exp).then_inc(*s.done("ea"))
            act.wait_ge(*G.prep_dve.after("gt"))
            act.activation(G.eg, G.g, ACT.Exp).then_inc(*s.done("eg"))
            act.wait_ge(*G.prep_pe.after("last"))
            act.activation(G.egl, bank[7][:, 0:64], ACT.Exp).then_inc(*s.done("egl"))
            act.wait_ge(*G.prep_dve.after("diff"))
            act.activation(G.kd, G.diff, ACT.Exp).then_inc(*s.done("kd"))

            def turn(j, i, m):
                pe, dve, pool, own = ((lambda n, S=S: act.wait_ge(*S.after(n, j))) for S in (H.pe, H.dve, H.pool, H.act))

                def run(step, out, src, f, **kw):
                    act.activation(out, src, f, **kw).then_inc(*H.act.done(step))

                act.wait_ge(*H.dve.turns_before(j))
                for u in range(4):
                    split_hi(act, gdn_block(m, u) + AHEAD, i, 12)
                    act.wait_ge(block_done, SPLIT + gdn_block(m, u) + 1 + i * 12)
                    run(f"cw{u}", G.conv_to[u][:], gdn_bank(m, u)[:], ACT.Copy, scale=par[:, gdn_tap(3, u, j)])
                for u in range(4):
                    act.wait_ge(*gdn_taken(m, u, i))
                    run(f"cs{u}", G.conv_to[u][:], G.conv_to[u][:], ACT.Silu)
                for u, n in enumerate("qk"):
                    own(f"cs{u}")
                    run(f"sq_{n}", G.Pw[u][:], G.conv_to[u][:], ACT.Square)
                split_hi(act, gdn_block(m, 4) + AHEAD, i, 12)
                for u, n in enumerate("qk"):
                    pe(f"sum_{n}")
                    run(f"sd_{n}", G.W1[u][:], (first(0), second(1))[u][:], ACT.Sqrt, bias=eps_c)
                split_hi(act, gdn_block(m, 5) + AHEAD, i, 12)
                for h in range(2):
                    act.wait_ge(*gdn_taken(m, 4 + h, i))
                    run(f"zs{h}", G.zs[h][:], G.zs[h][:], ACT.Silu)
                pe("kt")
                run("kc", G.k_tok[:], second(0)[:], ACT.Copy)
                for h in range(2):
                    pe(f"gb_{h}")
                    run(f"eg_{h}", G.W5[h][:], second(h)[:], ACT.Exp)
                for h in range(2):
                    dve(f"db_{h}")
                    run(f"dec_{h}", G.W1[h][:], G.W1[h][:], ACT.Exp, scale=-1.0)

                def copies(step, dst, src):
                    for h in range(2):
                        pe(f"{step}_{h}")
                        run(f"{step}_{h}", dst[h][:], src(h)[:], ACT.Copy)
                copies("at", G.attnT, second)
                copies("y1", G.W1, first)
                for h in range(2):
                    pool(f"en_{h}")
                copies("y2", G.W3, first)
                pool("p0_0")
                pool("p0_1")
                copies("y4", G.W4, first)
                copies("y8", G.W2, second)
                copies("q3", G.W1, second)
                copies("g1", G.W4, second)
                copies("g2", G.W2, second)
                copies("f4", G.W3, second)
                copies("tt", G.W4, second)
                for h in range(2):
                    pe(f"wt_{h}")
                    run(f"wt_{h}", G.W2[h][:], first(h)[:], ACT.Copy, scale=-1.0)
                for t in range(TT):
                    for h in range(2):
                        pe(f"vn{t}_{h}")
                        if t >= 2:
                            pe(f"o{t - 2}_{h}")
                            pe(f"ds{t - 2}_{h}")
                        run(f"vn{t}_{h}", G.W1[h][:, (1 + t % 2) * P:(2 + t % 2) * P], first(h)[:, (t % 2) * P:(t % 2) * P + P], ACT.Copy)
                for h in range(2):
                    pe(f"o{TT - 1}_{h}")
                    run(f"sq_{h}", G.W3[h][:], second(h)[:], ACT.Square)
                for h in range(2):
                    pe(f"sum_{h}")
                    run(f"sd_{h}", G.W5[h][:], first(h)[:], ACT.Sqrt, bias=eps_c, scale=1.0 / P)
            gdn_turns(act, turn)
            act.wait_ge(*H.dve.turns_before(GDN_QK))
            for k in range(16):
                x = slice(k * T, k * T + T)
                act.activation(gdn_hi[:, x], G.o[:, x], ACT.Copy).then_inc(*G.end_act.done(f"hi{k}"))
            down_act(act, G.b0 + GDN_P, 16)

        def gdn_tap(tap, u, j):
            row = R_CONV + 32 * tap
            return bass.ds((j + row) if u == 0 else (j + (row + GDN_QK)) if u == 1 else (j * 2 + (row + 2 * GDN_QK + u - 2)), 1)

        def gdn_dve(dve):
            G, H, s = Gdn, GdnTurn, Gdn.prep_dve
            project_dve(dve, G.b0, G.t0, 1, lambda k, src: dve.tensor_copy(G.raw[:], src))
            r = slice(32, 48)
            dve.wait_ge(*G.prep_act.after("ea"))
            dve.scalar_tensor_tensor(G.x[r, :], G.x[r, :], 0.0, G.ax[r, :], ALU.max, ALU.add).then_inc(*s.done("sp"))
            dve.wait_ge(*s.after("sp"))
            dve.tensor_scalar(G.x[r, :], G.x[r, :], neg_a[r, :], -1.0, ALU.mult, ALU.mult).then_inc(*s.done("g"))
            dve.wait_ge(*s.after("g"))
            dve.wait_ge(*G.prep_pool.after("reset"))
            dve.tensor_tensor_scan(G.gates[r, :], G.reset[r, :], G.x[r, :], 0.0, ALU.mult, ALU.add).then_inc(*s.done("cum"))
            dve.tensor_copy(G.last_row[:, 0:P], ident[:, P - 1:P].to_broadcast([P, P])).then_inc(*s.done("last_row"))
            dve.wait_ge(*G.prep_pe.after("turn"))
            for n, dst, c in (("beta", G.beta, 0), ("gt", G.g, 32)):
                dve.tensor_copy(dst.rearrange("p (h t) -> p t h", t=TT),
                                bank[6][:, 0:48 * TT].rearrange("p (t x) -> p t x", x=48)[:, :, c:c + 16]).then_inc(*s.done(n))
            dve.wait_ge(*s.after("gt"))
            dve.wait_ge(*G.prep_act.after("egl"))
            dve.tensor_tensor(G.diff, bank[7][:, 0:64], G.g, ALU.subtract).then_inc(*s.done("diff"))
            dve.tensor_tensor(G.bexp, G.beta, G.eg, ALU.mult).then_inc(*s.done("bexp"))
            dve.tensor_scalar(G.negb, G.beta, -1.0, None, ALU.mult).then_inc(*s.done("negb"))
            dve.wait_ge(*s.after("negb"))
            dve.wait_ge(*G.prep_act.after("kd"))
            dve.sem_inc(H.dve.sem, 1)

            def turn(j, i, m):
                pe, act, pool, own = ((lambda n, S=S: dve.wait_ge(*S.after(n, j))) for S in (H.pe, H.act, H.pool, H.dve))

                def done(step):
                    return H.dve.done(step)

                def tt(step, out, x, y, op):
                    dve.tensor_tensor(out, x, y, op).then_inc(*done(step))

                def take(u):
                    split_lo(dve, gdn_block(m, u) + AHEAD, i, 12)
                    dve.wait_ge(block_done, SPLIT + gdn_block(m, u) + 1 + i * 12)
                    src = gdn_bank(m, u)
                    if u >= 4:
                        dve.tensor_copy(G.zs[u - 4][:], src[:]).then_inc(tile_free, 1)
                        return
                    act(f"cw{u}")
                    c = G.conv_to[u]
                    for d, n in ((1, "a"), (2, "b"), (3, None)):
                        if d > 1:
                            own(f"c{'ab'[d - 2]}{u}")
                        ins = dve.scalar_tensor_tensor(c[:, d:T], src[:, 0:T - d], par[:, gdn_tap(3 - d, u, j)], c[:, d:T], ALU.mult, ALU.add)
                        if n:
                            ins.then_inc(*done(f"c{n}{u}"))
                        else:
                            ins.then_inc(tile_free, 1)
                dve.wait_ge(*H.dve.turns_before(j))
                for u in range(5):
                    take(u)
                for u, n in enumerate("qk"):
                    act(f"sd_{n}")
                    dve.reciprocal(G.W2[u][:], G.W1[u][:]).then_inc(*done(f"rc_{n}"))
                    own(f"rc_{n}")
                    dve.scalar_tensor_tensor(G.conv_to[u][:], G.conv_to[u][:], (GDN_DH ** -0.5, 1.0)[u], G.W2[u][:],
                                             ALU.mult, ALU.mult).then_inc(*done(f"n_{n}"))
                for h in range(2):
                    dve.tensor_scalar(G.gsel[h][32:48, :], G.gates[32:48, :], ident[32:48, bass.ds(j * 2 + (32 + h), 1)], None,
                                      ALU.mult).then_inc(*done(f"gs_{h}"))
                take(5)
                for h in range(2):
                    pe(f"vt_{h}")
                    tt(f"vb_{h}", t3(G.vb[h]), t3(first(1 - h)), by_col(G.beta, j * 2 + h), ALU.mult)
                for h in range(2):
                    act(f"eg_{h}")
                    own("n_k")
                    tt(f"da_{h}", t3(G.W1[h]), t3(second(h)), by_row(above_big), ALU.add)
                for h in range(2):
                    own(f"da_{h}")
                    tt(f"db_{h}", t3(G.W1[h]), t3(G.W1[h]), by_col(G.g, j * 2 + h), ALU.subtract)
                for h in range(2):
                    act(f"dec_{h}")
                    pe("qk")
                    tt(f"at_{h}", G.W2[h][:], first(1)[:], G.W1[h][:], ALU.mult)
                for h in range(2):
                    pe("kk")
                    tt(f"kk_{h}", G.W3[h][:], first(0)[:], G.W1[h][:], ALU.mult)
                for h in range(2):
                    own(f"kk_{h}")
                    tt(f"nb_{h}", t3(G.W3[h]), t3(G.W3[h]), by_col(G.negb, j * 2 + h), ALU.mult)
                for h in range(2):
                    own(f"nb_{h}")
                    tt(f"m_{h}", t3(G.W4[h]), t3(G.W3[h]), by_row(in_block), ALU.mult)
                for h in range(2):
                    pe(f"x2_{h}")
                    pe(f"at_{h}")
                    dve.tensor_copy(G.W2[h][:], second(h)[:]).then_inc(*done(f"x2_{h}"))
                for h in range(2):
                    pe(f"x4_{h}")
                    pe(f"y2_{h}")
                    dve.tensor_copy(G.W1[h][:], second(h)[:]).then_inc(*done(f"x4_{h}"))
                for n, src in (("p1", first), ("p2", second), ("p3", first)):
                    for h in range(2):
                        pe(f"{n}_{h}")
                        if n != "p1":
                            own(f"p{int(n[1]) - 1}_{h}")
                        tt(f"{n}_{h}", G.Pw[h][:], G.Pw[h][:], src(h)[:], ALU.add)
                for h in range(2):
                    pe(f"f_{h}")
                    dve.tensor_copy(G.W3[h][:], first(h)[:]).then_inc(*done(f"f_{h}"))
                for h in range(2):
                    act(f"g1_{h}")
                    tt(f"v0_{h}", t3(G.W5[h]), t3(second(h)), by_row(ident), ALU.add)
                for h in range(2):
                    pe(f"f2_{h}")
                    dve.tensor_copy(G.W1[h][:], first(h)[:]).then_inc(*done(f"f2_{h}"))
                for n, before in (("v1", "v0"), ("v2", "v1")):
                    for h in range(2):
                        pe(f"{n}_{h}")
                        own(f"{before}_{h}")
                        tt(f"{n}_{h}", G.W5[h][:], G.W5[h][:], first(h)[:], ALU.add)
                for t in range(TT - 1):
                    for h in range(2):
                        pe(f"ds{t}_{h}")
                        S, add = G.W1[h][:, 0:P], first(h)[:, 2 * P:3 * P]
                        if t:
                            own(f"s{t - 1}_{h}")
                            dve.scalar_tensor_tensor(S, S, G.egl[:, bass.ds((j * 2 + h) * TT + t, 1)], add, ALU.mult, ALU.add).then_inc(*done(f"s{t}_{h}"))
                        else:
                            dve.tensor_copy(S, add).then_inc(*done(f"s{t}_{h}"))
                for h in range(2):
                    act(f"sd_{h}")
                    dve.reciprocal(G.W3[h][:], G.W5[h][:]).then_inc(*done(f"rc_{h}"))
                    own(f"rc_{h}")
                    dve.scalar_tensor_tensor(G.W2[h][:], second(h)[:], par[:, R_GDNN:R_GDNN + 1], G.W3[h][:], ALU.mult, ALU.mult).then_inc(*done(f"on_{h}"))
                    own(f"on_{h}")
                    tt(f"o_{h}", G.o[:, col(j * 2 + h)], G.W2[h][:], G.zs[h][:], ALU.mult)
            gdn_turns(dve, turn)
            for k in range(16):
                x = slice(k * T, k * T + T)
                dve.wait_ge(*G.end_act.after(f"hi{k}"))
                dve.tensor_tensor(gdn_lo[:, x], G.o[:, x], gdn_hi[:, x].bitcast(F32), ALU.subtract).then_inc(*G.end_dve.done(f"lo{k}"))
            down_dve(dve, G.b0 + GDN_P, G.t0 + GDN_P, 16, mod[:, 2 * KT:3 * KT])

        def gdn_pool(pool):
            G, H, s = Gdn, GdnTurn, Gdn.prep_pool
            pool.wait_ge(x_ready, KT * 7)
            pool.memset(G.gates[:], 0.0).then_inc(*s.done("gates"))
            pool.memset(G.reset[:], 1.0).then_inc(*s.done("ones"))
            pool.wait_ge(*s.after("ones"))
            pool.memset(t3(G.reset)[:, :, 0:1], 0.0).then_inc(*s.done("reset"))

            def turn(j, i, m):
                act, dve = ((lambda n, S=S: pool.wait_ge(*S.after(n, j))) for S in (H.act, H.dve))

                def tt(step, out, x, y, op):
                    pool.tensor_tensor(out, x, y, op).then_inc(*H.pool.done(step))
                act("kc")
                for h in range(2):
                    tt(f"kd_{h}", t3(G.kdec[h]), t3(G.k_tok), by_col(G.kd, j * 2 + h), ALU.mult)
                for h in range(2):
                    tt(f"kb_{h}", t3(G.kbg[h]), t3(G.k_tok), by_col(G.bexp, j * 2 + h), ALU.mult)
                for h in range(2):
                    act(f"eg_{h}")
                    tt(f"qd_{h}", G.qdec[h][:], G.qT[:], G.W5[h][:], ALU.mult)
                for h in range(2):
                    dve(f"nb_{h}")
                    tt(f"en_{h}", t3(G.E[h]), t3(G.W3[h]), by_row(off_block), ALU.mult)
                for h in range(2):
                    dve(f"m_{h}")
                    tt(f"p0_{h}", t3(G.Pw[h]), t3(G.W4[h]), by_row(ident), ALU.add)
            gdn_turns(pool, turn)

        class Fox:
            b0, t0 = BASE["fox"]
            f, x, ax, ex, all_ones, cum = (tile(f"fox_{n}", 32 + k) for k, n in enumerate(("f", "x", "ax", "ex", "all_ones", "cum")))
            qkvz = [tile(f"fox_{n}", 8 + k) for k, n in enumerate(("q", "k", "v", "z"))]
            sq, sd, rs = ([tile(f"fox_{n}{k}", t + k) for k in range(2)] for n, t in (("sq", 12), ("sd", 14), ("rs", 38)))
            v_tok, csel = tile("fox_v_tok", 16), [tile(f"fox_csel{h}", 17 + h) for h in range(2)]
            p, pT = [tile(f"fox_p{k}", 19 + k) for k in range(2)], [tile(f"fox_pT{k}", 30 + k) for k in range(2)]
            gated = tile("fox_gated", 21)
            act = Steps(sem("fox_act"), ["x", "ax", "ex", "ln"])
            dve = Steps(sem("fox_dve"), ["log_f", "cum"])
            pool = Steps(sem("fox_pool"), ["ones"])

        class FoxTurn:
            n = att_names(2 * TT)
            pe = Steps(sem("fox_turn_pe"), ["sum_q", "sum_k", "vt"] + n["pe"])
            act = Steps(sem("fox_turn_act"), ["sq_q", "sq_k", "sd_q", "sd_k", "zs", "vt"] + n["act"] + ["hi"])
            dve = Steps(sem("fox_turn_dve"), ["cs_0", "cs_1", "rc_q", "n_q", "rc_k", "n_k"] + n["dve"] + ["gated", "lo"], 1)
            pool = Steps(sem("fox_turn_pool"), n["pool"])

        FOX_W = FOX_HEADS * FOX_DH

        def fox_turns(eng, body):
            with eng.Fori(0, FOX_HEADS // 4) as i:
                for m in range(2):
                    body(i * 2 + m, i, m)

        def fox_block(m, u):
            return Fox.b0 + 1 + 4 * m + u

        def fox_taken(m, u, i):
            return tile_free, BANKS + Fox.t0 + 1 + 4 * m + u + 1 + i * 8

        def fox_keys(u):
            return (u % TT + 1) * P

        def fox_sp(sp):
            w, b0 = a["b_w_in_2"][0], Fox.b0
            load(sp, b0, weight_cols(w, slice(4 * FOX_W, 4 * FOX_W + FOX_HEADS)), cols=(0, FOX_HEADS))
            with sp.Fori(0, FOX_HEADS // 4) as i:
                for m in range(2):
                    for u in range(4):
                        load(sp, fox_block(m, u), weight_cols(w, bass.ds(i * (2 * P) + (u * FOX_W + m * P), P)), i, 8)
            down_sp(sp, a["b_w_out_2"][0], b0 + FOX_P, KT)

        def fox_pe(pe, run):
            F, H = Fox, FoxTurn
            project_pe(pe, run, F.b0, F.t0, 1)
            pe.wait_ge(*F.dve.after("cum"))

            def turn(j, i, m):
                act, dve = ((lambda n, S=S: pe.wait_ge(*S.after(n, j))) for S in (H.act, H.dve))

                def project(u):
                    pe.wait_ge(tile_free, F.t0 + 1 + 4 * m + u + 1 + i * 8)
                    products(pe, fox_block(m, u), bank[(F.t0 + 1 + 4 * m + u) % BANKS][:], x_of(x_hi), x_of(x_lo), range(KT),
                             True, True, i, 8)
                for u in range(3):
                    project(u)
                for k, n in enumerate("qk"):
                    act(f"sq_{n}")
                    pe.matmul(bank[4 + k][:], ones64[:], F.sq[k][:], start=True, stop=True).then_inc(*H.pe.done(f"sum_{n}"))
                project(3)
                for t in range(TT):
                    pe.wait_ge(*fox_taken(m, 2, i))
                    mm = pe.transpose(bank[6][:, t * P:t * P + P], F.qkvz[2][:, t * P:t * P + P], ident[:])
                mm.then_inc(*H.pe.done("vt"))
                pe.wait_ge(*fox_taken(m, 3, i))
                dve("n_k")
                act("vt")

                def scores(u, out):
                    h, t = divmod(u, TT)
                    r = slice(64 * h, 64 * h + 64)
                    pe.matmul(out, F.qkvz[0][r, t * P:t * P + P], F.qkvz[1][r, 0:fox_keys(u)], start=True, stop=False)
                    pe.matmul(out, ones[0:16, :], F.csel[h][0:16, 0:fox_keys(u)], start=False, stop=False)
                    return pe.matmul(out[:, t * P:t * P + P], ident[:], causal[:], start=False, stop=True)

                def values(u):
                    h, t = divmod(u, TT)
                    return (bank[7][64 * h:64 * h + 64, t * P:t * P + P],
                            lambda k: F.v_tok[:, k * P + 64 * h:k * P + 64 * h + 64])
                att_pe(pe, H, j, 2 * TT, fox_keys, scores, values, F.p, F.pT)
            fox_turns(pe, turn)
            down_pe(pe, F.b0 + FOX_P, F.t0 + FOX_P, KT, h_hi, h_lo, *H.dve.turns_before(FOX_HEADS // 2))

        def fox_act(act):
            F, H, s = Fox, FoxTurn, Fox.act
            project_act(act, F.b0, 1)
            act.wait_ge(tile_free, BANKS + F.t0 + 1)
            r = slice(0, FOX_HEADS)
            act.activation(F.x[r, :], F.f[r, :], ACT.Identity, bias=nfox_b[r, :]).then_inc(*s.done("x"))
            act.activation(F.ax[r, :], F.f[r, :], ACT.Abs, bias=nfox_b[r, :]).then_inc(*s.done("ax"))
            act.wait_ge(*s.after("ax"))
            act.activation(F.ex[r, :], F.ax[r, :], ACT.Exp, scale=-1.0).then_inc(*s.done("ex"))
            act.wait_ge(*s.after("ex"))
            act.activation(F.ax[r, :], F.ex[r, :], ACT.Ln, bias=1.0).then_inc(*s.done("ln"))

            def turn(j, i, m):
                pe, own = ((lambda n, S=S: act.wait_ge(*S.after(n, j))) for S in (H.pe, H.act))
                act.wait_ge(*H.dve.turns_before(j))
                for u in range(3):
                    split_hi(act, fox_block(m, u) + AHEAD, i, 8)
                for k, n in enumerate("qk"):
                    act.wait_ge(*fox_taken(m, k, i))
                    act.activation(F.sq[k][:], F.qkvz[k][:], ACT.Square).then_inc(*H.act.done(f"sq_{n}"))
                split_hi(act, fox_block(m, 3) + AHEAD, i, 8)
                for k, n in enumerate("qk"):
                    pe(f"sum_{n}")
                    act.activation(F.sd[k][:], bank[4 + k][:], ACT.Sqrt, bias=eps_c, scale=1.0 / FOX_DH).then_inc(*H.act.done(f"sd_{n}"))
                act.wait_ge(*fox_taken(m, 3, i))
                act.activation(F.qkvz[3][:], F.qkvz[3][:], ACT.Silu).then_inc(*H.act.done("zs"))
                pe("vt")
                act.activation(F.v_tok[:], bank[6][:], ACT.Copy).then_inc(*H.act.done("vt"))
                att_act(act, H, j, 2 * TT, fox_keys, FOX_DH ** -0.5, F.p, F.pT)
                act.wait_ge(*H.dve.after("gated", j))
                act.activation(h_hi[:, col(j)], F.gated[:], ACT.Copy).then_inc(*H.act.done("hi"))
            fox_turns(act, turn)
            down_act(act, F.b0 + FOX_P, KT)

        def fox_dve(dve):
            F, H, s = Fox, FoxTurn, Fox.dve
            project_dve(dve, F.b0, F.t0, 1, lambda k, src: dve.tensor_copy(F.f[:], src))
            r = slice(0, FOX_HEADS)
            dve.wait_ge(*F.act.after("ln"))
            dve.scalar_tensor_tensor(F.x[r, :], F.x[r, :], 0.0, F.ax[r, :], ALU.min, ALU.subtract).then_inc(*s.done("log_f"))
            dve.wait_ge(*s.after("log_f"))
            dve.wait_ge(*F.pool.after("ones"))
            dve.tensor_tensor_scan(F.cum[r, :], F.all_ones[r, :], F.x[r, :], 0.0, ALU.mult, ALU.add).then_inc(*s.done("cum"))
            dve.wait_ge(*s.after("cum"))
            dve.sem_inc(H.dve.sem, 1)

            def turn(j, i, m):
                pe, act, own = ((lambda n, S=S: dve.wait_ge(*S.after(n, j))) for S in (H.pe, H.act, H.dve))
                dve.wait_ge(*H.dve.turns_before(j))
                for h in range(2):
                    dve.tensor_scalar(F.csel[h][r, :], F.cum[r, :], ident[r, bass.ds(j * 2 + h, 1)], -(FOX_DH ** 0.5),
                                      ALU.mult, ALU.mult).then_inc(*H.dve.done(f"cs_{h}"))
                for u in range(4):
                    split_lo(dve, fox_block(m, u) + AHEAD, i, 8)
                    dve.wait_ge(block_done, SPLIT + fox_block(m, u) + 1 + i * 8)
                    dve.tensor_copy(F.qkvz[u][:], bank[(F.t0 + 1 + 4 * m + u) % BANKS][:]).then_inc(tile_free, 1)
                for k, (n, row) in enumerate((("q", R_QN), ("k", R_KN))):
                    act(f"sd_{n}")
                    dve.reciprocal(F.rs[k][:], F.sd[k][:]).then_inc(*H.dve.done(f"rc_{n}"))
                    own(f"rc_{n}")
                    dve.scalar_tensor_tensor(F.qkvz[k][:], F.qkvz[k][:], par[:, row:row + 1], F.rs[k][:],
                                             ALU.mult, ALU.mult).then_inc(*H.dve.done(f"n_{n}"))
                att_dve(dve, H, j, 2 * TT, fox_keys, FOX_DH ** -0.5)
                pe(f"pv{2 * TT - 1}")
                act("zs")
                dve.tensor_tensor(F.gated[:], bank[7][:], F.qkvz[3][:], ALU.mult).then_inc(*H.dve.done("gated"))
                act("hi")
                dve.tensor_tensor(h_lo[:, col(j)], F.gated[:], h_hi[:, col(j)].bitcast(F32), ALU.subtract).then_inc(*H.dve.done("lo"))
            fox_turns(dve, turn)
            down_dve(dve, F.b0 + FOX_P, F.t0 + FOX_P, KT, mod[:, 5 * KT:6 * KT])

        def fox_pool(pool):
            F, H = Fox, FoxTurn
            pool.memset(F.all_ones[:], 1.0).then_inc(*F.pool.done("ones"))

            def turn(j, i, m):
                att_pool(pool, H, j, 2 * TT, fox_keys, F.p)
            fox_turns(pool, turn)

        ROWS = [("ffn1_norm", R_FFN1), ("mix_norm", R_MIX), ("ffn2_norm", R_FFN2), ("final_norm", R_FINAL),
                ("norm_w_2", R_NORM2), ("final_norm_w_2", R_FINAL2), ("gla_out_norm", R_GLAN), ("pool_scale", R_POOLS),
                ("gla_gate_b", R_GATEB), ("a_norm_w_2", R_GDNN), ("c_2", R_C)]
        PARAM_LOADS = len(ROWS) + 2 * 4 + 2 + 2 + 3

        def start_sp(sp):
            for t in range(TT):
                sp.dma_start(x_in[:, t * D:t * D + D], a["x"][0, t * P:t * P + P, :]).then_inc(x_loaded, 16)

        def start_act(act):
            def rows(src):
                src = src.flatten()
                return src.rearrange("(r c) -> r c", c=P)
            act.wait_ge(rows_zeroed, 1)
            for name, r in ROWS:
                src = rows(a[name])
                act.dma_start(stage_rows[0][r:r + src.shape[0], 0:P], src).then_inc(params_loaded, 16)
            for name, r in (("b_qn_w_2", R_QN), ("b_kn_w_2", R_KN)):
                for half in range(2):
                    act.dma_start(stage_rows[0][r:r + 1, half * 64:half * 64 + 64], a[name]).then_inc(params_loaded, 16)
            for half in range(2):
                act.dma_start(stage_rows[0][R_INV128:R_INV128 + 1, half * 64:half * 64 + 64], a["inv"][:, 0:64]).then_inc(params_loaded, 16)
            act.dma_start(stage_rows[0][R_INV64:R_INV64 + 1, 0:64], a["inv"][:, 64:128]).then_inc(params_loaded, 16)
            act.dma_start(stage_rows[0][R_INV64:R_INV64 + 1, 64:128], a["inv"][:, 64:128]).then_inc(params_loaded, 16)
            act.dma_start(stage_rows[1][:, 0:P], rows(a["a_conv_w_2"])).then_inc(params_loaded, 16)
            act.dma_start(stage_rows[2][0:2 * 3 * KT, 0:P], rows(a["ada_b_2"])).then_inc(params_loaded, 16)
            act.dma_start(gate_w[:], a["gla_gate_w"][0]).then_inc(params_loaded, 16)
            act.dma_start(pool_w[:, :].rearrange("c (g d) -> c g d", g=POOL_GROUPS),
                          a["pool_w"][0].rearrange("g c d -> c g d")).then_inc(params_loaded, 16)
            act.dma_start(nfox_b[0:16, :], a["b_f_bias_2"].rearrange("o h -> h o")).then_inc(params_loaded, 16)
            act.dma_start(dt_b[32:48, :], a["a_dt_bias_2"].rearrange("o h -> h o")).then_inc(params_loaded, 16)
            act.dma_start(neg_a[32:48, :], a["a_A_log_2"].rearrange("o h -> h o")).then_inc(params_loaded, 16)
            for b in range(AHEAD):
                split_hi(act, b)
            act.wait_ge(rows_taken, 1)
            act.wait_ge(eps_made, 1)
            c = par[:, R_C:R_C + KT].rearrange("p (k r) -> p k r", r=1).to_broadcast([P, KT, 2])
            act.activation(cond2[:, :].rearrange("p (k r) -> p k r", r=2), c, ACT.Silu).then_inc(cond_made, 1)

        consts_total = []

        def start_pool(pool):
            made = [0]

            def step(ins):
                made[0] += 1
                ins.then_inc(consts_made, 1)
                pool.wait_ge(consts_made, made[0])

            def keep(t, pattern, base, cm, op, fill):
                step(pool.affine_select(out=t, in_=t, pattern=pattern, compare_op=op, fill=fill, base=base, channel_multiplier=cm))
            for k in range(2):
                step(pool.memset(stage_rows[2 * k][:, 0:P], 0.0))
            pool.sem_inc(rows_zeroed, 1)
            for t, v in ((ident, 0.0), (ones, 1.0), (ones64, 0.0), (swap128, 0.0), (swap64, 0.0), (above_big, 0.0),
                         (causal, 0.0), (in_block, 1.0), (off_block, 1.0)):
                step(pool.memset(t[:], v))
            line = [[-1, P]]
            keep(ident[:], line, 0, 1, ALU.not_equal, 1.0)
            pool.sem_inc(ident_made, 1)
            for r in (slice(0, 64), slice(64, P)):
                step(pool.memset(ones64[r, r], 1.0))
            keep(swap128[:], line, -64, 1, ALU.not_equal, -1.0)
            keep(swap128[:], line, 64, 1, ALU.not_equal, 1.0)
            for b in range(4):
                keep(swap64[:, 32 * b:32 * b + 32], [[-1, 32]], (32 if b % 2 else -32) - 32 * b, 1, ALU.not_equal, 1.0 if b % 2 else -1.0)
            keep(above_big[:], line, 0, 1, ALU.is_ge, -NEG)
            keep(causal[:], line, 0, 1, ALU.is_ge, NEG)
            for t in (in_block, off_block):
                keep(t[:], line, -1, 1, ALU.is_ge, 0.0)
            blocks = in_block[:, :].rearrange("p (b j) -> p b j", j=INV_BLOCK)
            keep(blocks, [[-INV_BLOCK, P // INV_BLOCK], [0, INV_BLOCK]], 0, 1, ALU.is_ge, 0.0)
            keep(blocks, [[INV_BLOCK, P // INV_BLOCK], [0, INV_BLOCK]], INV_BLOCK - 1, -1, ALU.is_ge, 0.0)
            step(pool.tensor_tensor(off_block[:], off_block[:], in_block[:], ALU.subtract))
            step(pool.memset(chunk_T[:], 1.0))
            keep(chunk_T[:], [[1, P]], 0, -1, ALU.is_ge, 0.0)
            step(pool.memset(chunk_T[0:64, 64:P], 0.0))
            for g in range(POOL_GROUPS):
                w = 2 ** (g + 1)
                step(pool.memset(inv_count[:, 16 * g:16 * g + 16], 1.0 / w))
                for t in range(w - 1):
                    step(pool.memset(inv_count[:, 16 * g + t:16 * g + t + 1], 1.0 / (t + 1)))
            consts_total.append(made[0])

        def start_pe(pe):
            pe.sem_inc(block_done, SPLIT)
            pe.wait_ge(ident_made, 1)
            pe.wait_ge(x_loaded, 16 * TT)
            for k in range(KT):
                if k >= 2:
                    pe.wait_ge(x_taken, k - 1)
                for t in range(TT):
                    mm = pe.transpose(bank[5 + k % 2][:, t * P:t * P + P], x_in[:, t * D + k * P:t * D + k * P + P], ident[:])
                mm.then_inc(x_turned, 1)
            pe.wait_ge(params_loaded, 16 * PARAM_LOADS)
            for k in range(3):
                mm = pe.transpose(bank[7][:, k * P:k * P + P], stage_rows[k][:, 0:P], ident[:])
            mm.then_inc(rows_turned, 1)
            pe.wait_ge(consts_made, consts_total[0])

        def start_dve(dve):
            dve.sem_inc(w_lo_done, RAW)
            dve.sem_inc(tile_free, BANKS)
            dve.memset(eps_c, EPS)
            dve.memset(half_pi, TWO_PI / 4).then_inc(eps_made, 1)
            for k in range(KT):
                dve.wait_ge(x_turned, k + 1)
                dve.tensor_copy(hres[:, k * T:k * T + T], bank[5 + k % 2][:]).then_inc(x_taken, 1)
            for b in range(AHEAD):
                split_lo(dve, b)
            dve.wait_ge(rows_turned, 1)
            dve.tensor_copy(par[:], bank[7][:, 0:3 * P]).then_inc(rows_taken, 1)
            dve.wait_ge(rows_taken, 1)
            dve.wait_ge(cond_made, 1)
            dve.wait_ge(consts_made, consts_total[0])
            dve.tensor_copy(cond_hi[:], cond2[:]).then_inc(cond_split, 1)
            dve.wait_ge(cond_split, 1)
            dve.tensor_tensor(cond_lo[:], cond2[:], cond_hi[:].bitcast(F32), ALU.subtract).then_inc(cond_split, 1)

        y_T, y = tile("y_T", 0, KT), tile("y", 8, KT)

        def end_sp(sp):
            for b in range(BLOCKS, BLOCKS + AHEAD):
                load(sp, b, weight_cols(a["b_w_out_2"][0], slice(0, P)))
            for t in range(TT):
                sp.wait_ge(out_taken, 2 * t + 2)
                sp.dma_start(out[0, t * P:t * P + P, :], y[:, t * D:t * D + D]).then_inc(out_stored, 16)
            sp.wait_ge(out_stored, 16 * TT)

        def end_dve(dve, r, gain):
            rstd_dve(dve, r)
            for k in range(KT):
                x = slice(k * T, k * T + T)
                dve.scalar_tensor_tensor(y_T[:, x], hres[:, x], gain[:, k:k + 1], rstd[:], ALU.mult, ALU.mult).then_inc(out_normed, 1)
            for n in range(2 * TT):
                dve.wait_ge(out_turned, n + 1)
                dve.tensor_copy(y[:, n * T:n * T + T], bank[4 + n % 2][:]).then_inc(out_taken, 1)

        def end_pe(pe):
            pe.wait_ge(out_normed, KT)
            for n in range(2 * TT):
                if n >= 2:
                    pe.wait_ge(out_taken, n - 1)
                for k in range(4):
                    mm = pe.transpose(bank[4 + n % 2][:, k * P:k * P + P], y_T[:, ((n % 2) * 4 + k) * T + (n // 2) * P:((n % 2) * 4 + k) * T + (n // 2 + 1) * P], ident[:])
                mm.then_inc(out_turned, 1)

        def resid(name):
            b0, t0 = BASE[name]
            nt = dict((n, t) for n, _, t in STAGES)[name]
            return BANKS + t0 + nt - KT + 1

        def gain(r):
            return par[:, r:r + KT]

        @block.sync
        def _(sp):
            start_sp(sp)
            ffn_sp(sp, 0, a["ffn1_wi"][0], a["ffn1_wo"][0])
            gla_sp(sp)
            ffn_sp(sp, 1, a["ffn2_wi"][0], a["ffn2_wo"][0])
            ffn_sp(sp, 2, a["ffn1_wi"][1], a["ffn1_wo"][1])
            dsa_sp(sp)
            ffn_sp(sp, 3, a["ffn2_wi"][1], a["ffn2_wo"][1])
            ada_sp(sp)
            gdn_sp(sp)
            fox_sp(sp)
            end_sp(sp)

        @block.gpsimd
        def _(pool):
            start_pool(pool)
            squares_pool(pool, 0, x_taken, 1)
            squares_pool(pool, 1, tile_free, resid("ffn0"))
            gla_pool(pool)
            squares_pool(pool, 2, tile_free, resid("gla"))
            squares_pool(pool, 3, tile_free, resid("ffn1"))
            squares_pool(pool, 4, tile_free, resid("ffn2"))
            dsa_pool(pool)
            squares_pool(pool, 5, tile_free, resid("dsa"))
            squares_pool(pool, 6, tile_free, resid("ffn3"))
            squares_pool(pool, 7, normed, 1)
            gdn_pool(pool)
            squares_pool(pool, 8, tile_free, resid("gdn"))
            fox_pool(pool)
            squares_pool(pool, 9, tile_free, resid("fox"))

        @block.scalar
        def _(act):
            start_act(act)
            norm_act(act, 0, 0)
            ffn_act(act, 0)
            norm_act(act, 1, 1)
            gla_act(act)
            norm_act(act, 2, 2)
            ffn_act(act, 1)
            norm_act(act, 3, 3)
            ffn_act(act, 2)
            norm_act(act, 4, 4)
            dsa_act(act)
            norm_act(act, 5, 5)
            ffn_act(act, 3)
            std_act(act, 6)
            ada_act(act)
            norm_act(act, 7, 6, mod[:, 0:KT])
            gdn_act(act)
            norm_act(act, 8, 7, mod[:, 3 * KT:4 * KT])
            fox_act(act)
            std_act(act, 9)

        @block.vector
        def _(dve):
            start_dve(dve)
            norm_dve(dve, 0, 0, gain(R_FFN1))
            ffn_dve(dve, 0)
            norm_dve(dve, 1, 1, gain(R_MIX))
            gla_dve(dve)
            norm_dve(dve, 2, 2, gain(R_FFN2))
            ffn_dve(dve, 1)
            norm_dve(dve, 3, 3, gain(R_FFN1 + KT))
            ffn_dve(dve, 2)
            norm_dve(dve, 4, 4, gain(R_MIX + KT))
            dsa_dve(dve)
            norm_dve(dve, 5, 5, gain(R_FFN2 + KT))
            ffn_dve(dve, 3)
            rstd_dve(dve, 6)
            ada_dve(dve)
            norm_dve(dve, 7, 6, gain2[:, 0:KT], mod[:, 0:KT])
            gdn_dve(dve)
            norm_dve(dve, 8, 7, gain2[:, KT:2 * KT], mod[:, 3 * KT:4 * KT])
            fox_dve(dve)
            end_dve(dve, 9, gain(R_FINAL2))

        @block.tensor
        def _(pe):
            start_pe(pe)
            mean_pe(pe, 0)
            ffn_pe(pe, 0, 0, 0)
            mean_pe(pe, 1)
            gla_pe(pe, 1)
            mean_pe(pe, 2)
            ffn_pe(pe, 1, 2, FT)
            mean_pe(pe, 3)
            ffn_pe(pe, 2, 3, 2 * FT)
            mean_pe(pe, 4)
            dsa_pe(pe, 4)
            mean_pe(pe, 5)
            ffn_pe(pe, 3, 5, 3 * FT)
            mean_pe(pe, 6)
            ada_pe(pe)
            mean_pe(pe, 7)
            gdn_pe(pe, 6)
            mean_pe(pe, 8)
            fox_pe(pe, 7)
            mean_pe(pe, 9)
            end_pe(pe)


_INS = ['x', 'positions', 'ffn1_norm', 'ffn1_wi', 'ffn1_wo', 'mix_norm', 'ffn2_norm', 'ffn2_wi', 'ffn2_wo', 'even_w_in',
        'gla_gate_w', 'gla_gate_b', 'gla_out_norm', 'pool_w', 'pool_scale', 'even_w_out', 'odd_w_in', 'odd_w_out',
        'final_norm', 'c_2', 'norm_w_2', 'ada_w_2', 'ada_b_2', 'a_w_in_2', 'a_conv_w_2', 'a_A_log_2', 'a_dt_bias_2',
        'a_norm_w_2', 'a_w_out_2', 'b_w_in_2', 'b_f_bias_2', 'b_qn_w_2', 'b_kn_w_2', 'b_w_out_2', 'final_norm_w_2']


def kernel(**inputs):
    import numpy as _np
    import concourse.bacc as _bacc
    from concourse import mybir as _mybir
    from concourse.bass_utils import run_bass_kernel_spmd as _run

    nc = _bacc.Bacc("TRN2", target_bir_lowering=False, num_devices=1)
    arrays, args = {}, {}
    for name in _INS:
        v = _np.ascontiguousarray(inputs[name])
        arrays[f"in_{name}_dram"] = v
        args[name] = nc.dram_tensor(f"in_{name}_dram", v.shape, _mybir.dt.from_np(v.dtype), kind="ExternalInput").ap()
    inv = _np.concatenate([_np.float32(ROPE_THETA) ** (-_np.arange(0, d, 2, dtype=_np.float32) / _np.float32(d))
                           for d in (ATT_DH, IDX_DIM, IDX_DIM)]).astype(_np.float32)[None, :]
    arrays["in_inv_dram"] = inv
    args["inv"] = nc.dram_tensor("in_inv_dram", inv.shape, _mybir.dt.float32, kind="ExternalInput").ap()
    out = nc.dram_tensor("out_0_dram", (1, T, D), _mybir.dt.float32, kind="ExternalOutput").ap()
    first_and_second_block(nc, args, out)
    r = _run(nc, [arrays], core_ids=[0])
    return r.results[0]["out_0_dram"]
```

```python
from contextlib import ExitStack

import concourse.bass as bass
from concourse import mybir

ALU = mybir.AluOpType
ACT = mybir.ActivationFunctionType
AX = mybir.AxisListType
F32 = mybir.dt.float32
F32R = mybir.dt.float32r
I32 = mybir.dt.int32

P = 128
T = 512
D = 1024
KT = D // P
TT = T // P
FF = 2816
FT = FF // P
EPS = 1e-6
NEG = -1.0e30
TAKEN = -3.0e38
ROPE_THETA = 10000.0
TWO_PI = 6.283185307179586
ROUND = 12582912.0
PI_A, PI_B, PI_C = 6.28125, 1.9350051879882812e-3, 3.0199157e-7

GLA_HEADS, GLA_DK, GLA_CHUNK, GLA_TAU = 4, 64, 64, 16.0
GLA_CH = T // GLA_CHUNK
POOL_GROUPS = 4
ATT_HEADS, ATT_KV, ATT_DH = 8, 2, 128
IDX_HEADS, IDX_DIM, TOPK = 4, 64, 128
GDN_QK, GDN_HEADS, GDN_DH, CONV = 8, 16, 128, 4
GDN_QW, GDN_VW = GDN_QK * GDN_DH, GDN_HEADS * GDN_DH
GDN_Z, GDN_B = 2 * GDN_QW + GDN_VW, 2 * GDN_QW + 2 * GDN_VW
FOX_HEADS, FOX_DH = 16, 64
INV_BLOCK = 16

RAW, SPLIT, BANKS = 4, 4, 4
AHEAD = 2

OUT3 = 3
FFN_B, FFN_T = 2 * FT + OUT3 * KT, 2 * FT + KT
GLA_P = 17
DSA_P = 16
GDN_P = 1 + 6 * GDN_QK
FOX_P = 1 + 4 * (FOX_HEADS // 2)
ADA_P = 2 * 3 * KT
STAGES = [("ffn0", FFN_B, FFN_T), ("gla", GLA_P + KT, GLA_P + KT), ("ffn1", FFN_B, FFN_T), ("ffn2", FFN_B, FFN_T),
          ("dsa", DSA_P + KT, DSA_P + KT), ("ffn3", FFN_B + ADA_P, FFN_T), ("ada", 0, 0),
          ("gdn", GDN_P + 2 * KT, GDN_P + KT), ("fox", FOX_P + KT, FOX_P + KT)]
BASE, _b, _t = {}, 0, 0
for _n, _nb, _nt in STAGES:
    BASE[_n] = (_b, _t)
    _b, _t = _b + _nb, _t + _nt

BLOCKS = _b

R_FFN1, R_MIX, R_FFN2, R_FINAL, R_NORM2, R_FINAL2 = 0, 16, 32, 48, 56, 72
R_GLAN, R_POOLS, R_GATEB, R_GDNN, R_C, R_QN, R_KN, R_INV128, R_INV64 = 80, 84, 88, 90, 91, 99, 100, 101, 102
R_CONV, R_ADAB = P, 2 * P


class Steps:

    def __init__(self, sem, names, lead=0):
        self.sem, self.names, self.n, self.lead = sem, list(names), len(names), lead
        self.at = {name: k + 1 + lead for k, name in enumerate(self.names)}
        assert len(self.at) == self.n
        self.next = 0

    def done(self, name):
        assert self.names[self.next % self.n] == name, (name, self.names[self.next % self.n])
        self.next += 1
        return self.sem, 1

    def after(self, name, turn=0):
        return self.sem, turn * self.n + self.at[name]

    def turns_before(self, turn):
        return self.sem, turn * self.n + self.lead


def col(i, n=1, step=T):
    return bass.ds(i * step, n * step)


def first_and_second_block(nc, a, out):
    with ExitStack() as ctx:
        def sem(name):
            return ctx.enter_context(nc.semaphore(name))

        cursor = [16512]

        def sb(name, cols, dt=F32, parts=P):
            at = cursor[0]
            cursor[0] += -(-cols * 4 // 32) * 32
            return nc.alloc_sbuf_tensor_at(name, [parts, cols], dt, offset=at)

        hres = sb("hres", KT * T)
        x_hi, x_lo = sb("x_hi", KT * T, F32R), sb("x_lo", KT * T, F32R)
        w_raw = [sb(f"w_raw{s}", D) for s in range(RAW)]
        w_hi = [sb(f"w_hi{s}", D, F32R) for s in range(SPLIT)]
        w_lo = [sb(f"w_lo{s}", D, F32R) for s in range(SPLIT)]
        ada_prod = nc.alloc_sbuf_tensor_at("ada_prod", [P, D], F32, offset=cursor[0])
        sumsq, rstd = sb("sumsq", T), sb("rstd", T)
        arena = cursor[0]
        cursor[0] += 48 * T * 4

        def tile(name, k, n=1, dt=F32):
            assert k + n <= 48
            return nc.alloc_sbuf_tensor_at(name, [P, n * T], dt, offset=arena + k * T * 4)

        h_hi, h_lo = tile("h_hi", 0, FT, F32R), tile("h_lo", FT, FT, F32R)
        gdn_hi, gdn_lo = tile("gdn_hi", FT, 16, F32R), tile("gdn_lo", 0, 16, F32R)
        gate_s = [tile(f"gate_s{s}", 44 + s) for s in range(2)]
        prod = [tile(f"prod{s}", 46 + s) for s in range(2)]
        xn = [tile(f"xn{s}", 44 + s) for s in range(2)]
        std, square = tile("std", 46), tile("square", 47)

        ident_r, ones_r, causal_r = sb("ident_r", P, F32R), sb("ones_r", P, F32R), sb("causal_r", P, F32R)
        fox_pick = sb("fox_pick", FOX_HEADS)
        ident, ones, ones64 = sb("ident", P), sb("ones", P), sb("ones64", P)
        swap128, swap64 = sb("swap128", P), sb("swap64", P)
        above_big, in_block, off_block = sb("above_big", P), sb("in_block", P), sb("off_block", P)
        chunk_T = sb("chunk_T", P)
        par = sb("par", 3 * P)
        gate_w = sb("gate_w", 256, parts=16)
        ada_sum = [nc.alloc_sbuf_tensor_at(f"ada_sum{k}", [P, P], F32, offset=cursor[0] + k * P * 4) for k in range(2)]
        pool_w = sb("pool_w", POOL_GROUPS * P)
        gla_cols = sb("gla_cols", 8 * GLA_CH)
        inv_count = sb("inv_count", 16 * POOL_GROUPS)
        small = sb("small", 64)
        eps_c, half_pi, nfox_b, dt_b, neg_a = (small[:, k:k + 1] for k in range(5))
        cond = sb("cond", KT)
        mod = sb("mod", ADA_P)
        gain2 = sb("gain2", 2 * KT)
        assert cursor[0] <= 229344, cursor[0]
        stage_rows = [tile(f"stage_rows{k}", 16 + k) for k in range(3)]
        x_in = tile("x_in", 0, 8)
        causal = tile("causal", 20)[:, 0:P]

        bank = [ctx.enter_context(nc.psum_tensor(f"bank{k}", [P, T], F32)) for k in range(8)]

        w_loaded = [sem(f"w_loaded{s}") for s in range(RAW)]
        part_loaded = sem("part_loaded")
        w_hi_done = sem("w_hi_done")
        w_lo_done = sem("w_lo_done")
        block_done = sem("block_done")
        tile_free = sem("tile_free")
        x_loaded, x_turned, x_taken = sem("x_loaded"), sem("x_turned"), sem("x_taken")
        params_loaded, rows_zeroed = sem("params_loaded"), sem("rows_zeroed")
        rows_turned, rows_taken = sem("rows_turned"), sem("rows_taken")
        consts_made, ident_made = sem("consts_made"), sem("ident_made")
        eps_made, cond_made = sem("eps_made"), sem("cond_made")
        sum_cleared, sum_square, sum_added = sem("sum_cleared"), sem("sum_square"), sem("sum_added")
        mean_done, std_done, rstd_done = sem("mean_done"), sem("std_done"), sem("rstd_done")
        xn_done, x_hi_done, x_ready = sem("xn_done"), sem("x_hi_done"), sem("x_ready")
        silu_done, h_hi_done, h_ready = sem("silu_done"), sem("h_hi_done"), sem("h_ready")
        normed = sem("normed")
        mod_done = sem("mod_done")
        gain_done = sem("gain_done")
        out_normed, out_turned, out_taken, out_stored = (sem(n) for n in ("out_normed", "out_turned", "out_taken", "out_stored"))

        block = ctx.enter_context(nc.Block())
        pe_, act_, dve_, pool_, sp_ = nc.tensor, nc.scalar, nc.vector, nc.gpsimd, nc.sync

        def load(sp, b, src, i=0, n=0, cols=(0, P), kts=KT):
            sp.wait_ge(w_lo_done, b + 1 + i * n)
            dst = w_raw[b % RAW].rearrange("p (k c) -> p k c", c=P)[:, 0:kts, cols[0]:cols[1]]
            sp.dma_start(dst, src).then_inc(w_loaded[b % RAW], 16)

        def load_pair(sp, b, pair, parts):
            sp.wait_ge(w_lo_done, b + 1)
            for k, (src, (c0, c1)) in enumerate(parts):
                dst = w_raw[b % RAW].rearrange("p (k c) -> p k c", c=P)[:, :, c0:c1]
                if k == 0:
                    sp.dma_start(dst, src).then_inc(part_loaded, 16)
                    sp.wait_ge(part_loaded, 16 * (pair + 1))
                else:
                    sp.dma_start(dst, src).then_inc(w_loaded[b % RAW], 16)

        def split_hi(act, b, i=0, n=0):
            act.wait_ge(w_loaded[b % RAW], 16 * (b // RAW + 1) + i * (16 * n // RAW))
            act.wait_ge(block_done, b + 1 + i * n)
            act.activation(w_hi[b % SPLIT][:], w_raw[b % RAW][:], ACT.Copy).then_inc(w_hi_done, 1)

        def split_lo(dve, b, i=0, n=0, split=None):
            dve.wait_ge(w_hi_done, b + 1 - ada_before(b) + i * (n if split is None else split))
            s = b % SPLIT
            dve.tensor_tensor(w_lo[s][:], w_raw[b % RAW][:], w_hi[s][:].bitcast(F32), ALU.subtract).then_inc(w_lo_done, 1)

        def products(pe, b, out, rhs_hi, rhs_lo, kts, first, last, i=0, n=0, part=None, parts=2):
            if not part:
                pe.wait_ge(w_lo_done, RAW + b + 1 + i * n)
            s = b % SPLIT
            for kk, kt in enumerate(kts):
                if part is not None and kk // (KT // parts) != part:
                    continue
                w = slice(kk * P, kk * P + P)
                for m, (lhs, rhs) in enumerate(((w_hi[s], rhs_hi), (w_hi[s], rhs_lo), (w_lo[s], rhs_hi))):
                    mm = pe.matmul(out, lhs[:, w], rhs(kt), start=first and kk == 0 and m == 0,
                                   stop=last and kk == len(kts) - 1 and m == 2)
            if part is None or part == parts - 1:
                mm.then_inc(block_done, 1)

        def x_of(buf):
            return lambda kt: buf[:, kt * T:kt * T + T]

        def weight_cols(w, i, k0=0, k1=KT):
            return w.rearrange("(k p) n -> p k n", p=P)[:, k0:k1, i]

        def in_turns(eng, count, body):
            turns = count // 4
            if turns > 1:
                with eng.Fori(0, turns) as i:
                    for u in range(4):
                        body(u, i, 4)
            else:
                turns = 0
            for u in range(4 * turns, count):
                body(u, 0, 0)

        def project_sp(sp, w, b0, count, col0):
            in_turns(sp, count, lambda u, i, n: load(sp, b0 + u, weight_cols(w, bass.ds(col0 + u * P + i * (n * P), P)), i, n))

        def project_act(act, b0, count):
            in_turns(act, count, lambda u, i, n: split_hi(act, b0 + u + AHEAD, i, n))

        def project_pe(pe, run, b0, t0, count):
            def one(u, i, n):
                pe.wait_ge(tile_free, t0 + u + 1 + i * n)
                products(pe, b0 + u, bank[(t0 + u) % BANKS][:], x_of(x_hi), x_of(x_lo), range(KT), True, True, i, n)
            first_product(pe, run, b0, t0)
            for u in range(1, min(count, 4)):
                one(u, 0, 0)
            if count > 4:
                with pe.Fori(1, count // 4) as i:
                    for u in range(4):
                        one(u, i, 4)
                for u in range(count // 4 * 4, count):
                    one(u, 0, 0)

        def first_product(pe, run, b0, t0):
            pe.wait_ge(tile_free, t0 + 1)
            for k in range(KT):
                pe.wait_ge(x_ready, KT * run + k + 1)
                products(pe, b0, bank[t0 % BANKS][:], x_of(x_hi), x_of(x_lo), range(KT), True, True, part=k, parts=KT)

        def project_dve(dve, b0, t0, count, take):
            def one(u, i, n):
                split_lo(dve, b0 + u + AHEAD, i, n)
                dve.wait_ge(block_done, SPLIT + b0 + u + 1 + i * n)
                take(u + i * n, bank[(t0 + u) % BANKS][:]).then_inc(tile_free, 1)
            in_turns(dve, count, one)

        def cuts(kts):
            return [range(k, min(k + KT, kts)) for k in range(0, kts, KT)]

        def down_sp(sp, w, b0, kts):
            parts = cuts(kts)
            with sp.Fori(0, KT // 4) as i:
                for q in range(4):
                    for m, ks in enumerate(parts):
                        load(sp, b0 + q * len(parts) + m, weight_cols(w, bass.ds(i * (4 * P) + q * P, P), ks[0], ks[-1] + 1),
                             i, 4 * len(parts), kts=len(ks))

        def down_act(act, b0, kts):
            n = len(cuts(kts))
            with act.Fori(0, KT // 4) as i:
                for u in range(4 * n):
                    split_hi(act, b0 + u + AHEAD, i, 4 * n)

        def down_pe(pe, b0, t0, kts, hi, lo, h_sem, h_count):
            parts = cuts(kts)
            with pe.Fori(0, KT // 4) as i:
                for q in range(4):
                    pe.wait_ge(tile_free, t0 + q + 1 + i * 4)
                    for m, ks in enumerate(parts):
                        if q == 0:
                            pe.wait_ge(h_sem, h_count - (kts - 1 - ks[-1]))
                        products(pe, b0 + q * len(parts) + m, bank[(t0 + q) % BANKS][:], x_of(hi), x_of(lo), ks,
                                 m == 0, m == len(parts) - 1, i, 4 * len(parts))

        def down_dve(dve, b0, t0, kts, scale):
            n = len(cuts(kts))
            with dve.Fori(0, KT // 4) as i:
                for q in range(4):
                    for m in range(n):
                        split_lo(dve, b0 + q * n + m + AHEAD, i, 4 * n)
                    dve.wait_ge(block_done, SPLIT + b0 + q * n + n + i * (4 * n))
                    r = hres[:, col(i * 4 + q)]
                    s = scale if isinstance(scale, float) else scale[:, bass.ds(i * 4 + q, 1)]
                    dve.scalar_tensor_tensor(r, bank[(t0 + q) % BANKS][:], s, r, ALU.mult, ALU.add).then_inc(tile_free, 1)

        def squares_pool(pool, r, ready, count0):
            if r:
                pool.wait_ge(mean_done, r)
            pool.memset(sumsq[:], 0.0).then_inc(sum_cleared, 1)
            pool.wait_ge(sum_cleared, r + 1)
            with pool.Fori(0, KT) as n:
                pool.wait_ge(ready, n + count0)
                x = hres[:, col(n)]
                pool.tensor_tensor(square[:], x, x, ALU.mult).then_inc(sum_square, 1)
                pool.wait_ge(sum_square, n + KT * r + 1)
                pool.tensor_tensor(sumsq[:], sumsq[:], square[:], ALU.add).then_inc(sum_added, 1)
                pool.wait_ge(sum_added, n + KT * r + 1)

        def mean_pe(pe, r):
            pe.wait_ge(sum_added, KT * (r + 1))
            pe.matmul(bank[4][:], ones[:], sumsq[:], start=True, stop=True).then_inc(mean_done, 1)

        def std_act(act, r):
            act.activation(small[:, 56 + r % 8:57 + r % 8], eps_c, ACT.Sqrt)
            act.wait_ge(mean_done, r + 1)
            act.activation(std[:], bank[4][:], ACT.Sqrt, bias=eps_c, scale=1.0 / D).then_inc(std_done, 1)

        def rstd_dve(dve, r):
            dve.wait_ge(std_done, r + 1)
            dve.reciprocal(rstd[:], std[:]).then_inc(rstd_done, 1)
            dve.wait_ge(rstd_done, r + 1)

        def norm_act(act, r, run, shift=None):
            std_act(act, r)
            for k in range(KT):
                act.wait_ge(xn_done, KT * run + k + 1)
                if shift is None:
                    act.activation(x_hi[:, k * T:k * T + T], xn[k % 2][:], ACT.Copy).then_inc(x_hi_done, 1)
                else:
                    act.activation(x_hi[:, k * T:k * T + T], xn[k % 2][:], ACT.Identity,
                                   bias=shift[:, k:k + 1]).then_inc(x_hi_done, 1)

        def norm_dve(dve, r, run, gain, shift=None):
            rstd_dve(dve, r)

            def low(k):
                dve.wait_ge(x_hi_done, KT * run + k + 1)
                hi = x_hi[:, k * T:k * T + T].bitcast(F32)
                if shift is None:
                    dve.tensor_tensor(x_lo[:, k * T:k * T + T], xn[k % 2][:], hi, ALU.subtract).then_inc(x_ready, 1)
                else:
                    dve.scalar_tensor_tensor(x_lo[:, k * T:k * T + T], xn[k % 2][:], shift[:, k:k + 1], hi,
                                             ALU.add, ALU.subtract).then_inc(x_ready, 1)
            for k in range(KT):
                if k >= 2:
                    low(k - 2)
                    dve.wait_ge(x_ready, KT * run + k - 1)
                dve.scalar_tensor_tensor(xn[k % 2][:], hres[:, k * T:k * T + T], gain[:, k:k + 1], rstd[:],
                                         ALU.mult, ALU.mult).then_inc(xn_done, 1)
            low(KT - 2)
            low(KT - 1)

        LAST_FFN = 3
        ADA_LATE = ADA_P - 2 * FT
        ada_added = sem("ada_added")

        def ffn_blocks(f):
            own = 4 if f == LAST_FFN else 2
            return *BASE[f"ffn{f}"], own, 2 * FT + (ADA_P if f == LAST_FFN else 0)

        def is_ada(b):
            x = b - BASE[f"ffn{LAST_FFN}"][0]
            return 0 <= x < 2 * FT + ADA_P and (x % 4 >= 2 or x >= 4 * FT)

        def ada_before(b):
            return sum(is_ada(k) for k in range(b))

        def ffn_sp(sp, f, wi, wo):
            b0, _, own, before = ffn_blocks(f)
            layer_turns = 3 * KT // 4
            for m, (i0, i1) in enumerate(((0, layer_turns), (layer_turns, FT // 2)) if own == 4 else ((0, FT // 2),)):
                with sp.Fori(i0, i1) as i:
                    for s in range(2):
                        for g in range(2):
                            load(sp, b0 + own * s + g, weight_cols(wi, bass.ds(i * (2 * P) + s * P + g * FF, P)), i, 2 * own)
                        for g in range(own - 2):
                            c = (2 * s + g - 4 * layer_turns * m) * P
                            load(sp, b0 + own * s + 2 + g, weight_cols(a["ada_w_2"][m], bass.ds(i * (4 * P) + c, P)), i, 2 * own)
            for n in range(before - FT * own):
                c = (2 * FT + n - 3 * KT) * P
                load(sp, b0 + FT * own + n, weight_cols(a["ada_w_2"][1], slice(c, c + P)))
            down_sp(sp, wo, b0 + before, FT)

        def ada_multiply(dve, b, n, i=0):
            dve.wait_ge(w_loaded[b % RAW], 16 * (b // RAW + 1) + i * (16 * 8 // RAW))
            dve.wait_ge(ada_added, 1 + 3 * n + i * 12)
            by_tile = [P, KT, P]
            dve.tensor_tensor(ada_prod[:, :].rearrange("p (k c) -> p k c", c=P), w_raw[b % RAW].rearrange("p (k c) -> p k c", c=P),
                              cond[:, :].rearrange("p (k c) -> p k c", c=1).to_broadcast(by_tile), ALU.mult).then_inc(w_lo_done, 1)

        def ada_add(pool, b, n, i=0, before=4):
            pool.wait_ge(w_lo_done, RAW + b + 1 + i * 8)
            pool.wait_ge(block_done, SPLIT + b - before + 1 + i * 8)
            half = D // 2
            for k in range(3):
                dst = ada_prod[:, 0:half] if k < 2 else ada_sum[n % 2][:]
                pool.tensor_tensor(dst, ada_prod[:, 0:half], ada_prod[:, half:2 * half], ALU.add).then_inc(ada_added, 1)
                pool.wait_ge(ada_added, 1 + 3 * n + k + 1 + i * 12)
                half //= 2

        def ada_column(pe, b, n, i=0):
            pe.wait_ge(ada_added, 1 + 3 * n + 3 + i * 12)
            pe.matmul(bank[5][:, bass.ds(i * 4 + n, 1)], ada_sum[n % 2][:], ones[:, 0:1], start=True, stop=True).then_inc(block_done, 1)

        def ada_pool(pool):
            b0, _, own, before = ffn_blocks(LAST_FFN)
            with pool.Fori(0, FT // 2) as i:
                for n in range(4):
                    ada_add(pool, b0 + n // 2 * 4 + 2 + n % 2, n, i)
            for n in range(ADA_LATE):
                ada_add(pool, b0 + 4 * FT + n, 2 * FT + n, before=2)

        def ffn_pe(pe, f, run, h0):
            b0, t0, own, before = ffn_blocks(f)
            if own == 2:
                project_pe(pe, run, b0, t0, 2 * FT)
            else:
                def one(n, i):
                    b = b0 + n // 2 * 4 + n % 2
                    if n or not isinstance(i, int):
                        pe.wait_ge(tile_free, t0 + n + 1 + i * 4)
                        products(pe, b, bank[(t0 + n) % BANKS][:], x_of(x_hi), x_of(x_lo), range(KT), True, True, i, 8)
                    if n % 2:
                        for g in range(2):
                            ada_column(pe, b + 1 + g, n - 1 + g, i)
                first_product(pe, run, b0, t0)
                for n in range(4):
                    one(n, 0)
                with pe.Fori(1, FT // 2) as i:
                    for n in range(4):
                        one(n, i)
                for n in range(ADA_LATE):
                    ada_column(pe, b0 + 4 * FT + n, 2 * FT + n)
            down_pe(pe, b0 + before, t0 + 2 * FT, FT, h_hi, h_lo, h_ready, h0 + FT)

        def ffn_turns(eng, f, body):
            b0, t0, own, _ = ffn_blocks(f)
            last = FT // 2 - (own == 4)
            with eng.Fori(0, last) as i:
                body(b0, t0, 0, i)
            for turn in range(last, FT // 2):
                body(b0 + 2 * own * turn, t0 + 4 * turn, 2 * turn, 0)

        def ffn_act(act, f):
            b0, t0, own, before = ffn_blocks(f)

            def pairs(b0, t0, k0, i):
                for s in range(2):
                    for b in range(b0 + own * s, b0 + own * s + own):
                        if b == b0 + own * s + own - 1:
                            act.wait_ge(block_done, SPLIT + b0 + own * s + 1 + i * (2 * own))
                            act.activation(gate_s[s][:], bank[(t0 + 2 * s) % BANKS][:], ACT.Silu).then_inc(silu_done, 1)
                        if not is_ada(b + AHEAD):
                            split_hi(act, b + AHEAD, i, 2 * own)
                    act.wait_ge(tile_free, BANKS + t0 + 2 * s + 2 + i * 4)
                    act.activation(h_hi[:, col(i * 2 + k0 + s)], prod[s][:], ACT.Copy).then_inc(h_hi_done, 1)
            ffn_turns(act, f, pairs)
            for b in range(b0 + FT * own, b0 + before):
                if not is_ada(b + AHEAD):
                    split_hi(act, b + AHEAD)
            down_act(act, b0 + before, FT)

        def ffn_dve(dve, f):
            b0, t0, own, before = ffn_blocks(f)

            def ahead_of(b, i=0):
                b += AHEAD
                if is_ada(b):
                    ada_multiply(dve, b, ada_before(b), i)
                else:
                    split_lo(dve, b, i, 2 * own, 4)

            def pairs(b0, t0, k0, i):
                for s in range(2):
                    for b in range(b0 + own * s, b0 + own * s + own):
                        ahead_of(b, i)
                        if b == b0 + own * s + own // 2:
                            dve.wait_ge(silu_done, FT * f + k0 + s + 1 + i * 2)
                            dve.wait_ge(block_done, SPLIT + b0 + own * s + 2 + i * (2 * own))
                            dve.tensor_tensor(prod[s][:], gate_s[s][:], bank[(t0 + 2 * s + 1) % BANKS][:], ALU.mult).then_inc(tile_free, 2)
                    dve.wait_ge(h_hi_done, FT * f + k0 + s + 1 + i * 2)
                    h = col(i * 2 + k0 + s)
                    dve.tensor_tensor(h_lo[:, h], prod[s][:], h_hi[:, h].bitcast(F32), ALU.subtract).then_inc(h_ready, 1)
            ffn_turns(dve, f, pairs)
            for b in range(b0 + FT * own, b0 + before):
                ahead_of(b)
            down_dve(dve, b0 + before, t0 + 2 * FT, FT, 0.5)

        def gla_windows(g):
            return [f"{n}{d}_{g}" for d in range(g + 1) for n in ("head", "sum")] + [f"cnt{g}", f"rest{g}", f"less{g}"]

        gla_qkvg = tile("gla_qkvg", 9, 12)

        class Gla:
            b0, t0 = BASE["gla"]
            a_lr = tile("gla_a_lr", 8)
            q, k, v, g = ([gla_qkvg[:, n * T:n * T + T] for n in range(n0, n1)] for n0, n1 in ((0, 2), (2, 4), (4, 8), (8, 12)))
            g_all = gla_qkvg[:, 8 * T:12 * T]
            u = [tile(f"gla_u{n}", (21, 30, 31, 32)[n]) for n in range(4)]
            zb, az, cum, rel = ([tile(f"gla_{n}{m}", 33 + 2 * k + m) for m in range(2)]
                                for k, n in enumerate(("zb", "az", "cum", "rel")))
            v_tok = [tile(f"gla_v_tok{k}", 41 + k) for k in range(TT)]
            k_tok = [tile(f"gla_k_tok{m}", 45 + m) for m in range(2)]
            states = [tile(f"gla_states{m}", 33 + 2 * m, 2) for m in range(2)]
            probs = [tile(f"gla_probs{h}", (37, 38, 45, 46)[h]) for h in range(4)]
            o_sq, o_std, o_rs, o_n = tile("gla_o_sq", 13), tile("gla_o_std", 39), a_lr, tile("gla_o_n", 40)
            reset = tile("gla_reset", 47)
            win = [sumsq, rstd]
            e_mid, e_end, e_all, end = ([gla_cols[:, (2 * k + m) * GLA_CH:(2 * k + m + 1) * GLA_CH] for m in range(2)] for k in range(4))
            run_s, add_s = tile("gla_state", 14)[:, 0:P], tile("gla_add", 15)[:, 0:P]

            pe = Steps(sem("gla_pe"), ["z0", "z1"] + [f"vt{t}" for t in range(TT)] + ["kt0", "kt1"]
                       + ["kv00", "kv01", "kv10", "kv11"] + [f"sc{h}" for h in range(4)]
                       + [f"{n}{h}" for h in range(4) for n in ("o", "sum")] + [f"pw{g}" for g in range(4)])
            act = Steps(sem("gla_act"), [f"{n}{m}" for m in range(2) for n in ("zb", "az", "ez", "lz")]
                        + [f"{n}{m}" for m in range(2) for n in ("eq", "ek", "e_mid", "e_all", "e_end")]
                        + [f"vt{t}" for t in range(TT)] + ["kt0", "kt1", "silu"]
                        + [f"{n}{h}" for h in range(4) for n in ("sq", "std")] + [f"hi{h}" for h in range(8)])
            dve = Steps(sem("gla_dve"), [f"{n}{m}" for m in range(2) for n in ("la", "cum", "rel", "end")]
                        + ["q0", "k0", "q1", "k1"]
                        + [f"{n}{m}{c}" for m in range(2) for c in range(GLA_CH - 1) for n in ("add", "state", "scaled")]
                        + [f"pr{h}" for h in range(4)] + [f"{n}{h}" for h in range(4) for n in ("rs", "on")]
                        + [f"pw{g}" for g in range(4)] + [f"lo{h}" for h in range(8)])
            pool = Steps(sem("gla_pool"), ["ones", "reset"] + [n for g in range(4) for n in gla_windows(g)]
                         + [f"og{h}" for h in range(4)])

            def out(h):
                return Gla.g[h] if h < 4 else Gla.u[h - 4]

        def gla_sp(sp):
            w, b0 = a["even_w_in"][0], Gla.b0
            load(sp, b0, weight_cols(w, slice(1536, 1552)), cols=(0, 16))
            project_sp(sp, w, b0 + 1, 12, 0)
            project_sp(sp, w, b0 + 13, 4, 1552)
            down_sp(sp, a["even_w_out"][0], b0 + GLA_P, KT)

        def gla_taken(k):
            return tile_free, BANKS + Gla.t0 + k + 1

        def c3(x):
            return x[:, :].rearrange("p (c j) -> p c j", j=GLA_CHUNK)

        def gla_pe(pe, run):
            G, s = Gla, Gla.pe
            project_pe(pe, run, G.b0, G.t0, 1)
            project_pe(pe, run, G.b0 + 1, G.t0 + 1, 12)
            project_pe(pe, run, G.b0 + 13, G.t0 + 13, 4)
            pe.wait_ge(*gla_taken(0))
            for m in range(2):
                pe.matmul(bank[4 + m][:], gate_w[:, m * P:m * P + P], G.a_lr[0:16, :], start=True, stop=True).then_inc(*s.done(f"z{m}"))
            pe.wait_ge(*gla_taken(8))
            for t in range(TT):
                if t >= 2:
                    pe.wait_ge(*G.act.after(f"vt{t - 2}"))
                for h in range(4):
                    mm = pe.transpose(bank[6 + t % 2][:, h * P:h * P + P], G.v[h][:, t * P:t * P + P], ident[:])
                mm.then_inc(*s.done(f"vt{t}"))
            for m in range(2):
                pe.wait_ge(*G.dve.after(f"k{m}"))
                for t in range(TT):
                    mm = pe.transpose(bank[4 + m][:, t * P:t * P + P], G.k[m][:, t * P:t * P + P], ident[:])
                mm.then_inc(*s.done(f"kt{m}"))
            for m in range(2):
                pe.wait_ge(*G.act.after(f"kt{m}"))
                for f in range(2):
                    if m:
                        pe.wait_ge(*G.dve.after(f"add0{(6, 5)[f]}"))
                    for c in range(f, GLA_CH - 1, 2):
                        r = slice(64 * f, 64 * f + 64)
                        for hh in range(2):
                            mm = pe.matmul(bank[6 + f][64 * hh:64 * hh + 64, (c // 2) * P:(c // 2) * P + P],
                                           G.k_tok[m][r, (c // 2) * P + 64 * hh:(c // 2) * P + 64 * hh + 64],
                                           G.v_tok[c // 2][r, (2 * m + hh) * P:(2 * m + hh + 1) * P], start=True, stop=True)
                    mm.then_inc(*s.done(f"kv{m}{f}"))
            for h in range(4):
                m, r = h // 2, slice(64 * (h % 2), 64 * (h % 2) + 64)
                if h >= 2:
                    pe.wait_ge(*G.dve.after(f"pr{h - 2}"))
                for c in range(GLA_CH):
                    x = slice(c * 64, c * 64 + 64)
                    mm = pe.matmul(bank[4 + h % 2][64 * (c % 2):64 * (c % 2) + 64, (c // 2) * 64:(c // 2) * 64 + 64],
                                   G.k[m][r, x], G.q[m][r, x], start=True, stop=True)
                mm.then_inc(*s.done(f"sc{h}"))
            pe.wait_ge(*G.dve.after("pr3"))
            for h in range(4):
                m, r = h // 2, slice(64 * (h % 2), 64 * (h % 2) + 64)
                if h >= 2:
                    pe.wait_ge(*G.dve.after(f"on{h - 2}"))
                for c in range(GLA_CH):
                    x = slice(c * 64, c * 64 + 64)
                    if c % 2 == 0:
                        y = slice(c * 64, c * 64 + P)
                        pe.matmul(bank[6 + h % 2][:, y], G.v_tok[c // 2][:, h * P:h * P + P], G.probs[h][:, y], start=True, stop=False)
                    if c:
                        mm = pe.matmul(bank[6 + h % 2][:, x], G.states[m][r, c * P:c * P + P], G.q[m][r, x], start=False, stop=c % 2 == 1)
                mm.then_inc(*s.done(f"o{h}"))
                pe.wait_ge(*G.act.after(f"sq{h}"))
                pe.matmul(bank[4 + h % 2][:], ones[:], G.o_sq[:], start=True, stop=True).then_inc(*s.done(f"sum{h}"))
            for g in range(4):
                pe.wait_ge(*(G.act.after("std3") if g < 2 else G.dve.after(f"pw{g - 2}")))
                pe.wait_ge(*G.pool.after(f"less{g}"))
                pe.matmul(bank[4 + g % 2][:], pool_w[:, g * P:g * P + P], G.u[g][:], start=True, stop=True).then_inc(*s.done(f"pw{g}"))
            down_pe(pe, G.b0 + GLA_P, G.t0 + GLA_P, KT, h_hi, h_lo, *G.dve.after("lo7"))

        def gla_act(act):
            G, s = Gla, Gla.act
            project_act(act, G.b0, 1)
            project_act(act, G.b0 + 1, 12)
            project_act(act, G.b0 + 13, 4)
            for m in range(2):
                gb = par[:, R_GATEB + m:R_GATEB + m + 1]
                act.wait_ge(*G.pe.after(f"z{m}"))
                act.activation(G.zb[m][:], bank[4 + m][:], ACT.Identity, bias=gb).then_inc(*s.done(f"zb{m}"))
                act.activation(G.az[m][:], bank[4 + m][:], ACT.Abs, bias=gb).then_inc(*s.done(f"az{m}"))
                act.wait_ge(*s.after(f"az{m}"))
                act.activation(G.rel[m][:], G.az[m][:], ACT.Exp, scale=-1.0).then_inc(*s.done(f"ez{m}"))
                act.wait_ge(*s.after(f"ez{m}"))
                act.activation(G.az[m][:], G.rel[m][:], ACT.Ln, bias=1.0).then_inc(*s.done(f"lz{m}"))
            for m in range(2):
                tau = 1.0 / GLA_TAU
                act.wait_ge(*G.dve.after(f"rel{m}"))
                act.activation(G.zb[m][:], G.rel[m][:], ACT.Exp, scale=tau).then_inc(*s.done(f"eq{m}"))
                act.activation(G.az[m][:], G.rel[m][:], ACT.Exp, scale=-tau).then_inc(*s.done(f"ek{m}"))
                act.activation(G.e_mid[m], c3(G.cum[m])[:, :, 31], ACT.Exp, scale=tau).then_inc(*s.done(f"e_mid{m}"))
                act.activation(G.e_all[m], c3(G.cum[m])[:, :, 63], ACT.Exp, scale=tau).then_inc(*s.done(f"e_all{m}"))
                act.wait_ge(*G.dve.after(f"end{m}"))
                act.activation(G.e_end[m], G.end[m], ACT.Exp, scale=tau).then_inc(*s.done(f"e_end{m}"))
            for t in range(TT):
                act.wait_ge(*G.pe.after(f"vt{t}"))
                act.activation(G.v_tok[t][:], bank[6 + t % 2][:], ACT.Copy).then_inc(*s.done(f"vt{t}"))
            for m in range(2):
                act.wait_ge(*G.pe.after(f"kt{m}"))
                act.activation(G.k_tok[m][:], bank[4 + m][:], ACT.Copy).then_inc(*s.done(f"kt{m}"))
            act.wait_ge(*gla_taken(12))
            act.activation(G.g_all[:], G.g_all[:], ACT.Silu).then_inc(*s.done("silu"))
            for h in range(4):
                act.wait_ge(*G.pe.after(f"o{h}"))
                act.activation(G.o_sq[:], bank[6 + h % 2][:], ACT.Square).then_inc(*s.done(f"sq{h}"))
                act.wait_ge(*G.pe.after(f"sum{h}"))
                if h:
                    act.wait_ge(*G.dve.after(f"rs{h - 1}"))
                act.activation(G.o_std[:], bank[4 + h % 2][:], ACT.Sqrt, bias=eps_c, scale=1.0 / P).then_inc(*s.done(f"std{h}"))
            for h in range(8):
                act.wait_ge(*(G.pool.after(f"og{h}") if h < 4 else G.dve.after(f"pw{h - 4}")))
                act.activation(h_hi[:, h * T:h * T + T], G.out(h)[:], ACT.Copy).then_inc(*s.done(f"hi{h}"))
            down_act(act, G.b0 + GLA_P, KT)

        def gla_dve(dve):
            G, s = Gla, Gla.dve

            project_dve(dve, G.b0, G.t0, 1, lambda k, src: dve.tensor_copy(G.a_lr[:], src))
            project_dve(dve, G.b0 + 1, G.t0 + 1, 12, lambda k, src: dve.tensor_copy(gla_qkvg[:, col(k)], src))
            project_dve(dve, G.b0 + 13, G.t0 + 13, 4, lambda k, src: dve.tensor_copy(G.u[k][:], src))
            for m in range(2):
                dve.wait_ge(*G.act.after(f"lz{m}"))
                dve.scalar_tensor_tensor(G.zb[m][:], G.zb[m][:], 0.0, G.az[m][:], ALU.min, ALU.subtract).then_inc(*s.done(f"la{m}"))
                dve.wait_ge(*s.after(f"la{m}"))
                dve.wait_ge(*G.pool.after("reset"))
                dve.tensor_tensor_scan(G.cum[m][:], G.reset[:], G.zb[m][:], 0.0, ALU.mult, ALU.add).then_inc(*s.done(f"cum{m}"))
                dve.wait_ge(*s.after(f"cum{m}"))
                b = c3(G.cum[m])
                dve.tensor_tensor(c3(G.rel[m]), b, b[:, :, 31:32].to_broadcast([P, GLA_CH, GLA_CHUNK]),
                                  ALU.subtract).then_inc(*s.done(f"rel{m}"))
                dve.tensor_tensor(G.end[m], b[:, :, 63], b[:, :, 31], ALU.subtract).then_inc(*s.done(f"end{m}"))
            for m in range(2):
                dve.wait_ge(*G.act.after(f"ek{m}"))
                dve.scalar_tensor_tensor(G.q[m][:], G.q[m][:], GLA_DK ** -0.5, G.zb[m][:], ALU.mult, ALU.mult).then_inc(*s.done(f"q{m}"))
                dve.tensor_tensor(G.k[m][:], G.k[m][:], G.az[m][:], ALU.mult).then_inc(*s.done(f"k{m}"))
            for m in range(2):
                dve.wait_ge(*G.act.after(f"e_end{m}"))
                for c in range(GLA_CH - 1):
                    kv = bank[6 + c % 2][:, (c // 2) * P:(c // 2) * P + P]
                    if c < 2:
                        dve.wait_ge(*G.pe.after(f"kv{m}{c}"))
                    if c or m:
                        dve.wait_ge(*s.after(f"scaled{m}{c - 1}" if c else f"scaled0{GLA_CH - 2}"))
                    dve.tensor_scalar(G.add_s, kv, G.e_end[m][:, c:c + 1], None, ALU.mult).then_inc(*s.done(f"add{m}{c}"))
                    dve.wait_ge(*s.after(f"add{m}{c}"))
                    if c:
                        dve.scalar_tensor_tensor(G.run_s, G.run_s, G.e_all[m][:, c:c + 1], G.add_s,
                                                 ALU.mult, ALU.add).then_inc(*s.done(f"state{m}{c}"))
                    else:
                        dve.tensor_copy(G.run_s, G.add_s).then_inc(*s.done(f"state{m}{c}"))
                    dve.wait_ge(*s.after(f"state{m}{c}"))
                    dve.tensor_scalar(G.states[m][:, (c + 1) * P:(c + 2) * P], G.run_s, G.e_mid[m][:, c + 1:c + 2], None,
                                      ALU.mult).then_inc(*s.done(f"scaled{m}{c}"))
            for h in range(4):
                dve.wait_ge(*G.pe.after(f"sc{h}"))
                halves = [P, TT, 2, GLA_CHUNK]
                dve.tensor_tensor(G.probs[h][:, :].rearrange("p (t r j) -> p t r j", r=2, j=GLA_CHUNK),
                                  bank[4 + h % 2][:, 0:T // 2].rearrange("p (t r j) -> p t r j", r=1, j=GLA_CHUNK).to_broadcast(halves),
                                  chunk_T[:, :].rearrange("p (t r j) -> p t r j", t=1, r=2).to_broadcast(halves),
                                  ALU.mult).then_inc(*s.done(f"pr{h}"))
            for h in range(4):
                dve.wait_ge(*G.act.after(f"std{h}"))
                if h:
                    dve.wait_ge(*s.after(f"on{h - 1}"))
                dve.reciprocal(G.o_rs[:], G.o_std[:]).then_inc(*s.done(f"rs{h}"))
                dve.wait_ge(*s.after(f"rs{h}"))
                if h:
                    dve.wait_ge(*G.pool.after(f"og{h - 1}"))
                dve.scalar_tensor_tensor(G.o_n[:], bank[6 + h % 2][:], par[:, R_GLAN + h:R_GLAN + h + 1], G.o_rs[:],
                                         ALU.mult, ALU.mult).then_inc(*s.done(f"on{h}"))
            for g in range(4):
                dve.wait_ge(*G.pe.after(f"pw{g}"))
                dve.tensor_scalar(G.u[g][:], bank[4 + g % 2][:], par[:, R_POOLS + g:R_POOLS + g + 1], None,
                                  ALU.mult).then_inc(*s.done(f"pw{g}"))
            for h in range(8):
                dve.wait_ge(*G.act.after(f"hi{h}"))
                x = slice(h * T, h * T + T)
                dve.tensor_tensor(h_lo[:, x], G.out(h)[:], h_hi[:, x].bitcast(F32), ALU.subtract).then_inc(*s.done(f"lo{h}"))
            down_dve(dve, G.b0 + GLA_P, G.t0 + GLA_P, KT, 1.0)

        def gla_pool(pool):
            G, s = Gla, Gla.pool
            pool.wait_ge(*gla_taken(0))
            pool.memset(G.reset[:], 1.0).then_inc(*s.done("ones"))
            pool.wait_ge(*s.after("ones"))
            pool.memset(c3(G.reset)[:, :, 0:1], 0.0).then_inc(*s.done("reset"))
            for g in range(POOL_GROUPS):
                pool.wait_ge(*gla_taken(13 + g))
                src = G.u[g]
                for d in range(g + 1):
                    w, dst = 2 ** d, G.win[d % 2]
                    pool.tensor_copy(dst[:, 0:w], src[:, 0:w]).then_inc(*s.done(f"head{d}_{g}"))
                    pool.tensor_tensor(dst[:, w:T], src[:, w:T], src[:, 0:T - w], ALU.add).then_inc(*s.done(f"sum{d}_{g}"))
                    pool.wait_ge(*s.after(f"sum{d}_{g}"))
                    src = dst
                pool.tensor_tensor(src[:, 0:16], src[:, 0:16], inv_count[:, 16 * g:16 * g + 16], ALU.mult).then_inc(*s.done(f"cnt{g}"))
                pool.tensor_scalar(src[:, 16:T], src[:, 16:T], 2.0 ** -(g + 1), None, ALU.mult).then_inc(*s.done(f"rest{g}"))
                pool.wait_ge(*s.after(f"rest{g}"))
                pool.tensor_tensor(G.u[g][:], src[:], G.u[g][:], ALU.subtract).then_inc(*s.done(f"less{g}"))
                pool.wait_ge(*s.after(f"less{g}"))
            pool.wait_ge(*G.act.after("silu"))
            for h in range(4):
                pool.wait_ge(*G.dve.after(f"on{h}"))
                pool.tensor_tensor(G.g[h][:], G.o_n[:], G.g[h][:], ALU.mult).then_inc(*s.done(f"og{h}"))

        nmax, rowsum, rinv = (small[:, 8 + 8 * k:16 + 8 * k] for k in range(3))

        def pipelined(units, first, second, third, between=None):
            out = [first(0), first(1)]
            for u in range(units):
                out.append(second(u))
                if u and third:
                    out.append(third(u - 1))
                if u + 2 < units:
                    out.append(first(u + 2))
                if between:
                    out.append(between(u))
            if third:
                out.append(third(units - 1))
            return out

        def ahead(units, first, second, between=None):
            out = [first(0), first(1), second(0)]
            for u in range(units):
                if u + 2 < units:
                    out.append(first(u + 2))
                if u + 1 < units:
                    out.append(second(u + 1))
                if between:
                    out.append(between(u))
            return out

        def att_names(units):
            def flat(names):
                return [n for ns in names for n in ns.split()]
            return dict(pe=flat(pipelined(units, "s{}".format, "pt{}".format, "pv{}".format)),
                        dve=flat(ahead(units, lambda u: f"mx{u} nm{u}", "ri{}".format)),
                        act=flat(pipelined(units, "ex{}".format, "pc{}".format, None)),
                        pool=[f"pn{u}" for u in range(units)])

        def att_pe(pe, S, turn, units, width, scores, values, p, pT, between=None, out_free=None):
            def score(u):
                if u >= 2:
                    pe.wait_ge(*S.act.after(f"ex{u - 2}", turn))
                scores(u, bank[4 + u % 2][:, 0:width(u)]).then_inc(*S.pe.done(f"s{u}"))

            def turned(u):
                pe.wait_ge(*S.pool.after(f"pn{u}", turn))
                if u >= 1:
                    pe.wait_ge(*S.act.after(f"pc{u - 1}", turn))
                for j in range(width(u) // P):
                    mm = pe.transpose(bank[6][:, j * P:j * P + P], p[u % 2][:, j * P:j * P + P], ident[:])
                mm.then_inc(*S.pe.done(f"pt{u}"))

            def value(u):
                pe.wait_ge(*S.act.after(f"pc{u}", turn))
                if u == 0 and out_free:
                    pe.wait_ge(*out_free)
                out, n = values(u)
                for j in range(width(u) // P):
                    mm = pe.matmul(out, n(j), pT[u % 2][:, j * P:j * P + P], start=j == 0, stop=(j + 1) * P == width(u))
                mm.then_inc(*S.pe.done(f"pv{u}"))
            pipelined(units, score, turned, value, between)

        def att_dve(dve, S, turn, units, width, scale, between=None):
            def top(u):
                dve.wait_ge(*S.pe.after(f"s{u}", turn))
                dve.tensor_reduce(rowsum[:, u:u + 1], bank[4 + u % 2][:, 0:width(u)], AX.X, ALU.max).then_inc(*S.dve.done(f"mx{u}"))
                dve.wait_ge(*S.dve.after(f"mx{u}", turn))
                dve.tensor_scalar(nmax[:, u:u + 1], rowsum[:, u:u + 1], -scale, None, ALU.mult).then_inc(*S.dve.done(f"nm{u}"))

            def inverse(u):
                dve.wait_ge(*S.act.after(f"ex{u}", turn))
                dve.reciprocal(rinv[:, u:u + 1], rowsum[:, u:u + 1]).then_inc(*S.dve.done(f"ri{u}"))
            ahead(units, top, inverse, between)

        def att_act(act, S, turn, units, width, scale, p, pT, between=None):
            def exponentials(u):
                act.wait_ge(*S.dve.after(f"nm{u}", turn))
                act.activation(p[u % 2][:, 0:width(u)], bank[4 + u % 2][:, 0:width(u)], ACT.Exp, bias=nmax[:, u:u + 1],
                               scale=scale, accum_out=rowsum[:, u:u + 1]).then_inc(*S.act.done(f"ex{u}"))

            def copies(u):
                act.wait_ge(*S.pe.after(f"pt{u}", turn))
                if u >= 2:
                    act.wait_ge(*S.pe.after(f"pv{u - 2}", turn))
                act.activation(pT[u % 2][:, 0:width(u)], bank[6][:, 0:width(u)], ACT.Copy).then_inc(*S.act.done(f"pc{u}"))
            pipelined(units, exponentials, copies, None, between)

        def att_pool(pool, S, turn, units, width, p):
            for u in range(units):
                pool.wait_ge(*S.dve.after(f"ri{u}", turn))
                x = p[u % 2][:, 0:width(u)]
                pool.tensor_tensor(x, x, rinv[:, u:u + 1].to_broadcast([P, width(u)]), ALU.mult).then_inc(*S.pool.done(f"pn{u}"))

        dsa_qkv = tile("dsa_qkv", 30, 12)

        class Dsa:
            b0, t0 = BASE["dsa"]
            kk, wi, qi = tile("dsa_kk", 8), tile("dsa_wi", 9), [tile(f"dsa_qi{m}", 10 + m) for m in range(2)]
            qkv = dsa_qkv
            k, v = ([dsa_qkv[:, n * T:n * T + T] for n in range(n0, n0 + 2)] for n0 in (8, 10))
            cos, sin = [tile(f"dsa_cos{m}", 12 + m) for m in range(2)], [tile(f"dsa_sin{m}", 14 + m) for m in range(2)]
            bias = [tile(f"dsa_bias{t}", 16 + t, dt=F32R) for t in range(TT)]
            v_tok = tile("dsa_v_tok", 20, 2)
            work = [None, tile("dsa_work1", 42), tile("dsa_work2", 43), tile("dsa_work3", 46)]
            relu = [tile(f"dsa_relu{m}", 44 + m) for m in range(2)]
            part = [tile(f"dsa_part{m}", 47 - 4 * m) for m in range(2)]
            part2 = [tile(f"dsa_part2{m}", 44 + m) for m in range(2)]
            q_now = [tile(f"dsa_q_now{h}", 42 + 4 * h) for h in range(2)]
            p, pT = [tile(f"dsa_p{m}", 8 + m) for m in range(2)], [tile(f"dsa_pT{m}", 10 + m) for m in range(2)]
            pos = nc.alloc_sbuf_tensor_at("dsa_pos", [P, T], I32, offset=arena + 42 * T * 4)
            posf, ang, turns_ = tile("dsa_posf", 43), tile("dsa_ang", 44), tile("dsa_turns", 45)
            wi_tok, top8 = small[:, 32:48], small[:, 48:56]
            ropes = ["kk", "qi0", "qi1"]
            late = ["k0", "k1"] + [f"q{h}" for h in range(ATT_HEADS)]
            rounds = TOPK // 8
            pos_loaded = sem("dsa_pos_loaded")
            pe = Steps(sem("dsa_pe"), ["wt"] + [f"sw_{n}" for n in ropes] + [f"is{t}{h}" for t in range(1, TT) for h in range(IDX_HEADS)]
                       + [f"sw_{r}" for r in late] + ["vt0", "vt1"])
            act = Steps(sem("dsa_act"), [f"{n}{m}" for m in range(2) for n in ("sin", "abs", "cos")]
                        + [f"rl{t}{h}" for t in range(1, TT) for h in range(IDX_HEADS)] + ["vt0", "vt1"])
            dve = Steps(sem("dsa_dve"), ["posf"] + [f"{n}{m}" for m in range(2) for n in ("ang", "near", "whole", "r1", "r2", "r3", "r4")]
                        + ["wt"] + [f"{n}_{r}" for r in ("kk", "qi0", "qi1") for n in ("sw", "add")]
                        + [n for t in range(1, TT) for n in [f"ac{t}{h}" for h in range(IDX_HEADS)] + [f"diag{t}"] + [f"rest{t}"] * (t < TT - 1)]
                        + [f"{n}{t}_{k}" for t in range(1, TT) for k in range(TOPK // 8) for n in ("top", "out")]
                        + ["bias0", "bias1", "bias2", "bias3"] + [f"{n}_{r}" for r in late for n in ("sw", "add")])
            pool = Steps(sem("dsa_pool"), [f"cos_{r}" for r in ropes + late])

        class DsaPair:
            n = att_names(2 * TT)
            pe = Steps(sem("dsa_pair_pe"), n["pe"], len(n["pe"]))
            act = Steps(sem("dsa_pair_act"), n["act"] + ["hi_0", "hi_1"])
            dve = Steps(sem("dsa_pair_dve"), n["dve"] + ["lo_0", "lo_1"], 1)
            pool = Steps(sem("dsa_pair_pool"), ["q_0", "q_1"] + n["pool"])

        def dsa_taken(k):
            return tile_free, BANKS + Dsa.t0 + k + 1

        def dsa_pairs(eng, body):
            for g in range(ATT_KV):
                with eng.Fori(0, ATT_HEADS // ATT_KV // 2) as i:
                    body(i + g * (ATT_HEADS // ATT_KV // 2), g)

        def dsa_keys(u):
            return (u % TT + 1) * P

        def dsa_out(h):
            return bank[(7, 1)[h]]

        def dsa_sp(sp):
            b0, w = Dsa.b0, a["odd_w_in"][0]
            ki = weight_cols(w, slice(1792, 1856))
            load_pair(sp, b0, 0, ((ki, (0, 64)), (ki, (64, P))))
            load(sp, b0 + 1, weight_cols(w, slice(1856, 1860)), cols=(0, 4))
            for m in range(2):
                load(sp, b0 + 2 + m, weight_cols(w, slice(1536 + m * P, 1536 + m * P + P)))
            project_sp(sp, w, b0 + 4, 12, 0)
            down_sp(sp, a["odd_w_out"][0], b0 + DSA_P, KT)

        def rope_tile(r):
            if r[0] == "q" and r[1] != "i":
                return dsa_qkv[:, int(r[1]) * T:int(r[1]) * T + T]
            return {"kk": Dsa.kk, "qi0": Dsa.qi[0], "qi1": Dsa.qi[1], "k0": Dsa.k[0], "k1": Dsa.k[1]}[r]

        def rope_bank(r):
            return bank[{"kk": 4, "qi0": 5, "qi1": 6}[r]] if r in Dsa.ropes else bank[(4, 5)[Dsa.late.index(r) % 2]]

        def dsa_pe(pe, run):
            S, H, s = Dsa, DsaPair, Dsa.pe
            project_pe(pe, run, S.b0, S.t0, 4)
            pe.wait_ge(*dsa_taken(1))
            for t in range(TT):
                mm = pe.transpose(bank[7][:, 4 * t:4 * t + 4], S.wi[0:4, t * P:t * P + P], ident[0:4, 0:4])
            mm.then_inc(*s.done("wt"))

            def swap(r):
                if r in S.ropes:
                    pe.wait_ge(*dsa_taken({"kk": 0, "qi0": 2, "qi1": 3}[r]))
                else:
                    pe.wait_ge(*dsa_taken(13))
                    k = S.late.index(r)
                    if k >= 2:
                        pe.wait_ge(*S.dve.after(f"sw_{S.late[k - 2]}"))
                pe.matmul(rope_bank(r)[:], (swap64 if r in S.ropes else swap128)[:], rope_tile(r)[:], start=True, stop=True).then_inc(*s.done(f"sw_{r}"))
            for r in S.ropes:
                swap(r)
            for t in range(1, TT):
                for h in range(IDX_HEADS):
                    x = slice(64 * (h % 2), 64 * (h % 2) + 64)
                    if t == 1:
                        pe.wait_ge(*S.dve.after("add_qi1"))
                    else:
                        pe.wait_ge(*S.act.after(f"rl{t - 1}{h}"))
                    pe.matmul(bank[4 + h][:], S.qi[h // 2][x, t * P:t * P + P], S.kk[x, :], start=True, stop=True).then_inc(*s.done(f"is{t}{h}"))
            project_pe(pe, run, S.b0 + 4, S.t0 + 4, 12)
            pe.wait_ge(*S.act.after(f"rl3{IDX_HEADS - 1}"))
            for r in S.late:
                swap(r)
            pe.wait_ge(*dsa_taken(15))
            for f in range(2):
                for t in range(2):
                    for g in range(2):
                        mm = pe.transpose(bank[6 + f][:, (2 * t + g) * P:(2 * t + g + 1) * P],
                                          S.v[g][:, (2 * f + t) * P:(2 * f + t + 1) * P], ident[:])
                mm.then_inc(*s.done(f"vt{f}"))
            pe.wait_ge(*S.dve.after(f"add_{S.late[-1]}"))
            pe.wait_ge(*S.act.after("vt1"))

            pe.sem_inc(H.pe.sem, H.pe.n)

            def pair(j, g):
                pe.wait_ge(*H.pool.after("q_0", j))
                pe.wait_ge(*H.pool.after("q_1", j))

                def scores(u, out):
                    h, t = divmod(u, TT)
                    pe.matmul(out, S.q_now[h][:, t * P:t * P + P], S.k[g][:, 0:dsa_keys(u)], start=True, stop=False)
                    return pe.matmul(out, ident_r[:], S.bias[t][:, 0:dsa_keys(u)], start=False, stop=True)

                def values(u):
                    h, t = divmod(u, TT)
                    return dsa_out(h)[:, t * P:t * P + P], lambda k: S.v_tok[:, (2 * k + g) * P:(2 * k + g + 1) * P]
                att_pe(pe, H, j, 2 * TT, dsa_keys, scores, values, S.p, S.pT, None, H.dve.turns_before(j))
            dsa_pairs(pe, pair)
            down_pe(pe, S.b0 + DSA_P, S.t0 + DSA_P, KT, h_hi, h_lo, *H.dve.turns_before(ATT_HEADS // 2))

        def dsa_act(act):
            S, H, s = Dsa, DsaPair, Dsa.act
            act.dma_start(S.pos[:], a["positions"].to_broadcast([P, T])).then_inc(S.pos_loaded, 16)
            project_act(act, S.b0, 4)
            for m in range(2):
                act.wait_ge(*S.dve.after(f"r4{m}"))
                act.activation(S.sin[m][:], S.ang[:], ACT.Sin).then_inc(*s.done(f"sin{m}"))
                act.activation(S.cos[m][:], S.ang[:], ACT.Abs).then_inc(*s.done(f"abs{m}"))
                act.wait_ge(*s.after(f"abs{m}"))
                act.activation(S.cos[m][:], S.cos[m][:], ACT.Sin, bias=half_pi, scale=-1.0).then_inc(*s.done(f"cos{m}"))
            for t in range(1, TT):
                for h in range(IDX_HEADS):
                    act.wait_ge(*S.pe.after(f"is{t}{h}"))
                    n = IDX_HEADS * (t - 1) + h
                    if n >= 2:
                        tt, hh = divmod(n - 2, IDX_HEADS)
                        act.wait_ge(*S.dve.after(f"ac{tt + 1}{hh}"))
                    act.activation(S.relu[n % 2][:], bank[4 + h][:], ACT.Relu).then_inc(*s.done(f"rl{t}{h}"))
            project_act(act, S.b0 + 4, 12)
            for f in range(2):
                act.wait_ge(*S.pe.after(f"vt{f}"))
                act.activation(S.v_tok[:, f * T:f * T + T], bank[6 + f][:], ACT.Copy).then_inc(*s.done(f"vt{f}"))

            def pair(j, g):
                att_act(act, H, j, 2 * TT, dsa_keys, ATT_DH ** -0.5, S.p, S.pT)
                for h in range(2):
                    act.wait_ge(*H.pe.after(f"pv{TT * h + TT - 1}", j))
                    act.activation(h_hi[:, col(j * 2 + h)], dsa_out(h)[:], ACT.Copy).then_inc(*H.act.done(f"hi_{h}"))
            dsa_pairs(act, pair)
            down_act(act, S.b0 + DSA_P, KT)

        def dsa_dve(dve):
            S, H, s = Dsa, DsaPair, Dsa.dve
            project_dve(dve, S.b0, S.t0, 4, lambda k, src: dve.tensor_copy([S.kk, S.wi, S.qi[0], S.qi[1]][k][:], src))
            dve.wait_ge(S.pos_loaded, 16)
            dve.tensor_copy(S.posf[:], S.pos[:]).then_inc(*s.done("posf"))
            dve.wait_ge(*s.after("posf"))
            for m, row in enumerate((R_INV128, R_INV64)):
                if m:
                    dve.wait_ge(*S.act.after("abs0"))
                dve.tensor_scalar(S.ang[:], S.posf[:], par[:, row:row + 1], None, ALU.mult).then_inc(*s.done(f"ang{m}"))
                dve.wait_ge(*s.after(f"ang{m}"))
                dve.tensor_scalar(S.turns_[:], S.ang[:], 1.0 / TWO_PI, ROUND, ALU.mult, ALU.add).then_inc(*s.done(f"near{m}"))
                dve.wait_ge(*s.after(f"near{m}"))
                dve.tensor_scalar(S.turns_[:], S.turns_[:], -ROUND, None, ALU.add).then_inc(*s.done(f"whole{m}"))
                dve.wait_ge(*s.after(f"whole{m}"))
                for k, c in enumerate((PI_A, PI_B, PI_C)):
                    dve.scalar_tensor_tensor(S.ang[:], S.turns_[:], -c, S.ang[:], ALU.mult, ALU.add).then_inc(*s.done(f"r{k + 1}{m}"))
                    dve.wait_ge(*s.after(f"r{k + 1}{m}"))
                dve.tensor_scalar(S.ang[:], S.ang[:], 3.1415925, -3.1415925, ALU.min, ALU.max).then_inc(*s.done(f"r4{m}"))
            dve.wait_ge(*S.pe.after("wt"))
            dve.tensor_scalar(S.wi_tok, bank[7][:, 0:16], IDX_DIM ** -0.5 * IDX_HEADS ** -0.5, None, ALU.mult).then_inc(*s.done("wt"))

            def rotate(r, m):
                order = S.ropes + S.late
                n = order.index(r)
                dve.wait_ge(*S.pe.after(f"sw_{r}"))
                dve.wait_ge(*S.pool.after(f"cos_{r}"))
                if n >= 2:
                    dve.wait_ge(*s.after(f"add_{order[n - 2]}"))
                dve.tensor_tensor(S.part2[n % 2][:], rope_bank(r)[:], S.sin[m][:], ALU.mult).then_inc(*s.done(f"sw_{r}"))
                dve.wait_ge(*s.after(f"sw_{r}"))
                dve.tensor_tensor(rope_tile(r)[:], S.part[n % 2][:], S.part2[n % 2][:], ALU.add).then_inc(*s.done(f"add_{r}"))
            for r in S.ropes:
                rotate(r, 1)
            for t in range(1, TT):
                for h in range(IDX_HEADS):
                    dve.wait_ge(*S.act.after(f"rl{t}{h}"))
                    r, w = S.relu[h % 2][:], S.wi_tok[:, 4 * t + h:4 * t + h + 1]
                    if h == 0:
                        dve.tensor_scalar(S.work[t][:], r, w, None, ALU.mult).then_inc(*s.done(f"ac{t}{h}"))
                    else:
                        dve.wait_ge(*s.after(f"ac{t}{h - 1}"))
                        dve.scalar_tensor_tensor(S.work[t][:], r, w, S.work[t][:], ALU.mult, ALU.add).then_inc(*s.done(f"ac{t}{h}"))
                dve.wait_ge(*s.after(f"ac{t}{IDX_HEADS - 1}"))
                x = slice(t * P, t * P + P)
                dve.tensor_tensor(S.work[t][:, x], S.work[t][:, x], causal_r[:].bitcast(F32), ALU.add).then_inc(*s.done(f"diag{t}"))
                if t < TT - 1:
                    dve.memset(S.work[t][:, (t + 1) * P:T], NEG).then_inc(*s.done(f"rest{t}"))
            dve.wait_ge(*s.after("diag3"))
            for u in range(12):
                split_lo(dve, S.b0 + 4 + u + AHEAD)
                dve.wait_ge(block_done, SPLIT + S.b0 + 4 + u + 1)
                dve.tensor_copy(S.qkv[:, u * T:u * T + T], bank[(S.t0 + 4 + u) % BANKS][:]).then_inc(tile_free, 1)
                t = 1 + u // 4
                w = S.work[t][:, 0:dsa_keys(t)]
                for k in range(4 * (u % 4), 4 * (u % 4) + 4):
                    if k or t > 1:
                        dve.wait_ge(*s.after(f"out{t}_{k - 1}" if k else f"out{t - 1}_{S.rounds - 1}"))
                    dve.max(S.top8, w).then_inc(*s.done(f"top{t}_{k}"))
                    dve.wait_ge(*s.after(f"top{t}_{k}"))
                    dve.match_replace(w, S.top8, w, TAKEN).then_inc(*s.done(f"out{t}_{k}"))
            dve.wait_ge(*s.after(f"out3_{S.rounds - 1}"))
            dve.tensor_copy(S.bias[0][:, 0:P], causal_r[:].bitcast(F32)).then_inc(*s.done("bias0"))
            for t in range(1, TT):
                w = slice(0, dsa_keys(t))
                dve.tensor_scalar(S.bias[t][:, w], S.work[t][:, w], TAKEN / 2, NEG, ALU.is_gt, ALU.mult).then_inc(*s.done(f"bias{t}"))
            for r in S.late:
                rotate(r, 0)
            dve.sem_inc(H.dve.sem, 1)

            def pair(j, g):
                att_dve(dve, H, j, 2 * TT, dsa_keys, ATT_DH ** -0.5)
                for h in range(2):
                    x = col(j * 2 + h)
                    dve.wait_ge(*H.act.after(f"hi_{h}", j))
                    dve.tensor_tensor(h_lo[:, x], dsa_out(h)[:], h_hi[:, x].bitcast(F32), ALU.subtract).then_inc(*H.dve.done(f"lo_{h}"))
            dsa_pairs(dve, pair)
            down_dve(dve, S.b0 + DSA_P, S.t0 + DSA_P, KT, 1.0)

        def dsa_pool(pool):
            S, H, s = Dsa, DsaPair, Dsa.pool
            pool.wait_ge(*dsa_taken(3))
            pool.wait_ge(*S.act.after("cos1"))
            order = S.ropes + S.late
            for n, r in enumerate(order):
                if r == "k0":
                    pool.wait_ge(*dsa_taken(13))
                    pool.wait_ge(*S.dve.after("bias3"))
                if n >= 2:
                    pool.wait_ge(*S.dve.after(f"add_{order[n - 2]}"))
                pool.tensor_tensor(S.part[n % 2][:], rope_tile(r)[:], S.cos[r in S.ropes][:], ALU.mult).then_inc(*s.done(f"cos_{r}"))
            pool.wait_ge(*S.dve.after(f"add_{S.late[-1]}"))

            def pair(j, g):
                for h in range(2):
                    pool.wait_ge(H.pe.sem, j * H.pe.n + H.pe.at[f"s{TT * h + TT - 1}"] - H.pe.n)
                    pool.tensor_copy(S.q_now[h][:], S.qkv[:, col(j * 2 + h)]).then_inc(*H.pool.done(f"q_{h}"))
                att_pool(pool, H, j, 2 * TT, dsa_keys, S.p)
            dsa_pairs(pool, pair)

        def ada_dve(dve):
            for k in range(KT):
                x = hres[:, k * T:k * T + T]
                dve.scalar_tensor_tensor(x, x, par[:, R_FINAL + k:R_FINAL + k + 1], rstd[:], ALU.mult, ALU.mult).then_inc(normed, 1)
            dve.wait_ge(block_done, SPLIT + BASE["gdn"][0] - OUT3 * KT)
            dve.tensor_tensor(mod[:], bank[5][:, 0:ADA_P], par[:, R_ADAB:R_ADAB + ADA_P], ALU.add).then_inc(mod_done, 1)
            dve.wait_ge(mod_done, 1)
            for m in range(2):
                s = 3 * KT * m + KT
                dve.scalar_tensor_tensor(gain2[:, m * KT:m * KT + KT], mod[:, s:s + KT], 1.0,
                                         par[:, R_NORM2 + m * KT:R_NORM2 + m * KT + KT], ALU.add, ALU.mult).then_inc(gain_done, 1)
            dve.wait_ge(gain_done, 2)

        gdn_cols = tile("gdn_cols", 22)

        def both(names):
            return [f"{n}_{h}" for n in names for h in range(2)]

        class Gdn:
            b0, t0 = BASE["gdn"]
            o = tile("gdn_o", 0, 16)
            qT, kT, k_tok, gates = tile("gdn_qT", 16), tile("gdn_kT", 17), tile("gdn_k_tok", 20), tile("gdn_gates", 21)
            zs = [tile(f"gdn_zs{h}", 18 + h) for h in range(2)]
            vb, kdec, qdec, attnT, E, Pw, W1, W2, W3, W4, W5 = (
                [tile(f"gdn_{n}{h}", 23 + 11 * h + k) for h in range(2)]
                for k, n in enumerate(("vb", "kdec", "qdec", "attnT", "E", "P", "W1_", "W2_", "W3_", "W4_", "W5_")))
            kbg = E
            vT = [tile(f"gdn_vT{h}", 45 + h) for h in range(2)]
            gsel = [sumsq, rstd]
            beta, g, kd, egl, bexp, negb, eg, diff = (gdn_cols[:, 64 * k:64 * k + 64] for k in range(8))
            conv_to = [qT, kT, vT[0], vT[1]]
            raw, x, ax, ex = W1[0], W2[0], W3[0], W4[0]
            reset, last_row = W5[0], W1[1]
            prep_pe = Steps(sem("gdn_prep_pe"), ["turn", "last"])
            prep_act = Steps(sem("gdn_prep_act"), ["beta", "x", "ax", "ex", "ln", "ea", "eg", "egl", "kd"])
            prep_dve = Steps(sem("gdn_prep_dve"), ["sp", "g", "cum", "last_row", "beta", "gt", "diff", "bexp", "negb"])
            prep_pool = Steps(sem("gdn_prep_pool"), ["gates", "ones", "reset"])
            end_act = Steps(sem("gdn_end_act"), [f"hi{k}" for k in range(16)])
            end_dve = Steps(sem("gdn_end_dve"), [f"lo{k}" for k in range(16)])

        class GdnNext:
            act = Steps(sem("gdn_next_act"), [f"cw{u}" for u in range(4)] + [f"cs{u}" for u in range(4)])
            dve = Steps(sem("gdn_next_dve"), [f"c{n}{u}" for u in range(4) for n in "ab"])

        GDN_QUARTERS = ["y1", "at", "y2", "y4", "p1", "p2", "p3", "q3", "g1", "g2", "v1", "f4", "v2", "tt", "wt", "vn0"]

        class GdnTurn:
            pe = Steps(sem("gdn_pe"), ["sum_q", "sum_k", "vt_0", "vt_1", "gb_0", "gb_1", "kt", "kk", "qk"]
                       + both(["y1", "at", "x2", "y2", "x4", "y4", "y8", "p1", "p2", "p3", "q3", "f", "g1", "f2", "g2", "v1", "f4", "v2", "tt", "wt"])
                       + [n for t in range(TT) for n in both([f"vn{t}"]) + [f"{n}{t}_{h}" for h in range(2) for n in (["o", "ds"] if t < TT - 1 else ["o"])]]
                       + both(["sum"]))
            act = Steps(sem("gdn_act"), ["sq_k", "sq_q", "sd_k", "sd_q", "eg_0", "eg_1", "kc"]
                        + both(["dec", "y1", "at", "y2", "y4", "y8", "q3", "g1", "g2", "f4", "tt", "wt"])
                        + [n for t in range(TT) for n in both([f"vn{t}"])] + both(["sq", "oc", "sd"]) + ["zs0", "zs1"])
            dve = Steps(sem("gdn_dve"), ["gs_0", "gs_1", "rc_k", "n_k", "vb_0", "vb_1"]
                        + both(["da", "db"]) + ["rc_q", "n_q"] + both(["kk"]) + ["nb_0", "m_0", "nb_1", "m_1"] + both(["at"])
                        + both(["x2", "x4", "p1", "p2", "p3", "f", "v0", "f2", "v1", "v2"])
                        + [n for t in range(TT - 1) for n in both([f"s{t}"])] + [f"{n}_{h}" for h in range(2) for n in ("rc", "on", "o")], 1)
            pool = Steps(sem("gdn_pool"), both(["kd", "en", "p0", "qd", "kb"]))

        def gdn_turns(eng, body):
            with eng.Fori(0, GDN_QK // 2 - 1) as i:
                for m in range(2):
                    body(i * 2 + m, i, m, False)
            for m in range(2):
                body(GDN_QK - 2 + m, GDN_QK // 2 - 1, m, m == 1)

        def gdn_block(m, u):
            return Gdn.b0 + 1 + 6 * m + u

        def gdn_bank(m, u):
            return bank[(Gdn.t0 + 1 + 6 * m + u) % BANKS]

        def gdn_taken(m, u, i):
            return tile_free, BANKS + Gdn.t0 + 1 + 6 * m + u + 1 + i * 12

        def first(h):
            return bank[(4, 7)[h]]

        def second(h):
            return bank[(5, 6)[h]]

        def t3(x):
            return x[:, :].rearrange("p (t c) -> p t c", c=P)

        def by_row(x):
            return x[:, :].rearrange("p (t c) -> p t c", t=1).to_broadcast([P, TT, P])

        def by_col(x, h):
            return x[:, bass.ds(h * TT, TT)].rearrange("p (t c) -> p t c", c=1).to_broadcast([P, TT, P])

        def gdn_sp(sp):
            w, b0 = a["a_w_in_2"][0], Gdn.b0
            load_pair(sp, b0, 1, tuple((weight_cols(w, slice(GDN_B + 16 * k, GDN_B + 16 * k + 16)), (32 * k, 32 * k + 16)) for k in range(2)))
            with sp.Fori(0, GDN_QK // 2) as i:
                for m in range(2):
                    for u, (c, width) in enumerate(((0, P), (GDN_QW, P), (2 * GDN_QW, 2 * P), (2 * GDN_QW + P, 2 * P),
                                                    (GDN_Z, 2 * P), (GDN_Z + P, 2 * P))):
                        load(sp, gdn_block(m, u), weight_cols(w, bass.ds(i * (2 * width) + (c + m * width), P)), i, 12)
            down_sp(sp, a["a_w_out_2"][0], b0 + GDN_P, 16)

        def gdn_pe(pe, run):
            G, H = Gdn, GdnTurn
            project_pe(pe, run, G.b0, G.t0, 1)
            s = G.prep_pe
            pe.wait_ge(*G.prep_act.after("beta"))
            pe.wait_ge(*G.prep_dve.after("cum"))
            for t in range(TT):
                mm = pe.transpose(bank[6][:, t * 48:t * 48 + 48], G.gates[0:48, t * P:t * P + P], ident[0:48, 0:48])
            mm.then_inc(*s.done("turn"))
            pe.wait_ge(*G.prep_dve.after("gt"))
            pe.wait_ge(*G.prep_dve.after("last_row"))
            pe.matmul(bank[7][:, 0:64], G.last_row[:, 0:P], G.g, start=True, stop=True).then_inc(*s.done("last"))

            def four(out, lhs, rhs, step):
                for t in range(TT):
                    x = slice(t * P, t * P + P)
                    mm = pe.matmul(out[:, x], lhs[:, x], rhs[:, x], start=True, stop=True)
                mm.then_inc(*H.pe.done(step))

            def turned(out, x, step):
                for t in range(TT):
                    c = slice(t * P, t * P + P)
                    mm = pe.transpose(out[:, c], x[:, c], ident[:])
                mm.then_inc(*H.pe.done(step))

            def project(m, u, i, part=None):
                if not part:
                    pe.wait_ge(tile_free, G.t0 + 1 + 6 * m + u + 1 + i * 12)
                products(pe, gdn_block(m, u), gdn_bank(m, u)[:], x_of(x_hi), x_of(x_lo), range(KT), True, True, i, 12, part, 4)
            for u in range(4):
                project(0, u, 0)

            def turn(j, i, m, last):
                act, dve, pool = ((lambda n, S=S: pe.wait_ge(*S.after(n, j))) for S in (H.act, H.dve, H.pool))

                def quarter(step):
                    if not last:
                        u, part = divmod(GDN_QUARTERS.index(step), 4)
                        project(m + 1, u, i, part)
                project(m, 4, i)
                act("sq_q")
                pe.matmul(first(0)[:], ones[:], G.Pw[0][:], start=True, stop=True).then_inc(*H.pe.done("sum_q"))
                pe.matmul(second(1)[:], ones[:], G.Pw[1][:], start=True, stop=True).then_inc(*H.pe.done("sum_k"))
                turned(first(1), G.vT[0], "vt_0")
                act("sd_q")
                turned(first(0), G.vT[1], "vt_1")
                for h in range(2):
                    dve(f"gs_{h}")
                    pe.matmul(second(h)[:], ones[32:48, :], G.gsel[h][32:48, :], start=True, stop=True).then_inc(*H.pe.done(f"gb_{h}"))
                project(m, 5, i)
                dve("vb_1")
                turned(first(0), G.kT, "kt")
                act("kc")
                four(first(0), G.kT, G.kT, "kk")
                dve("n_q")
                four(first(1), G.qT, G.kT, "qk")
                for h in range(2):
                    dve(("m_0", "at_1")[h])
                    turned(first(h), G.W4[h], f"y1_{h}")
                quarter("y1")
                for h in range(2):
                    dve(f"at_{h}")
                    turned(second(h), G.W2[h], f"at_{h}")
                quarter("at")
                for h in range(2):
                    act(f"at_{h}")
                    act(f"y1_{h}")
                    four(second(h), G.W1[h], G.W4[h], f"x2_{h}")
                for h in range(2):
                    four(first(h), G.W4[h], G.W1[h], f"y2_{h}")
                quarter("y2")
                for h in range(2):
                    dve(f"x2_{h}")
                    act(f"y2_{h}")
                    four(second(h), G.W3[h], G.W2[h], f"x4_{h}")
                for h in range(2):
                    four(first(h), G.W2[h], G.W3[h], f"y4_{h}")
                quarter("y4")
                for h in range(2):
                    dve(f"x4_{h}")
                    act(f"y4_{h}")
                    four(second(h), G.W1[h], G.W4[h], f"y8_{h}")
                for h in range(2):
                    pool(f"p0_{h}")
                    four(first(h), G.W3[h], G.Pw[h], f"p1_{h}")
                quarter("p1")
                for h in range(2):
                    act(f"y8_{h}")
                    dve(f"p1_{h}")
                    four(second(h), G.W4[h], G.Pw[h], f"p2_{h}")
                quarter("p2")
                for h in range(2):
                    dve(f"p2_{h}")
                    four(first(h), G.W2[h], G.Pw[h], f"p3_{h}")
                quarter("p3")
                for h in range(2):
                    dve(f"p3_{h}")
                    turned(second(h), G.Pw[h], f"q3_{h}")
                quarter("q3")
                for h in range(2):
                    act(f"q3_{h}")
                    pool(f"en_{h}")
                    four(first(h), G.W1[h], G.E[h], f"f_{h}")
                for h in range(2):
                    four(second(h), G.E[h], G.W1[h], f"g1_{h}")
                quarter("g1")
                for h in range(2):
                    dve(f"f_{h}")
                    act(f"g1_{h}")
                    four(first(h), G.W4[h], G.W3[h], f"f2_{h}")
                for h in range(2):
                    dve(f"v0_{h}")
                    four(second(h), G.W3[h], G.W4[h], f"g2_{h}")
                quarter("g2")
                for h in range(2):
                    dve(f"f2_{h}")
                    four(first(h), G.W1[h], G.W5[h], f"v1_{h}")
                quarter("v1")
                for h in range(2):
                    act(f"g2_{h}")
                    four(second(h), G.W2[h], G.W1[h], f"f4_{h}")
                quarter("f4")
                for h in range(2):
                    act(f"f4_{h}")
                    dve(f"v1_{h}")
                    four(first(h), G.W3[h], G.W5[h], f"v2_{h}")
                quarter("v2")
                for h in range(2):
                    dve(f"v2_{h}")
                    four(second(h), G.Pw[h], G.W5[h], f"tt_{h}")
                quarter("tt")
                for h in range(2):
                    act(f"tt_{h}")
                    pool(f"kb_{h}")
                    four(first(h), G.kbg[h], G.W4[h], f"wt_{h}")
                quarter("wt")
                for t in range(TT):
                    x = slice(t * P, t * P + P)
                    for h in range(2):
                        act(f"wt_{h}")
                        if t:
                            dve(f"s{t - 1}_{h}")
                        S, vn = G.W1[h][:, 0:P], first(h)[:, (t % 2) * P:(t % 2) * P + P]
                        mm = pe.matmul(vn, G.W4[h][:, x], G.vb[h][:, x], start=True, stop=t == 0)
                        if t:
                            mm = pe.matmul(vn, G.W2[h][:, x], S, start=False, stop=True)
                        mm.then_inc(*H.pe.done(f"vn{t}_{h}"))
                    if t == 0:
                        quarter("vn0")
                    for h in range(2):
                        S, new = G.W1[h][:, 0:P], G.W1[h][:, (1 + t % 2) * P:(2 + t % 2) * P]
                        if t:
                            pool(f"qd_{h}")
                            pe.matmul(second(h)[:, x], S, G.qdec[h][:, x], start=True, stop=False)
                        act(f"vn{t}_{h}")
                        pe.matmul(second(h)[:, x], new, G.attnT[h][:, x], start=t == 0, stop=True).then_inc(*H.pe.done(f"o{t}_{h}"))
                        if t < TT - 1:
                            pool(f"kd_{h}")
                            pe.matmul(first(h)[:, 2 * P:3 * P], G.kdec[h][:, x], new, start=True, stop=True).then_inc(*H.pe.done(f"ds{t}_{h}"))
                for h in range(2):
                    act(f"sq_{h}")
                    pe.matmul(first(h)[:], ones[:], G.W3[h][:], start=True, stop=True).then_inc(*H.pe.done(f"sum_{h}"))
            gdn_turns(pe, turn)
            down_pe(pe, G.b0 + GDN_P, G.t0 + GDN_P, 16, gdn_hi, gdn_lo, *G.end_dve.after("lo15"))

        def gdn_act(act):
            G, H, s = Gdn, GdnTurn, Gdn.prep_act
            project_act(act, G.b0, 1)
            act.wait_ge(tile_free, BANKS + G.t0 + 1)
            act.wait_ge(*G.prep_pool.after("gates"))
            r = slice(32, 48)
            act.activation(G.gates[0:16, :], G.raw[0:16, :], ACT.Sigmoid).then_inc(*s.done("beta"))
            act.activation(G.x[r, :], G.raw[r, :], ACT.Identity, bias=dt_b[r, :]).then_inc(*s.done("x"))
            act.activation(G.ax[r, :], G.raw[r, :], ACT.Abs, bias=dt_b[r, :]).then_inc(*s.done("ax"))
            act.wait_ge(*s.after("ax"))
            act.activation(G.ex[r, :], G.ax[r, :], ACT.Exp, scale=-1.0).then_inc(*s.done("ex"))
            act.wait_ge(*s.after("ex"))
            act.activation(G.ax[r, :], G.ex[r, :], ACT.Ln, bias=1.0).then_inc(*s.done("ln"))
            act.activation(neg_a[r, :], neg_a[r, :], ACT.Exp).then_inc(*s.done("ea"))
            act.wait_ge(*G.prep_dve.after("gt"))
            act.activation(G.eg, G.g, ACT.Exp).then_inc(*s.done("eg"))
            act.wait_ge(*G.prep_pe.after("last"))
            act.activation(G.egl, bank[7][:, 0:64], ACT.Exp).then_inc(*s.done("egl"))
            act.wait_ge(*G.prep_dve.after("diff"))
            act.activation(G.kd, G.diff, ACT.Exp).then_inc(*s.done("kd"))

            N = GdnNext

            def conv(u, j, i, m):
                split_hi(act, gdn_block(m, u) + AHEAD, i, 12)
                act.wait_ge(block_done, SPLIT + gdn_block(m, u) + 1 + i * 12)
                act.activation(G.conv_to[u][:], gdn_bank(m, u)[:], ACT.Copy, scale=par[:, gdn_tap(3, u, j)]).then_inc(*N.act.done(f"cw{u}"))

            def silus(j, i, m):
                for u in range(4):
                    act.wait_ge(*gdn_taken(m, u, i))
                    act.activation(G.conv_to[u][:], G.conv_to[u][:], ACT.Silu).then_inc(*N.act.done(f"cs{u}"))
            act.wait_ge(*G.prep_dve.after("negb"))
            for u in range(4):
                conv(u, 0, 0, 0)
            silus(0, 0, 0)

            def turn(j, i, m, last):
                pe, dve, pool, own = ((lambda n, S=S: act.wait_ge(*S.after(n, j))) for S in (H.pe, H.dve, H.pool, H.act))

                def conv_next(u):
                    if not last:
                        conv(u, j + 1, i, m + 1)

                def run(step, out, src, f, **kw):
                    act.activation(out, src, f, **kw).then_inc(*H.act.done(step))

                for u, n in ((1, "k"), (0, "q")):
                    act.wait_ge(*N.act.after(f"cs{u}", j))
                    run(f"sq_{n}", G.Pw[u][:], G.conv_to[u][:], ACT.Square)
                split_hi(act, gdn_block(m, 4) + AHEAD, i, 12)
                for u, n in ((1, "k"), (0, "q")):
                    pe(f"sum_{n}")
                    run(f"sd_{n}", G.W1[u][:], (first(0), second(1))[u][:], ACT.Sqrt, bias=eps_c)
                split_hi(act, gdn_block(m, 5) + AHEAD, i, 12)
                for h in range(2):
                    pe(f"gb_{h}")
                    run(f"eg_{h}", G.W5[h][:], second(h)[:], ACT.Exp)
                pe("kt")
                run("kc", G.k_tok[:], first(0)[:], ACT.Copy)
                for h in range(2):
                    dve(f"db_{h}")
                    run(f"dec_{h}", G.W3[h][:], G.W3[h][:], ACT.Exp, scale=-1.0)

                def copies(step, dst, src):
                    for h in range(2):
                        pe(f"{step}_{h}")
                        run(f"{step}_{h}", dst[h][:], src(h)[:], ACT.Copy)
                for h in range(2):
                    pool(f"en_{h}")
                copies("y1", G.W1, first)
                copies("at", G.attnT, second)
                copies("y2", G.W3, first)
                pool("p0_0")
                pool("p0_1")
                copies("y4", G.W4, first)
                copies("y8", G.W2, second)
                pool("qd_1")
                conv_next(0)
                copies("q3", G.W1, second)
                copies("g1", G.W4, second)
                conv_next(1)
                copies("g2", G.W2, second)
                copies("f4", G.W3, second)
                copies("tt", G.W4, second)
                conv_next(2)
                for h in range(2):
                    pe(f"wt_{h}")
                    run(f"wt_{h}", G.W2[h][:], first(h)[:], ACT.Copy, scale=-1.0)
                for t in range(TT):
                    for h in range(2):
                        pe(f"vn{t}_{h}")
                        if t >= 2:
                            pe(f"o{t - 2}_{h}")
                            pe(f"ds{t - 2}_{h}")
                        run(f"vn{t}_{h}", G.W1[h][:, (1 + t % 2) * P:(2 + t % 2) * P], first(h)[:, (t % 2) * P:(t % 2) * P + P], ACT.Copy)
                for h in range(2):
                    pe(f"o{TT - 1}_{h}")
                    run(f"sq_{h}", G.W3[h][:], second(h)[:], ACT.Square)
                for h in range(2):
                    run(f"oc_{h}", G.W2[h][:], second(h)[:], ACT.Copy, scale=par[:, R_GDNN:R_GDNN + 1])
                conv_next(3)
                for h in range(2):
                    pe(f"sum_{h}")
                    run(f"sd_{h}", G.W5[h][:], first(h)[:], ACT.Sqrt, bias=eps_c, scale=1.0 / P)
                for h in range(2):
                    act.wait_ge(*gdn_taken(m, 4 + h, i))
                    run(f"zs{h}", G.zs[h][:], G.zs[h][:], ACT.Silu)
                if not last:
                    silus(j + 1, i, m + 1)
            act.wait_ge(*H.dve.turns_before(0))
            gdn_turns(act, turn)
            act.wait_ge(*H.dve.turns_before(GDN_QK))
            for k in range(16):
                x = slice(k * T, k * T + T)
                act.activation(gdn_hi[:, x], G.o[:, x], ACT.Copy).then_inc(*G.end_act.done(f"hi{k}"))
            down_act(act, G.b0 + GDN_P, 16)

        def gdn_tap(tap, u, j):
            row = R_CONV + 32 * tap
            return bass.ds((j + row) if u == 0 else (j + (row + GDN_QK)) if u == 1 else (j * 2 + (row + 2 * GDN_QK + u - 2)), 1)

        def gdn_dve(dve):
            G, H, s = Gdn, GdnTurn, Gdn.prep_dve
            project_dve(dve, G.b0, G.t0, 1, lambda k, src: dve.tensor_copy(G.raw[:], src))
            r = slice(32, 48)
            dve.wait_ge(*G.prep_act.after("ea"))
            dve.scalar_tensor_tensor(G.x[r, :], G.x[r, :], 0.0, G.ax[r, :], ALU.max, ALU.add).then_inc(*s.done("sp"))
            dve.wait_ge(*s.after("sp"))
            dve.tensor_scalar(G.x[r, :], G.x[r, :], neg_a[r, :], -1.0, ALU.mult, ALU.mult).then_inc(*s.done("g"))
            dve.wait_ge(*s.after("g"))
            dve.wait_ge(*G.prep_pool.after("reset"))
            dve.tensor_tensor_scan(G.gates[r, :], G.reset[r, :], G.x[r, :], 0.0, ALU.mult, ALU.add).then_inc(*s.done("cum"))
            dve.tensor_copy(G.last_row[:, 0:P], ident[:, P - 1:P].to_broadcast([P, P])).then_inc(*s.done("last_row"))
            dve.wait_ge(*G.prep_pe.after("turn"))
            for n, dst, c in (("beta", G.beta, 0), ("gt", G.g, 32)):
                dve.tensor_copy(dst.rearrange("p (h t) -> p t h", t=TT),
                                bank[6][:, 0:48 * TT].rearrange("p (t x) -> p t x", x=48)[:, :, c:c + 16]).then_inc(*s.done(n))
            dve.wait_ge(*s.after("gt"))
            dve.wait_ge(*G.prep_act.after("egl"))
            dve.tensor_tensor(G.diff, bank[7][:, 0:64], G.g, ALU.subtract).then_inc(*s.done("diff"))
            dve.tensor_tensor(G.bexp, G.beta, G.eg, ALU.mult).then_inc(*s.done("bexp"))
            dve.tensor_scalar(G.negb, G.beta, -1.0, None, ALU.mult).then_inc(*s.done("negb"))
            dve.wait_ge(*s.after("negb"))
            dve.wait_ge(*G.prep_act.after("kd"))
            dve.sem_inc(H.dve.sem, 1)

            def take(u, j, i, m):
                split_lo(dve, gdn_block(m, u) + AHEAD, i, 12)
                dve.wait_ge(block_done, SPLIT + gdn_block(m, u) + 1 + i * 12)
                src = gdn_bank(m, u)
                if u >= 4:
                    dve.tensor_copy(G.zs[u - 4][:], src[:]).then_inc(tile_free, 1)
                    return
                dve.wait_ge(*N.act.after(f"cw{u}", j))
                c = G.conv_to[u]
                for d, n in ((1, "a"), (2, "b"), (3, None)):
                    if d > 1:
                        dve.wait_ge(*N.dve.after(f"c{'ab'[d - 2]}{u}", j))
                    ins = dve.scalar_tensor_tensor(c[:, d:T], src[:, 0:T - d], par[:, gdn_tap(3 - d, u, j)], c[:, d:T], ALU.mult, ALU.add)
                    if n:
                        ins.then_inc(*N.dve.done(f"c{n}{u}"))
                    else:
                        ins.then_inc(tile_free, 1)
            N = GdnNext
            for u in range(4):
                take(u, 0, 0, 0)

            def turn(j, i, m, last):
                pe, act, pool, own = ((lambda n, S=S: dve.wait_ge(*S.after(n, j))) for S in (H.pe, H.act, H.pool, H.dve))

                def done(step):
                    return H.dve.done(step)

                def tt(step, out, x, y, op):
                    dve.tensor_tensor(out, x, y, op).then_inc(*done(step))

                def take_next(u):
                    if not last:
                        take(u, j + 1, i, m + 1)
                dve.wait_ge(*H.dve.turns_before(j))
                for h in range(2):
                    dve.tensor_scalar(G.gsel[h][32:48, :], G.gates[32:48, :], ident[32:48, bass.ds(j * 2 + (32 + h), 1)], None,
                                      ALU.mult).then_inc(*done(f"gs_{h}"))
                take(4, j, i, m)

                def normed_qk(u, n, scale):
                    act(f"sd_{n}")
                    dve.reciprocal(G.W2[u][:], G.W1[u][:]).then_inc(*done(f"rc_{n}"))
                    own(f"rc_{n}")
                    dve.scalar_tensor_tensor(G.conv_to[u][:], G.conv_to[u][:], scale, G.W2[u][:], ALU.mult, ALU.mult).then_inc(*done(f"n_{n}"))
                normed_qk(1, "k", 1.0)
                for h in range(2):
                    pe(f"vt_{h}")
                    tt(f"vb_{h}", t3(G.vb[h]), t3(first(1 - h)), by_col(G.beta, j * 2 + h), ALU.mult)
                for h in range(2):
                    act(f"eg_{h}")
                    tt(f"da_{h}", t3(G.W3[h]), t3(second(h)), by_row(above_big), ALU.add)
                for h in range(2):
                    own(f"da_{h}")
                    tt(f"db_{h}", t3(G.W3[h]), t3(G.W3[h]), by_col(G.g, j * 2 + h), ALU.subtract)
                normed_qk(0, "q", GDN_DH ** -0.5)
                take(5, j, i, m)
                for h in range(2):
                    act(f"dec_{h}")
                    pe("kk")
                    tt(f"kk_{h}", G.W4[h][:], first(0)[:], G.W3[h][:], ALU.mult)
                for h in range(2):
                    own(f"kk_{h}")
                    tt(f"nb_{h}", t3(G.W1[h]), t3(G.W4[h]), by_col(G.negb, j * 2 + h), ALU.mult)
                    own(f"nb_{h}")
                    tt(f"m_{h}", t3(G.W4[h]), t3(G.W1[h]), by_row(in_block), ALU.mult)
                for h in range(2):
                    pe("qk")
                    tt(f"at_{h}", G.W2[h][:], first(1)[:], G.W3[h][:], ALU.mult)
                for h in range(2):
                    pe(f"x2_{h}")
                    pe(f"at_{h}")
                    dve.tensor_copy(G.W2[h][:], second(h)[:]).then_inc(*done(f"x2_{h}"))
                for h in range(2):
                    pe(f"x4_{h}")
                    pe(f"y2_{h}")
                    dve.tensor_copy(G.W1[h][:], second(h)[:]).then_inc(*done(f"x4_{h}"))
                for n, src in (("p1", first), ("p2", second), ("p3", first)):
                    for h in range(2):
                        pe(f"{n}_{h}")
                        if n != "p1":
                            own(f"p{int(n[1]) - 1}_{h}")
                        tt(f"{n}_{h}", G.Pw[h][:], G.Pw[h][:], src(h)[:], ALU.add)
                    if n == "p1":
                        take_next(0)
                for h in range(2):
                    pe(f"f_{h}")
                    dve.tensor_copy(G.W3[h][:], first(h)[:]).then_inc(*done(f"f_{h}"))
                for h in range(2):
                    act(f"g1_{h}")
                    tt(f"v0_{h}", t3(G.W5[h]), t3(second(h)), by_row(ident), ALU.add)
                take_next(1)
                for h in range(2):
                    pe(f"f2_{h}")
                    dve.tensor_copy(G.W1[h][:], first(h)[:]).then_inc(*done(f"f2_{h}"))
                for n, before in (("v1", "v0"), ("v2", "v1")):
                    for h in range(2):
                        pe(f"{n}_{h}")
                        own(f"{before}_{h}")
                        tt(f"{n}_{h}", G.W5[h][:], G.W5[h][:], first(h)[:], ALU.add)
                take_next(2)
                for t in range(TT - 1):
                    for h in range(2):
                        pe(f"ds{t}_{h}")
                        S, add = G.W1[h][:, 0:P], first(h)[:, 2 * P:3 * P]
                        if t:
                            own(f"s{t - 1}_{h}")
                            dve.scalar_tensor_tensor(S, S, G.egl[:, bass.ds((j * 2 + h) * TT + t, 1)], add, ALU.mult, ALU.add).then_inc(*done(f"s{t}_{h}"))
                        else:
                            dve.tensor_copy(S, add).then_inc(*done(f"s{t}_{h}"))
                take_next(3)
                for h in range(2):
                    act(f"sd_{h}")
                    dve.reciprocal(G.W3[h][:], G.W5[h][:]).then_inc(*done(f"rc_{h}"))
                    own(f"rc_{h}")
                    tt(f"on_{h}", G.W2[h][:], G.W2[h][:], G.W3[h][:], ALU.mult)
                    own(f"on_{h}")
                    act(f"zs{h}")
                    tt(f"o_{h}", G.o[:, col(j * 2 + h)], G.W2[h][:], G.zs[h][:], ALU.mult)
            gdn_turns(dve, turn)
            for k in range(16):
                x = slice(k * T, k * T + T)
                dve.wait_ge(*G.end_act.after(f"hi{k}"))
                dve.tensor_tensor(gdn_lo[:, x], G.o[:, x], gdn_hi[:, x].bitcast(F32), ALU.subtract).then_inc(*G.end_dve.done(f"lo{k}"))
            down_dve(dve, G.b0 + GDN_P, G.t0 + GDN_P, 16, mod[:, 2 * KT:3 * KT])

        def gdn_pool(pool):
            G, H, s = Gdn, GdnTurn, Gdn.prep_pool
            pool.wait_ge(x_ready, KT * 7)
            pool.memset(G.gates[:], 0.0).then_inc(*s.done("gates"))
            pool.memset(G.reset[:], 1.0).then_inc(*s.done("ones"))
            pool.wait_ge(*s.after("ones"))
            pool.memset(t3(G.reset)[:, :, 0:1], 0.0).then_inc(*s.done("reset"))

            def turn(j, i, m, last):
                act, dve = ((lambda n, S=S: pool.wait_ge(*S.after(n, j))) for S in (H.act, H.dve))

                def tt(step, out, x, y, op):
                    pool.tensor_tensor(out, x, y, op).then_inc(*H.pool.done(step))
                act("kc")
                for h in range(2):
                    tt(f"kd_{h}", t3(G.kdec[h]), t3(G.k_tok), by_col(G.kd, j * 2 + h), ALU.mult)
                for h in range(2):
                    dve(f"nb_{h}")
                    tt(f"en_{h}", t3(G.E[h]), t3(G.W1[h]), by_row(off_block), ALU.mult)
                for h in range(2):
                    dve(f"m_{h}")
                    tt(f"p0_{h}", t3(G.Pw[h]), t3(G.W4[h]), by_row(ident), ALU.add)
                for h in range(2):
                    act(f"eg_{h}")
                    dve("n_q")
                    tt(f"qd_{h}", G.qdec[h][:], G.qT[:], G.W5[h][:], ALU.mult)
                for h in range(2):
                    pool.wait_ge(*H.pe.after(f"g1_{h}", j))
                    tt(f"kb_{h}", t3(G.kbg[h]), t3(G.k_tok), by_col(G.bexp, j * 2 + h), ALU.mult)
            gdn_turns(pool, turn)

        class Fox:
            b0, t0 = BASE["fox"]
            f, x, ax, ex, all_ones = (tile(f"fox_{n}", 8 + k) for k, n in enumerate(("f", "x", "ax", "ex", "all_ones")))
            cum, hi48 = tile("fox_cum", 13), tile("fox_hi48", 14, dt=F32R)
            c_parts = tile("fox_c_parts", 45, dt=F32R)
            q, k, v, z = ([tile(f"fox_{n}{m}", t + m) for m in range(2)] for n, t in (("q", 16), ("k", 18), ("v", 20), ("z", 30)))
            v_tok = [tile(f"fox_v_tok{m}", 32 + m) for m in range(2)]
            csel = [[tile(f"fox_csel{m}{h}", 34 + 2 * m + h, dt=F32R) for h in range(2)] for m in range(2)]
            sq, sd = ([tile(f"fox_{n}{k}", t + k) for k in range(2)] for n, t in (("sq", 8), ("sd", 10)))
            rs = tile("fox_rs", 12)
            p, pT = [tile(f"fox_p{k}", 38 + k) for k in range(2)], [tile(f"fox_pT{k}", 40 + k) for k in range(2)]
            gated = tile("fox_gated", 42)
            act = Steps(sem("fox_act"), ["x", "ax", "ex", "ln"])
            dve = Steps(sem("fox_dve"), ["log_f", "cum", "scaled", "high", "own_high", "parts"])
            pool = Steps(sem("fox_pool"), ["ones"])

        class FoxNext:
            pe = Steps(sem("fox_next_pe"), ["sum_q", "sum_k", "vt"])
            act = Steps(sem("fox_next_act"), ["sq_q", "sq_k", "sd_q", "sd_k", "vt"])
            dve = Steps(sem("fox_next_dve"), ["cs_0", "cs_1", "rc_q", "n_q", "rc_k", "n_k"])

        class FoxTurn:
            n = att_names(2 * TT)
            pe = Steps(sem("fox_turn_pe"), n["pe"])
            at = n["act"].index("ex6") + 1
            act = Steps(sem("fox_turn_act"), n["act"][:at] + ["zs"] + n["act"][at:] + ["hi"])
            dve = Steps(sem("fox_turn_dve"), n["dve"] + ["gated", "lo"], 1)
            pool = Steps(sem("fox_turn_pool"), n["pool"])

        FOX_W, FOX_PAIRS = FOX_HEADS * FOX_DH, FOX_HEADS // 2

        def fox_turns(eng, body):
            with eng.Fori(0, FOX_PAIRS // 2 - 1) as i:
                for m in range(2):
                    body(i * 2 + m, i, m, False)
            for m in range(2):
                body(FOX_PAIRS - 2 + m, FOX_PAIRS // 2 - 1, m, m == 1)

        def fox_block(m, u):
            return Fox.b0 + 1 + 4 * m + u

        def fox_bank(m, u):
            return bank[(Fox.t0 + 1 + 4 * m + u) % BANKS]

        def fox_taken(m, u, i):
            return tile_free, BANKS + Fox.t0 + 1 + 4 * m + u + 1 + i * 8

        def fox_keys(u):
            return (u % TT + 1) * P

        def fox_sp(sp):
            w, b0 = a["b_w_in_2"][0], Fox.b0
            wf = weight_cols(w, slice(4 * FOX_W, 4 * FOX_W + FOX_HEADS))
            load_pair(sp, b0, 2, ((wf, (0, FOX_HEADS)), (wf, (32, 32 + FOX_HEADS))))
            with sp.Fori(0, FOX_PAIRS // 2) as i:
                for m in range(2):
                    for u in range(4):
                        load(sp, fox_block(m, u), weight_cols(w, bass.ds(i * (2 * P) + (u * FOX_W + m * P), P)), i, 8)
            down_sp(sp, a["b_w_out_2"][0], b0 + FOX_P, KT)

        def fox_next_pe(pe, u, j, m, i):
            F, N = Fox, FoxNext

            def project(k, part=None):
                if not part:
                    pe.wait_ge(tile_free, F.t0 + 1 + 4 * m + k + 1 + i * 8)
                products(pe, fox_block(m, k), fox_bank(m, k)[:], x_of(x_hi), x_of(x_lo), range(KT), True, True, i, 8, part)
            if u in (3, 4):
                k, n = u - 3, "qk"[u - 3]
                pe.wait_ge(*N.act.after(f"sq_{n}", j))
                pe.matmul(fox_bank(m, k)[:], ones64[:], F.sq[k][:], start=True, stop=True).then_inc(*N.pe.done(f"sum_{n}"))
            if u < 2:
                project(u)
            elif u < 6:
                project(u // 2 + 1, u % 2)
            elif u == 7:
                pe.wait_ge(*fox_taken(m, 2, i))
                for t in range(TT):
                    mm = pe.transpose(fox_bank(m, 2)[:, t * P:t * P + P], F.v[m % 2][:, t * P:t * P + P], ident[:])
                mm.then_inc(*N.pe.done("vt"))

        def fox_next_act(act, u, j, m, i):
            F, N = Fox, FoxNext
            if u in (0, 1, 5, 6):
                split_hi(act, fox_block(m, (0, 1, 5, 6).index(u)) + AHEAD, i, 8)
            if u in (2, 3):
                k, n = u - 2, "qk"[u - 2]
                act.wait_ge(*fox_taken(m, k, i))
                act.activation(F.sq[k][:], (F.q, F.k)[k][m % 2][:], ACT.Square).then_inc(*N.act.done(f"sq_{n}"))
            if u == 4:
                for k, n in enumerate("qk"):
                    act.wait_ge(*N.pe.after(f"sum_{n}", j))
                    act.activation(F.sd[k][:], fox_bank(m, k)[:], ACT.Sqrt, bias=eps_c, scale=1.0 / FOX_DH).then_inc(*N.act.done(f"sd_{n}"))
            if u == 7:
                act.wait_ge(*N.pe.after("vt", j))
                act.activation(F.v_tok[m % 2][:], fox_bank(m, 2)[:], ACT.Copy).then_inc(*N.act.done("vt"))

        def fox_next_dve(dve, u, j, m, i):
            F, N = Fox, FoxNext
            if u == 1:
                for h in range(2):
                    dve.tensor_scalar(F.csel[m % 2][h][:], F.c_parts[:].bitcast(F32), fox_pick[:, bass.ds(j * 2 + h, 1)], None,
                                      ALU.mult).then_inc(*N.dve.done(f"cs_{h}"))
            if u in (1, 2, 6, 7):
                k = (1, 2, 6, 7).index(u)
                split_lo(dve, fox_block(m, k) + AHEAD, i, 8)
                dve.wait_ge(block_done, SPLIT + fox_block(m, k) + 1 + i * 8)
                dve.tensor_copy((F.q, F.k, F.v, F.z)[k][m % 2][:], fox_bank(m, k)[:]).then_inc(tile_free, 1)
            if u in (4, 5):
                k, n, row = ((0, "q", R_QN), (1, "k", R_KN))[u - 4]
                x = (F.q, F.k)[k][m % 2]
                dve.wait_ge(*N.act.after(f"sd_{n}", j))
                if k:
                    dve.wait_ge(*N.dve.after("n_q", j))
                dve.reciprocal(F.rs[:], F.sd[k][:]).then_inc(*N.dve.done(f"rc_{n}"))
                dve.wait_ge(*N.dve.after(f"rc_{n}", j))
                dve.scalar_tensor_tensor(x[:], x[:], par[:, row:row + 1], F.rs[:], ALU.mult, ALU.mult).then_inc(*N.dve.done(f"n_{n}"))

        def fox_pe(pe, run):
            F, N, H = Fox, FoxNext, FoxTurn
            project_pe(pe, run, F.b0, F.t0, 1)
            for u in range(2 * TT):
                fox_next_pe(pe, u, 0, 0, 0)

            def turn(j, i, m, last):
                pe.wait_ge(*N.dve.after("n_k", j))
                pe.wait_ge(*N.act.after("vt", j))

                def scores(u, out):
                    h, t = divmod(u, TT)
                    r = slice(64 * h, 64 * h + 64)
                    pe.matmul(out, F.q[m][r, t * P:t * P + P], F.k[m][r, 0:fox_keys(u)], start=True, stop=False)
                    pe.matmul(out, ones_r[:], F.csel[m][h][:, 0:fox_keys(u)], start=False, stop=False)
                    return pe.matmul(out[:, t * P:t * P + P], ident_r[:], causal_r[:], start=False, stop=True)

                def values(u):
                    h, t = divmod(u, TT)
                    return (bank[7][64 * h:64 * h + 64, t * P:t * P + P],
                            lambda k: F.v_tok[m][:, k * P + 64 * h:k * P + 64 * h + 64])
                att_pe(pe, H, j, 2 * TT, fox_keys, scores, values, F.p, F.pT,
                       None if last else lambda u: fox_next_pe(pe, u, j + 1, m + 1, i), H.dve.turns_before(j))
            fox_turns(pe, turn)
            down_pe(pe, F.b0 + FOX_P, F.t0 + FOX_P, KT, h_hi, h_lo, *H.dve.turns_before(FOX_PAIRS))

        def fox_act(act):
            F, H, s = Fox, FoxTurn, Fox.act
            project_act(act, F.b0, 1)
            act.wait_ge(tile_free, BANKS + F.t0 + 1)
            r = slice(0, P)
            act.activation(F.x[r, :], F.f[r, :], ACT.Identity, bias=nfox_b[r, :]).then_inc(*s.done("x"))
            act.activation(F.ax[r, :], F.f[r, :], ACT.Abs, bias=nfox_b[r, :]).then_inc(*s.done("ax"))
            act.wait_ge(*s.after("ax"))
            act.activation(F.ex[r, :], F.ax[r, :], ACT.Exp, scale=-1.0).then_inc(*s.done("ex"))
            act.wait_ge(*s.after("ex"))
            act.activation(F.ax[r, :], F.ex[r, :], ACT.Ln, bias=1.0).then_inc(*s.done("ln"))
            act.wait_ge(*F.dve.after("parts"))
            for u in range(2 * TT):
                fox_next_act(act, u, 0, 0, 0)

            def turn(j, i, m, last):
                def between(u):
                    if not last:
                        fox_next_act(act, u, j + 1, m + 1, i)
                    if u == 4:
                        act.wait_ge(*fox_taken(m, 3, i))
                        act.activation(F.z[m][:], F.z[m][:], ACT.Silu).then_inc(*H.act.done("zs"))
                att_act(act, H, j, 2 * TT, fox_keys, FOX_DH ** -0.5, F.p, F.pT, between)
                act.wait_ge(*H.dve.after("gated", j))
                act.activation(h_hi[:, col(j)], F.gated[:], ACT.Copy).then_inc(*H.act.done("hi"))
            fox_turns(act, turn)
            down_act(act, F.b0 + FOX_P, KT)

        def fox_dve(dve):
            F, H, s = Fox, FoxTurn, Fox.dve
            project_dve(dve, F.b0, F.t0, 1, lambda k, src: dve.tensor_copy(F.f[:], src))
            r = slice(0, P)
            dve.wait_ge(*F.act.after("ln"))
            dve.scalar_tensor_tensor(F.x[r, :], F.x[r, :], 0.0, F.ax[r, :], ALU.min, ALU.subtract).then_inc(*s.done("log_f"))
            dve.wait_ge(*s.after("log_f"))
            dve.wait_ge(*F.pool.after("ones"))
            dve.tensor_tensor_scan(F.cum[r, :], F.all_ones[r, :], F.x[r, :], 0.0, ALU.mult, ALU.add).then_inc(*s.done("cum"))
            dve.wait_ge(*s.after("cum"))
            dve.tensor_scalar(F.cum[r, :], F.cum[r, :], -(FOX_DH ** 0.5), None, ALU.mult).then_inc(*s.done("scaled"))
            dve.wait_ge(*s.after("scaled"))
            dve.tensor_copy(F.c_parts[0:32, :], F.cum[0:32, :])
            dve.tensor_copy(F.c_parts[64:P, :], F.cum[64:P, :]).then_inc(*s.done("high"))
            dve.tensor_copy(F.hi48[32:64, :], F.cum[32:64, :]).then_inc(*s.done("own_high"))
            dve.wait_ge(*s.after("own_high"))
            dve.tensor_tensor(F.c_parts[32:64, :], F.cum[32:64, :], F.hi48[32:64, :].bitcast(F32), ALU.subtract).then_inc(*s.done("parts"))
            dve.wait_ge(*s.after("parts"))
            dve.sem_inc(H.dve.sem, 1)
            for u in range(2 * TT):
                fox_next_dve(dve, u, 0, 0, 0)

            def turn(j, i, m, last):
                att_dve(dve, H, j, 2 * TT, fox_keys, FOX_DH ** -0.5,
                        None if last else lambda u: fox_next_dve(dve, u, j + 1, m + 1, i))
                dve.wait_ge(*H.pe.after(f"pv{2 * TT - 1}", j))
                dve.wait_ge(*H.act.after("zs", j))
                dve.tensor_tensor(F.gated[:], bank[7][:], F.z[m][:], ALU.mult).then_inc(*H.dve.done("gated"))
                dve.wait_ge(*H.act.after("hi", j))
                dve.tensor_tensor(h_lo[:, col(j)], F.gated[:], h_hi[:, col(j)].bitcast(F32), ALU.subtract).then_inc(*H.dve.done("lo"))
            fox_turns(dve, turn)
            down_dve(dve, F.b0 + FOX_P, F.t0 + FOX_P, KT, mod[:, 5 * KT:6 * KT])

        def fox_pool(pool):
            F, H = Fox, FoxTurn
            pool.memset(F.all_ones[:], 1.0).then_inc(*F.pool.done("ones"))

            def turn(j, i, m, last):
                att_pool(pool, H, j, 2 * TT, fox_keys, F.p)
            fox_turns(pool, turn)

        ROWS = [("ffn1_norm", R_FFN1), ("mix_norm", R_MIX), ("ffn2_norm", R_FFN2), ("final_norm", R_FINAL),
                ("norm_w_2", R_NORM2), ("final_norm_w_2", R_FINAL2), ("gla_out_norm", R_GLAN), ("pool_scale", R_POOLS),
                ("gla_gate_b", R_GATEB), ("a_norm_w_2", R_GDNN), ("c_2", R_C)]
        PARAM_LOADS = len(ROWS) + 2 * 4 + 2 + 2 + 4

        def start_sp(sp):
            for t in range(TT):
                sp.dma_start(x_in[:, t * D:t * D + D], a["x"][0, t * P:t * P + P, :]).then_inc(x_loaded, 16)

        def start_act(act):
            def rows(src):
                src = src.flatten()
                return src.rearrange("(r c) -> r c", c=P)
            act.wait_ge(rows_zeroed, 1)
            for name, r in ROWS:
                src = rows(a[name])
                act.dma_start(stage_rows[0][r:r + src.shape[0], 0:P], src).then_inc(params_loaded, 16)
            for name, r in (("b_qn_w_2", R_QN), ("b_kn_w_2", R_KN)):
                for half in range(2):
                    act.dma_start(stage_rows[0][r:r + 1, half * 64:half * 64 + 64], a[name]).then_inc(params_loaded, 16)
            for half in range(2):
                act.dma_start(stage_rows[0][R_INV128:R_INV128 + 1, half * 64:half * 64 + 64], a["inv"][:, 0:64]).then_inc(params_loaded, 16)
            act.dma_start(stage_rows[0][R_INV64:R_INV64 + 1, 0:64], a["inv"][:, 64:128]).then_inc(params_loaded, 16)
            act.dma_start(stage_rows[0][R_INV64:R_INV64 + 1, 64:128], a["inv"][:, 64:128]).then_inc(params_loaded, 16)
            act.dma_start(stage_rows[1][:, 0:P], rows(a["a_conv_w_2"])).then_inc(params_loaded, 16)
            act.dma_start(stage_rows[2][0:2 * 3 * KT, 0:P], rows(a["ada_b_2"])).then_inc(params_loaded, 16)
            act.dma_start(gate_w[:], a["gla_gate_w"][0]).then_inc(params_loaded, 16)
            act.dma_start(pool_w[:, :].rearrange("c (g d) -> c g d", g=POOL_GROUPS),
                          a["pool_w"][0].rearrange("g c d -> c g d")).then_inc(params_loaded, 16)
            for r in (0, 32):
                act.dma_start(nfox_b[r:r + FOX_HEADS, :], a["b_f_bias_2"].rearrange("o h -> h o")).then_inc(params_loaded, 16)
            act.dma_start(dt_b[32:48, :], a["a_dt_bias_2"].rearrange("o h -> h o")).then_inc(params_loaded, 16)
            act.dma_start(neg_a[32:48, :], a["a_A_log_2"].rearrange("o h -> h o")).then_inc(params_loaded, 16)
            for b in range(AHEAD):
                split_hi(act, b)
            act.wait_ge(rows_taken, 1)
            act.wait_ge(eps_made, 1)
            act.activation(cond[:], par[:, R_C:R_C + KT], ACT.Silu).then_inc(cond_made, 1)

        consts_total = []

        def start_pool(pool):
            made = [0]

            def step(ins):
                made[0] += 1
                ins.then_inc(consts_made, 1)
                pool.wait_ge(consts_made, made[0])

            def keep(t, pattern, base, cm, op, fill):
                step(pool.affine_select(out=t, in_=t, pattern=pattern, compare_op=op, fill=fill, base=base, channel_multiplier=cm))
            for k in range(2):
                step(pool.memset(stage_rows[2 * k][:, 0:P], 0.0))
            step(pool.memset(small[:], 0.0))
            pool.sem_inc(rows_zeroed, 1)
            step(pool.memset(causal, 0.0))
            for t, v in ((ident, 0.0), (ones, 1.0), (ones64, 0.0), (swap128, 0.0), (swap64, 0.0), (above_big, 0.0),
                         (in_block, 1.0), (off_block, 1.0)):
                step(pool.memset(t[:], v))
            line = [[-1, P]]
            keep(ident[:], line, 0, 1, ALU.not_equal, 1.0)
            pool.sem_inc(ident_made, 1)
            squares_pool(pool, 0, x_taken, 1)
            for r in (slice(0, 64), slice(64, P)):
                step(pool.memset(ones64[r, r], 1.0))
            keep(swap128[:], line, -64, 1, ALU.not_equal, -1.0)
            keep(swap128[:], line, 64, 1, ALU.not_equal, 1.0)
            for b in range(4):
                keep(swap64[:, 32 * b:32 * b + 32], [[-1, 32]], (32 if b % 2 else -32) - 32 * b, 1, ALU.not_equal, 1.0 if b % 2 else -1.0)
            keep(above_big[:], line, 0, 1, ALU.is_ge, -NEG)
            keep(causal, line, 0, 1, ALU.is_ge, NEG)
            for t in (in_block, off_block):
                keep(t[:], line, -1, 1, ALU.is_ge, 0.0)
            blocks = in_block[:, :].rearrange("p (b j) -> p b j", j=INV_BLOCK)
            keep(blocks, [[-INV_BLOCK, P // INV_BLOCK], [0, INV_BLOCK]], 0, 1, ALU.is_ge, 0.0)
            keep(blocks, [[INV_BLOCK, P // INV_BLOCK], [0, INV_BLOCK]], INV_BLOCK - 1, -1, ALU.is_ge, 0.0)
            step(pool.tensor_tensor(off_block[:], off_block[:], in_block[:], ALU.subtract))
            step(pool.memset(fox_pick[:], 0.0))
            for r in (0, 32):
                keep(fox_pick[:], [[-1, FOX_HEADS]], -r, 1, ALU.not_equal, 1.0)
            step(pool.memset(chunk_T[:], 1.0))
            keep(chunk_T[:], [[1, P]], 0, -1, ALU.is_ge, 0.0)
            step(pool.memset(chunk_T[0:64, 64:P], 0.0))
            for g in range(POOL_GROUPS):
                w = 2 ** (g + 1)
                step(pool.memset(inv_count[:, 16 * g:16 * g + 16], 1.0 / w))
                for t in range(w - 1):
                    step(pool.memset(inv_count[:, 16 * g + t:16 * g + t + 1], 1.0 / (t + 1)))
            consts_total.append(made[0])

        def start_pe(pe):
            pe.sem_inc(block_done, SPLIT)
            pe.wait_ge(ident_made, 1)
            pe.wait_ge(x_loaded, 16 * TT)
            for k in range(KT):
                if k >= 2:
                    pe.wait_ge(x_taken, k - 1)
                for t in range(TT):
                    mm = pe.transpose(bank[5 + k % 2][:, t * P:t * P + P], x_in[:, t * D + k * P:t * D + k * P + P], ident[:])
                mm.then_inc(x_turned, 1)
            pe.wait_ge(params_loaded, 16 * PARAM_LOADS)
            for k in range(3):
                mm = pe.transpose(bank[7][:, k * P:k * P + P], stage_rows[k][:, 0:P], ident[:])
            mm.then_inc(rows_turned, 1)

        def start_dve(dve):
            dve.sem_inc(w_lo_done, RAW)
            dve.sem_inc(tile_free, BANKS)
            dve.sem_inc(ada_added, 1)
            dve.wait_ge(rows_zeroed, 1)
            dve.memset(eps_c, EPS)
            dve.memset(half_pi, TWO_PI / 4).then_inc(eps_made, 1)
            for k in range(KT):
                dve.wait_ge(x_turned, k + 1)
                dve.tensor_copy(hres[:, k * T:k * T + T], bank[5 + k % 2][:]).then_inc(x_taken, 1)
            for b in range(AHEAD):
                split_lo(dve, b)
            dve.wait_ge(rows_turned, 1)
            dve.tensor_copy(par[:], bank[7][:, 0:3 * P]).then_inc(rows_taken, 1)
            dve.wait_ge(rows_taken, 1)
            dve.wait_ge(cond_made, 1)

        def constants_dve(dve):
            dve.wait_ge(consts_made, consts_total[0])
            dve.tensor_copy(ident_r[:], ident[:])
            dve.tensor_copy(ones_r[:], ones[:])
            dve.tensor_copy(causal_r[:], causal)

        y_T, y = tile("y_T", 0, KT), tile("y", 8, KT)

        def end_sp(sp):
            for b in range(BLOCKS, BLOCKS + AHEAD):
                load(sp, b, weight_cols(a["b_w_out_2"][0], slice(0, P)))
            for t in range(TT):
                sp.wait_ge(out_taken, 2 * t + 2)
                sp.dma_start(out[0, t * P:t * P + P, :], y[:, t * D:t * D + D]).then_inc(out_stored, 16)
            sp.wait_ge(out_stored, 16 * TT)

        def end_dve(dve, r, gain):
            rstd_dve(dve, r)
            for k in range(KT):
                x = slice(k * T, k * T + T)
                dve.scalar_tensor_tensor(y_T[:, x], hres[:, x], gain[:, k:k + 1], rstd[:], ALU.mult, ALU.mult).then_inc(out_normed, 1)
            for n in range(2 * TT):
                dve.wait_ge(out_turned, n + 1)
                dve.tensor_copy(y[:, n * T:n * T + T], bank[4 + n % 2][:]).then_inc(out_taken, 1)

        def end_pe(pe):
            pe.wait_ge(out_normed, KT)
            for n in range(2 * TT):
                if n >= 2:
                    pe.wait_ge(out_taken, n - 1)
                for k in range(4):
                    mm = pe.transpose(bank[4 + n % 2][:, k * P:k * P + P], y_T[:, ((n % 2) * 4 + k) * T + (n // 2) * P:((n % 2) * 4 + k) * T + (n // 2 + 1) * P], ident[:])
                mm.then_inc(out_turned, 1)

        def resid(name):
            b0, t0 = BASE[name]
            nt = dict((n, t) for n, _, t in STAGES)[name]
            return BANKS + t0 + nt - KT + 1

        def gain(r):
            return par[:, r:r + KT]

        @block.sync
        def _(sp):
            start_sp(sp)
            ffn_sp(sp, 0, a["ffn1_wi"][0], a["ffn1_wo"][0])
            gla_sp(sp)
            ffn_sp(sp, 1, a["ffn2_wi"][0], a["ffn2_wo"][0])
            ffn_sp(sp, 2, a["ffn1_wi"][1], a["ffn1_wo"][1])
            dsa_sp(sp)
            ffn_sp(sp, 3, a["ffn2_wi"][1], a["ffn2_wo"][1])
            gdn_sp(sp)
            fox_sp(sp)
            end_sp(sp)

        @block.gpsimd
        def _(pool):
            start_pool(pool)
            squares_pool(pool, 1, tile_free, resid("ffn0"))
            gla_pool(pool)
            squares_pool(pool, 2, tile_free, resid("gla"))
            squares_pool(pool, 3, tile_free, resid("ffn1"))
            squares_pool(pool, 4, tile_free, resid("ffn2"))
            dsa_pool(pool)
            squares_pool(pool, 5, tile_free, resid("dsa"))
            ada_pool(pool)
            squares_pool(pool, 6, tile_free, resid("ffn3"))
            squares_pool(pool, 7, normed, 1)
            gdn_pool(pool)
            squares_pool(pool, 8, tile_free, resid("gdn"))
            fox_pool(pool)
            squares_pool(pool, 9, tile_free, resid("fox"))

        @block.scalar
        def _(act):
            start_act(act)
            norm_act(act, 0, 0)
            ffn_act(act, 0)
            norm_act(act, 1, 1)
            gla_act(act)
            norm_act(act, 2, 2)
            ffn_act(act, 1)
            norm_act(act, 3, 3)
            ffn_act(act, 2)
            norm_act(act, 4, 4)
            dsa_act(act)
            norm_act(act, 5, 5)
            ffn_act(act, 3)
            std_act(act, 6)
            norm_act(act, 7, 6, mod[:, 0:KT])
            gdn_act(act)
            norm_act(act, 8, 7, mod[:, 3 * KT:4 * KT])
            fox_act(act)
            std_act(act, 9)

        @block.vector
        def _(dve):
            start_dve(dve)
            norm_dve(dve, 0, 0, gain(R_FFN1))
            constants_dve(dve)
            ffn_dve(dve, 0)
            norm_dve(dve, 1, 1, gain(R_MIX))
            gla_dve(dve)
            norm_dve(dve, 2, 2, gain(R_FFN2))
            ffn_dve(dve, 1)
            norm_dve(dve, 3, 3, gain(R_FFN1 + KT))
            ffn_dve(dve, 2)
            norm_dve(dve, 4, 4, gain(R_MIX + KT))
            dsa_dve(dve)
            norm_dve(dve, 5, 5, gain(R_FFN2 + KT))
            ffn_dve(dve, 3)
            rstd_dve(dve, 6)
            ada_dve(dve)
            norm_dve(dve, 7, 6, gain2[:, 0:KT], mod[:, 0:KT])
            gdn_dve(dve)
            norm_dve(dve, 8, 7, gain2[:, KT:2 * KT], mod[:, 3 * KT:4 * KT])
            fox_dve(dve)
            end_dve(dve, 9, gain(R_FINAL2))

        @block.tensor
        def _(pe):
            start_pe(pe)
            mean_pe(pe, 0)
            ffn_pe(pe, 0, 0, 0)
            pe.wait_ge(consts_made, consts_total[0])
            mean_pe(pe, 1)
            gla_pe(pe, 1)
            mean_pe(pe, 2)
            ffn_pe(pe, 1, 2, FT)
            mean_pe(pe, 3)
            ffn_pe(pe, 2, 3, 2 * FT)
            mean_pe(pe, 4)
            dsa_pe(pe, 4)
            mean_pe(pe, 5)
            ffn_pe(pe, 3, 5, 3 * FT)
            mean_pe(pe, 6)
            mean_pe(pe, 7)
            gdn_pe(pe, 6)
            mean_pe(pe, 8)
            fox_pe(pe, 7)
            mean_pe(pe, 9)
            end_pe(pe)


_INS = ['x', 'positions', 'ffn1_norm', 'ffn1_wi', 'ffn1_wo', 'mix_norm', 'ffn2_norm', 'ffn2_wi', 'ffn2_wo', 'even_w_in',
        'gla_gate_w', 'gla_gate_b', 'gla_out_norm', 'pool_w', 'pool_scale', 'even_w_out', 'odd_w_in', 'odd_w_out',
        'final_norm', 'c_2', 'norm_w_2', 'ada_w_2', 'ada_b_2', 'a_w_in_2', 'a_conv_w_2', 'a_A_log_2', 'a_dt_bias_2',
        'a_norm_w_2', 'a_w_out_2', 'b_w_in_2', 'b_f_bias_2', 'b_qn_w_2', 'b_kn_w_2', 'b_w_out_2', 'final_norm_w_2']


def kernel(**inputs):
    import numpy as _np
    import concourse.bacc as _bacc
    from concourse import mybir as _mybir
    from concourse.bass_utils import run_bass_kernel_spmd as _run

    nc = _bacc.Bacc("TRN2", target_bir_lowering=False, num_devices=1)
    arrays, args = {}, {}
    for name in _INS:
        v = _np.ascontiguousarray(inputs[name])
        arrays[f"in_{name}_dram"] = v
        args[name] = nc.dram_tensor(f"in_{name}_dram", v.shape, _mybir.dt.from_np(v.dtype), kind="ExternalInput").ap()
    inv = _np.concatenate([_np.float32(ROPE_THETA) ** (-_np.arange(0, d, 2, dtype=_np.float32) / _np.float32(d))
                           for d in (ATT_DH, IDX_DIM, IDX_DIM)]).astype(_np.float32)[None, :]
    arrays["in_inv_dram"] = inv
    args["inv"] = nc.dram_tensor("in_inv_dram", inv.shape, _mybir.dt.float32, kind="ExternalInput").ap()
    out = nc.dram_tensor("out_0_dram", (1, T, D), _mybir.dt.float32, kind="ExternalOutput").ap()
    first_and_second_block(nc, args, out)
    r = _run(nc, [arrays], core_ids=[0])
    return r.results[0]["out_0_dram"]
```
